# Optimizing a Trainium2 kernel written in Bass

```python
import jax, jax.numpy as jnp
from jax import lax
import numpy as np

D_MODEL = 2048
BATCH = 1
SEQ = 512
DEPTH = 1
DEC_BATCH = 8
DEC_SEQ = 8
PAST_LEN = 512
PAGE_SIZE = 128

N_HEADS = 8
HEAD_DIM = 128
D_ATT = N_HEADS * HEAD_DIM
N_KV_HEADS = 2
GROUP = N_HEADS // N_KV_HEADS
IDX_HEADS = 16
IDX_DIM = 64
TOPK_MAX = 256
D_CONV = 1024
CONV_WIDTH = 31
N_META = 16
Q_BLOCK = 128
N_BRANCH = 2
DEEPNORM_ALPHA = (2.0 * DEPTH) ** 0.25
DEEPNORM_BETA = (8.0 * DEPTH) ** -0.25
LN_EPS = 1e-5
NEG = -1e30
IN_SPLITS = (D_ATT, N_KV_HEADS * HEAD_DIM, N_KV_HEADS * HEAD_DIM, IDX_HEADS * IDX_DIM, IDX_DIM,
             IDX_HEADS, D_ATT, 2 * D_CONV, D_CONV, N_BRANCH * D_MODEL)
D_IN = sum(IN_SPLITS)

kernel_name = 'dsa_conformer_gated_hybrid_step'

def layer_norm(x, g, b):
    xf = x.astype(jnp.float32)
    mu = jnp.mean(xf, -1, keepdims=True)
    var = jnp.mean(jnp.square(xf - mu), -1, keepdims=True)
    return ((xf - mu) * lax.rsqrt(var + LN_EPS) * g.astype(jnp.float32) + b.astype(jnp.float32)).astype(x.dtype)

def alibi_slopes():
    return 2.0 ** (-8.0 * jnp.arange(1, N_HEADS + 1, dtype=jnp.float32) / N_HEADS)

def in_project(x, w_in, ln_idx_g, ln_idx_b):
    lead = x.shape[:-1]
    cuts = np.cumsum(IN_SPLITS)[:-1].tolist()
    q, k, v, iq, ik, iw, za, cu, zc, gt = jnp.split(x @ w_in, cuts, axis=-1)
    q = q.reshape(*lead, N_HEADS, HEAD_DIM)
    k = k.reshape(*lead, N_KV_HEADS, HEAD_DIM)
    v = v.reshape(*lead, N_KV_HEADS, HEAD_DIM)
    iq = iq.reshape(*lead, IDX_HEADS, IDX_DIM)
    ik = layer_norm(ik, ln_idx_g, ln_idx_b)
    ga, gb = jnp.split(cu, 2, axis=-1)
    u = ga * jax.nn.sigmoid(gb)
    gt = gt.reshape(*lead, N_BRANCH, D_MODEL)
    return q, k, v, iq, ik, iw, za, u, zc, gt

def indexer_scores(iq, iw, ik):
    s = jnp.einsum('bqhd,bkd->bqhk', iq, ik, preferred_element_type=jnp.float32) * (IDX_DIM ** -0.5)
    w = iw.astype(jnp.float32) * (IDX_HEADS ** -0.5)
    return jnp.einsum('bqhk,bqh->bqk', jax.nn.relu(s), w)

def sparse_attend(q, k_sel, v_sel, dist, valid):
    b, nq = q.shape[0], q.shape[1]
    qg = q.reshape(b, nq, N_KV_HEADS, GROUP, HEAD_DIM)
    logits = jnp.einsum('bqgrd,bqkgd->bqgrk', qg, k_sel, preferred_element_type=jnp.float32) * (HEAD_DIM ** -0.5)
    slopes = alibi_slopes().reshape(N_KV_HEADS, GROUP)
    logits = logits - slopes[None, None, :, :, None] * dist.astype(jnp.float32)[:, :, None, None, :]
    logits = jnp.where(valid[:, :, None, None, :], logits, NEG)
    p = jax.nn.softmax(logits, axis=-1)
    o = jnp.einsum('bqgrk,bqkgd->bqgrd', p.astype(v_sel.dtype), v_sel)
    return o.reshape(b, nq, D_ATT)

def depthwise_conv(u_ext, w_dw, b_dw):
    y = lax.conv_general_dilated(u_ext, w_dw[:, None, :].astype(u_ext.dtype), window_strides=(1,),
                                 padding='VALID', dimension_numbers=('NWC', 'WIO', 'NWC'),
                                 feature_group_count=D_CONV)
    return y + b_dw

def merge_and_norm(x, attn, za, c, zc, gt, ln_conv_g, ln_conv_b, w_att_out, w_conv_out, w_o, ln_post_g, ln_post_b):
    a_br = (attn * jax.nn.silu(za)) @ w_att_out
    c_br = (jax.nn.silu(layer_norm(c, ln_conv_g, ln_conv_b)) * jax.nn.silu(zc)) @ w_conv_out
    gate = jax.nn.sigmoid(gt.astype(jnp.float32)).astype(x.dtype)
    mixed = gate[..., 0, :] * a_br + gate[..., 1, :] * c_br
    return layer_norm(DEEPNORM_ALPHA * x + mixed @ w_o, ln_post_g, ln_post_b)

def setup_inputs(seed: int = 0) -> dict:
    key = jax.random.key(seed)
    ks = jax.random.split(key, 24)
    n_pages = PAST_LEN // PAGE_SIZE
    n_used = DEC_BATCH * n_pages
    n_phys = (n_used * 5 + 3) // 4
    f32 = jnp.float32
    nrm = lambda k, s: jax.random.normal(k, s, f32)
    page_table = jax.random.permutation(ks[6], n_phys)[:n_used].reshape(DEC_BATCH, n_pages).astype(jnp.int32)
    return {
        'x_prompt': nrm(ks[0], (BATCH, SEQ, D_MODEL)),
        'x_sample': nrm(ks[1], (DEC_BATCH, DEC_SEQ, D_MODEL)),
        'cache_k': nrm(ks[2], (n_phys, PAGE_SIZE, N_KV_HEADS, HEAD_DIM)),
        'cache_v': nrm(ks[3], (n_phys, PAGE_SIZE, N_KV_HEADS, HEAD_DIM)),
        'cache_idx_k': nrm(ks[4], (n_phys, PAGE_SIZE, IDX_DIM)),
        'state_conv': 0.5 * nrm(ks[5], (DEC_BATCH, CONV_WIDTH - 1, D_CONV)),
        'page_table': page_table,
        'meta_tokens': nrm(ks[7], (N_META, D_MODEL)),
        'w_in': nrm(ks[8], (D_MODEL, D_IN)) * D_MODEL ** -0.5,
        'ln_idx_g': 1.0 + 0.05 * nrm(ks[9], (IDX_DIM,)),
        'ln_idx_b': 0.02 * nrm(ks[10], (IDX_DIM,)),
        'w_dw': nrm(ks[11], (CONV_WIDTH, D_CONV)) * CONV_WIDTH ** -0.5,
        'b_dw': 0.02 * nrm(ks[12], (D_CONV,)),
        'ln_conv_g': 1.0 + 0.05 * nrm(ks[13], (D_CONV,)),
        'ln_conv_b': 0.02 * nrm(ks[14], (D_CONV,)),
        'w_att_out': nrm(ks[15], (D_ATT, D_MODEL)) * (D_ATT ** -0.5 * DEEPNORM_BETA),
        'w_conv_out': nrm(ks[16], (D_CONV, D_MODEL)) * (D_CONV ** -0.5 * DEEPNORM_BETA),
        'w_o': nrm(ks[17], (D_MODEL, D_MODEL)) * (D_MODEL ** -0.5 * DEEPNORM_BETA),
        'ln_post_g': 1.0 + 0.05 * nrm(ks[18], (D_MODEL,)),
        'ln_post_b': 0.02 * nrm(ks[19], (D_MODEL,)),
    }

def reference(x_prompt, x_sample, cache_k, cache_v, cache_idx_k, state_conv, page_table, meta_tokens,
              w_in, ln_idx_g, ln_idx_b, w_dw, b_dw, ln_conv_g, ln_conv_b, w_att_out, w_conv_out, w_o,
              ln_post_g, ln_post_b):
    B = x_prompt.shape[0]
    Lp = SEQ + N_META
    Lpad = -(-Lp // Q_BLOCK) * Q_BLOCK
    meta = jnp.broadcast_to(meta_tokens[None].astype(x_prompt.dtype), (B, N_META, D_MODEL))
    h = jnp.concatenate([meta, x_prompt, jnp.zeros((B, Lpad - Lp, D_MODEL), x_prompt.dtype)], axis=1)
    k_top_p = min(TOPK_MAX, SEQ // 4)
    pos = jnp.arange(Lpad)
    bidx = jnp.arange(B)[:, None, None]
    for _ in range(DEPTH):
        q, k, v, iq, ik, iw, za, u, zc, gt = in_project(h, w_in, ln_idx_g, ln_idx_b)

        def q_block(start):
            qb = lax.dynamic_slice_in_dim(q, start, Q_BLOCK, 1)
            iqb = lax.dynamic_slice_in_dim(iq, start, Q_BLOCK, 1)
            iwb = lax.dynamic_slice_in_dim(iw, start, Q_BLOCK, 1)
            qpos = start + jnp.arange(Q_BLOCK)
            sc = indexer_scores(iqb, iwb, ik)
            sc = jnp.where((pos[None, :] <= qpos[:, None])[None], sc, -jnp.inf)
            _, sel = lax.top_k(sc, k_top_p)
            valid = sel <= qpos[None, :, None]
            return sparse_attend(qb, k[bidx, sel], v[bidx, sel], qpos[None, :, None] - sel, valid)

        o_blocks = lax.map(q_block, jnp.arange(Lpad // Q_BLOCK) * Q_BLOCK)
        attn = jnp.transpose(o_blocks, (1, 0, 2, 3)).reshape(B, Lpad, D_ATT)
        u_ext = jnp.concatenate([jnp.zeros((B, CONV_WIDTH - 1, D_CONV), u.dtype), u], axis=1)
        c = depthwise_conv(u_ext, w_dw, b_dw)
        h_new = merge_and_norm(h, attn, za, c, zc, gt, ln_conv_g, ln_conv_b, w_att_out, w_conv_out, w_o,
                               ln_post_g, ln_post_b)
        k_prompt = k[:, :Lp]
        v_prompt = v[:, :Lp]
        idx_k_prompt = ik[:, :Lp]
        conv_prompt = u_ext[:, Lp:Lp + CONV_WIDTH - 1]
        h = h_new
    y_prompt = h[:, N_META:Lp]

    DB = x_sample.shape[0]
    L = PAST_LEN + DEC_SEQ
    k_top_s = min(TOPK_MAX, L // 4)
    qpos_s = PAST_LEN + jnp.arange(DEC_SEQ)
    bidx_s = jnp.arange(DB)[:, None, None]
    hs = x_sample
    for _ in range(DEPTH):
        q, k, v, iq, ik, iw, za, u, zc, gt = in_project(hs, w_in, ln_idx_g, ln_idx_b)
        ik_past = cache_idx_k[page_table].reshape(DB, PAST_LEN, IDX_DIM).astype(ik.dtype)
        ik_all = jnp.concatenate([ik_past, ik], axis=1)
        sc = indexer_scores(iq, iw, ik_all)
        sc = jnp.where((jnp.arange(L)[None, :] <= qpos_s[:, None])[None], sc, -jnp.inf)
        _, sel = lax.top_k(sc, k_top_s)
        valid = sel <= qpos_s[None, :, None]
        in_past = (sel < PAST_LEN)[..., None, None]
        sel_past = jnp.minimum(sel, PAST_LEN - 1)
        phys = page_table[bidx_s, sel_past // PAGE_SIZE]
        off = sel_past % PAGE_SIZE
        sel_new = jnp.clip(sel - PAST_LEN, 0, DEC_SEQ - 1)
        k_sel = jnp.where(in_past, cache_k[phys, off].astype(k.dtype), k[bidx_s, sel_new])
        v_sel = jnp.where(in_past, cache_v[phys, off].astype(v.dtype), v[bidx_s, sel_new])
        attn = sparse_attend(q, k_sel, v_sel, qpos_s[None, :, None] - sel, valid)
        u_ext = jnp.concatenate([state_conv.astype(u.dtype), u], axis=1)
        c = depthwise_conv(u_ext, w_dw, b_dw)
        hs_new = merge_and_norm(hs, attn, za, c, zc, gt, ln_conv_g, ln_conv_b, w_att_out, w_conv_out, w_o,
                                ln_post_g, ln_post_b)
        k_sample = k
        v_sample = v
        idx_k_sample = ik
        conv_sample = u_ext[:, DEC_SEQ:]
        hs = hs_new
    y_sample = hs
    return (y_prompt, y_sample, k_prompt, v_prompt, idx_k_prompt, conv_prompt,
            k_sample, v_sample, idx_k_sample, conv_sample)


_drawn_inputs = setup_inputs


def setup_inputs(seed=0):
    import zlib

    import numpy as np

    out = dict(_drawn_inputs(seed))
    spreads = {}
    factors = {'b_dw': 8.0, 'ln_conv_g': 8.0, 'ln_conv_b': 47.727, 'ln_post_b': 2.917, 'cache_k': 2.939}
    for name, (base, spread) in spreads.items():
        noise = np.random.default_rng([zlib.crc32(name.encode()), seed]).standard_normal(out[name].shape)
        drawn = base * np.exp(spread * noise) if base else spread * noise
        out[name] = __import__('jax').numpy.asarray(drawn.astype(out[name].dtype))
    for name, factor in factors.items():
        out[name] = (out[name] * factor).astype(out[name].dtype)
    return out
```

```python
from contextlib import ExitStack

import concourse.bass as bass
import numpy as np
from concourse import mybir

F32 = mybir.dt.float32
F32R = mybir.dt.float32r
I32 = mybir.dt.int32
ALU = mybir.AluOpType
ACT = mybir.ActivationFunctionType
AX_X = mybir.AxisListType.X
ds = bass.ds

P = 128
D = 2048
SEQ = 512
META = 16
LP = SEQ + META
DB = 8
DS = 8
PAST = 512
PAGES = PAST // P
HEADS, DH, KVH = 8, 128, 2
GROUP = HEADS // KVH
IH, IDIM = 16, 64
DC = 1024
CW = 31
TAIL = CW - 1
ALPHA = 2.0 ** 0.25
EPS = 1e-5
TOK = LP + DB * DS
HALF = TOK // 2
KC = D // P
TILES = 5
ROWS = [P, P, P, P, TOK - 4 * P]
LAST = LP - 4 * P
LS = PAST + DS
CUT = dict(q=0, kv=1024, iq=1536, ik=2560, za=2640, ga=3664, gb=4688, zc=5712, gt=6736)

MASKED = -3.0e38
TAKEN = -3.4e38
BETWEEN = -3.2e38
FAR = -1.0e32
PAD = 8
TOP_P = 128
TOP_S = 130
EXT = TAIL + LP
UW = EXT + DB * (TAIL + DS)

N_KV, N_IK, N_IQ, N_Q, N_GT, N_ZA, N_CU, N_ZC, N_BR, N_WO = 0, 4, 5, 13, 21, 53, 61, 77, 85, 101
N_END = 117
C_OF = N_IQ

C_ID, C_TRI, C_DIV, C_SLOPE, C_PAD, C_NEW, C_END = 0, 128, 256, 264, 266, 274, 290
E_DIST, E_DIST4, E_REP, E_END = 0, LP, 2 * LP, 2 * LP + 2 * P


def shape_constants():
    c = np.zeros((P, C_END), np.float32)
    p = np.arange(P)
    c[:, C_ID:C_ID + P] = np.eye(P)
    c[:, C_TRI:C_TRI + P] = np.where(p[None, :] > p[:, None], MASKED, 0.0)
    c[:, C_DIV:C_DIV + DS] = (p[:, None] % DS) == np.arange(DS)[None, :]
    for g in range(KVH):
        c[:, C_SLOPE + g] = 2.0 ** -(1.0 + g * GROUP + (p // DS) % GROUP)
    c[:, C_PAD:C_PAD + PAD] = -MASKED
    c[LAST:, C_PAD + PAD - (TOP_S - TOP_P):C_PAD + PAD] = MASKED
    new = np.zeros((P, META), np.float32)
    for r in range(ROWS[4]):
        seen = r + 1 if r < LAST else (r - LAST) % DS + 1
        new[r, seen:] = MASKED
    c[:, C_NEW:C_NEW + META] = new
    e = np.zeros((P, E_END), np.float32)
    k = np.arange(LP)
    e[:, E_DIST:E_DIST + LP] = k[None, :] - p[:, None]
    for r in range(ROWS[4]):
        at = 4 * P + r if r < LAST else PAST + (r - LAST) % DS
        e[r, E_DIST4:E_DIST4 + LP] = k - at
    for half in range(2):
        for m in range(P):
            b, t = m // (GROUP * DS), m % DS
            e[LAST + DS * (4 * half + b) + t, E_REP + half * P + m] = 1.0
    return c, e


def landed_after():
    total, out = [0, 0], []
    for n in range(N_END):
        total[n % 2] += 32 if N_BR <= n < N_WO else 16
        out.append(total[n % 2])
    return out


LANDED = landed_after()


def build(nc, x_prompt, x_sample, cache_k, cache_v, cache_idx_k, state_conv, page_table, meta_tokens,
          w_in, ln_idx_g, ln_idx_b, w_dw, b_dw, ln_conv_g, ln_conv_b, w_att_out, w_conv_out, w_o,
          ln_post_g, ln_post_b, consts, consts2,
          y_prompt, y_sample, k_prompt, v_prompt, idx_k_prompt, conv_prompt,
          k_sample, v_sample, idx_k_sample, conv_sample):
    gates = nc.dram_tensor("gates_dram", [32, P, TOK], F32)
    iw_dram = nc.dram_tensor("iw_dram", [DB * DS, IH], F32)

    base = -(-nc.sbuf_base // 32) * 32

    def at(name, shape, dt, offset):
        return nc.alloc_sbuf_tensor_at(name, shape, dt, offset=base + offset)

    XB = KC * TOK * 4
    xhi = at("xhi", [P, KC, TOK], F32R, 0)
    xlo = at("xlo", [P, KC, TOK], F32R, XB)
    y = at("y", [P, TILES, D], F32, 0)
    post_g = at("post_g", [P, D], F32, TILES * D * 4)
    post_b = at("post_b", [P, D], F32, (TILES + 1) * D * 4)
    W0 = 2 * XB
    BL = KC * P * 4
    raw = at("raw", [P, 2, KC * P], F32, W0)
    whi = at("whi", [P, 2, KC * P], F32R, W0 + 2 * BL)
    wlo = at("wlo", [P, 2, KC * P], F32R, W0 + 4 * BL)
    B0 = W0 + 6 * BL
    HB = 8 * TOK * 4
    xn = at("xn", [P, TILES, D], F32, B0)
    qT = at("qT", [P, 8, TOK], F32, B0)
    iqT = at("iqT", [P, 8, TOK], F32, B0 + HB)
    zc = at("zc", [P, 8, TOK], F32, B0 + HB)
    vpage = at("vpage", [P, 4, PAGES, 2 * DH], F32, B0 + HB)
    dist_c = at("dist_c", [P, 2 * LP], F32, B0 + HB)
    rep_c = at("rep_c", [P, 2 * P], F32, B0 + HB + 16384)
    idx_page = at("idx_page", [P, 2, PAGES, 2, IDIM], F32, B0)
    idx_kT = at("idx_kT", [P, 2, PAST], F32, B0 + 4096)
    w_sel = at("w_sel", [P, DB, ROWS[4]], F32, B0 + 8192)
    ik_norm = at("ik_norm", [P, TILES, 2, IDIM], F32, B0 + 10752)
    dw_rows = at("dw_rows", [CW + 3, DC], F32, B0 + 13312)
    idx_gb = at("idx_gb", [P, 2, IDIM], F32, B0 + 17408)
    R0 = B0 + 2 * HB
    kT = at("kT", [P, KVH, TOK], F32, R0)
    ikT = at("ikT", [P, TOK], F32, R0 + 4736)
    kv = at("kv", [P, TILES, 2 * KVH * DH], F32, R0 + 7104)
    v_new = at("v_new", [DS, DB, KVH * DH], F32, R0 + 7104)
    S0 = R0 + 17344
    bias_w = [P, 2 * P, 3 * P, 4 * P, PAD + LP]
    bias_at = [0, P, 3 * P, 6 * P, 10 * P]
    bias = at("bias", [P, sum(bias_w)], F32, S0)
    scores = at("scores", [P, 2, LP], F32, S0 + 7264)
    ikiw = at("ikiw", [P, TILES, IDIM + IH], F32, S0 + 11488)
    pT = at("pT", [P, 2, 4 * P], F32, S0 + 13088)
    bias_s = at("bias_s", [P, LS], F32, S0 + 17184)
    iq_new = at("iq_new", [P, DB, IH // 2 * DS], F32, S0 + 13088)
    q_new = at("q_new", [P, KVH, DB, GROUP * DS], F32, S0)
    pT_new = at("pT_new", [DS, 2, P], F32, S0 + 19264)
    U = at("U", [P, 8, UW], F32, R0)
    tmp_lin = at("tmp_lin", [P, 2, TOK], F32, R0 + 27584)
    tmp_tanh = at("tmp_tanh", [P, 2, TOK], F32, R0 + 27584 + 4736)
    u_tail = at("u_tail", [P, DC], F32, R0 + 27584)
    mhi = at("mhi", [P, KC, TOK], F32R, B0)
    mlo = at("mlo", [P, KC, TOK], F32R, B0 + XB)
    gate0 = at("gate0", [P, KC, TOK], F32, B0)
    gate1 = at("gate1", [P, KC, TOK], F32, B0 + XB)
    M0 = B0 + 2 * XB
    cst = at("cst", [P, C_END], F32, M0)
    ones = at("ones", [P, P], F32, M0 + 1184)
    dwT = at("dwT", [P, 8, CW + 3], F32, M0 + 1696)
    small = at("small", [P, 128], F32, M0 + 2784)
    pages = at("pages", [1, DB * PAGES], I32, M0 + 3296)
    kpage = at("kpage", [P, PAGES, 2 * DH], F32, M0 + 3424)
    kTs = at("kTs", [P, KVH, PAST], F32, M0 + 3424 + 4096)
    state = at("state", [P, 2, DC], F32, M0 + 3424)
    c_acc = at("c_acc", [P, TOK], F32, M0 + 3424)
    c_sum = at("c_sum", [P, TOK], F32, M0 + 3424 + 2368)
    c_rstd = at("c_rstd", [P, TOK], F32, M0 + 3424 + 4736)
    tailT = at("tailT", [P, 8, TAIL + DB * DS], F32, M0 + 3424 + 4736)
    m_tmp = at("m_tmp", [P, 2, TOK], F32, M0 + 3424)
    ident = cst[:, C_ID:C_ID + P]

    st = small[:, 0:30]
    mv = small[:, 30:40]
    rs = small[:, 40:45]
    wcol = small[:, 48:56]
    top8 = small[:, 56:64]
    neg_max = small[:, 64:66]
    exp_sum = small[:, 66:68]
    inv_sum = small[:, 68:70]
    half_g = small[:, 72:80]
    half_b = small[:, 80:88]
    yst = small[:, 88:112]
    ymv = small[:, 112:114]
    y_rstd = small[:, 114:119]
    y_shift = small[:, 119:124]
    wait_carrier = small[:, 124:125]

    with ExitStack() as ctx:
        ps_t = ctx.enter_context(nc.psum_tensor("ps", [P, 8 * 512], F32))
        ps = ps_t[:, :].rearrange("p (b n) -> p b n", b=8)

        def sem(name):
            return ctx.enter_context(nc.semaphore(name))

        x_here = [sem(f"x_here{i}") for i in range(TILES)]
        consts_here = sem("consts_here")
        consts2_here = sem("consts2_here")
        dw_here = sem("dw_here")
        pages_here = sem("pages_here")
        raw_here = [sem("raw_here0"), sem("raw_here1")]
        hi_ready = sem("hi_ready")
        lo_ready = sem("lo_ready")
        block_used = sem("block_used")
        xT_out = sem("xT_out")
        xhi_ready = sem("xhi_ready")
        xlo_ready = sem("xlo_ready")
        kv_out = sem("kv_out")
        kv_ready = sem("kv_ready")
        ikiw_ready = sem("ikiw_ready")
        ik_var = sem("ik_var")
        ik_std = sem("ik_std")
        ik_ready = sem("ik_ready")
        tile_taken = sem("tile_taken")
        turned = sem("turned")
        turned_taken = sem("turned_taken")
        iw_stored = sem("iw_stored")
        wcol_here = sem("wcol_here")
        wsel_ready = sem("wsel_ready")
        idx_here = [sem("idx_here0"), sem("idx_here1")]
        idx_turned = sem("idx_turned")
        idx_kT_ready = sem("idx_kT_ready")
        idx_out = sem("idx_out")
        relu_ready = sem("relu_ready")
        relu_used = sem("relu_used")
        sample_scored = sem("sample_scored")
        scores_done = sem("scores_done")
        bias_ready = sem("bias_ready")
        gate_stored = [sem("gate_stored0"), sem("gate_stored1")]
        logits_out = sem("logits_out")
        logits_taken = sem("logits_taken")
        max_ready = sem("max_ready")
        exp_ready = sem("exp_ready")
        probs_ready = sem("probs_ready")
        pT_out = sem("pT_out")
        pT_ready = sem("pT_ready")
        o_out = sem("o_out")
        o_taken = sem("o_taken")
        rep_out = sem("rep_out")
        rep_taken = sem("rep_taken")
        kpage_here = sem("kpage_here")
        vpage_here = sem("vpage_here")
        v_new_here = sem("v_new_here")
        kTs_out = sem("kTs_out")
        kTs_ready = sem("kTs_ready")
        s_logits = sem("s_logits")
        s_max = sem("s_max")
        s_exp = sem("s_exp")
        s_probs = sem("s_probs")
        s_pT_out = sem("s_pT_out")
        s_pT_ready = sem("s_pT_ready")
        s_o_out = sem("s_o_out")
        s_o_taken = sem("s_o_taken")
        za_used = sem("za_used")
        state_here = sem("state_here")
        state_out = sem("state_out")
        state_taken = sem("state_taken")
        conv_done = sem("conv_done")
        tail_out = sem("tail_out")
        tail_ready = sem("tail_ready")
        tail_stored = sem("tail_stored")
        zc_done = sem("zc_done")
        mean_out = sem("mean_out")
        sq_ready = sem("sq_ready")
        var_out = sem("var_out")
        std_in = sem("std_in")
        std_ready = sem("std_ready")
        n_ready = sem("n_ready")
        lin_ready = sem("lin_ready")
        tanh_ready = sem("tanh_ready")
        c_ready = sem("c_ready")
        gate_here = [sem(f"gate_here{i}") for i in range(8)]
        br_taken = sem("br_taken")
        m_ready = sem("m_ready")
        mhi_ready = sem("mhi_ready")
        mlo_ready = sem("mlo_ready")
        y_here = sem("y_here")
        post_here = sem("post_here")
        y_scaled = sem("y_scaled")
        y_out = sem("y_out")
        y_taken = sem("y_taken")
        y_var = sem("y_var")
        y_std = sem("y_std")
        y_norm_in = sem("y_norm_in")
        y_norm = sem("y_norm")
        y_final = sem("y_final")
        dve_step = sem("dve_step")
        pool_step = sem("pool_step")
        topk_step = sem("topk_step")
        conv_step = sem("conv_step")
        stored = sem("stored")
        idx_stored = sem("idx_stored")
        iq_new_ready = sem("iq_new_ready")
        q_new_ready = sem("q_new_ready")
        tailT_ready = sem("tailT_ready")

        stores = [0]

        def w_cols(c0, k0=0, kn=KC, width=P, w=w_in):
            return w[k0 * P:(k0 + kn) * P, c0:c0 + width] if isinstance(c0, int) else \
                w[k0 * P:(k0 + kn) * P, ds(c0, width)]

        def sample_cols(a, j):
            v = a[:, j, EXT:UW] if isinstance(j, int) else a[:, ds(j, 1), EXT:UW].rearrange("p a w -> p (a w)")
            return v.rearrange("p (b w) -> p b w", b=DB)

        block = ctx.enter_context(nc.Block())

        @block.sync
        def _(sp):
            def buffer_free(n):
                sp.wait_ge(hi_ready, n - 1)
                sp.wait_ge(lo_ready, n - 1)

            def load_rows(n, w, k0, c0):
                if n >= 2:
                    buffer_free(n)
                sp.dma_start(raw[:, n % 2, :].rearrange("p (k c) -> p k c", k=4),
                             w[k0 * P:(k0 + 4) * P, c0:c0 + 512].rearrange("(k p) c -> p k c", p=P)
                             ).then_inc(raw_here[n % 2], 16)

            def load_tile(n, c0, buf):
                buffer_free(n)
                sp.dma_start(raw[:, buf, :].rearrange("p (k c) -> p k c", k=KC),
                             w_cols(c0).rearrange("(k p) c -> p k c", p=P)).then_inc(raw_here[buf], 16)

            def load_tiles(n0, count, c0, c1=None):
                with sp.Fori(0, count // 2) as i:
                    if c1 is None:
                        load_tile(n0 + i * 2, c0 + i * 256, n0 % 2)
                        load_tile(n0 + 1 + i * 2, c0 + P + i * 256, (n0 + 1) % 2)
                    else:
                        load_tile(n0 + i * 2, c0 + i * P, n0 % 2)
                        load_tile(n0 + 1 + i * 2, c1 + i * P, (n0 + 1) % 2)

            sp.dma_start(cst[:, :], consts).then_inc(consts_here, 16)
            sp.dma_start(xn[0:META, 0, :], meta_tokens).then_inc(x_here[0], 16)
            sp.dma_start(xn[META:P, 0, :], x_prompt[0, 0:P - META, :]).then_inc(x_here[0], 16)
            for t in range(1, 4):
                sp.dma_start(xn[:, t, :], x_prompt[0, t * P - META:(t + 1) * P - META, :]).then_inc(x_here[t], 16)
            sp.dma_start(xn[0:LAST, 4, :], x_prompt[0, SEQ - LAST:SEQ, :]).then_inc(x_here[4], 16)
            sp.dma_start(xn[LAST:ROWS[4], 4, :], x_sample.rearrange("b t d -> (b t) d")).then_inc(x_here[4], 16)
            sp.dma_start(pages[:, :], page_table.rearrange("(o b) n -> o (b n)", o=1)).then_inc(pages_here, 16)
            for n in range(4):
                load_rows(n, w_in, 4 * n, CUT["kv"])
            buffer_free(N_IK)
            sp.dma_start(raw[:, 0, 0:KC * 80].rearrange("p (k c) -> p k c", k=KC),
                         w_cols(CUT["ik"], width=80).rearrange("(k p) c -> p k c", p=P)).then_inc(raw_here[0], 16)
            sp.wait_ge(xT_out, 4 * TILES)
            sp.dma_start(dw_rows[0:CW, :], w_dw).then_inc(dw_here, 16)
            for r, v in enumerate((b_dw, ln_conv_g, ln_conv_b)):
                sp.dma_start(dw_rows[CW + r:CW + r + 1, :], v.rearrange("(o c) -> o c", o=1)).then_inc(dw_here, 16)
            for r, v in enumerate((ln_idx_g, ln_idx_b)):
                sp.dma_start(idx_gb[:, r, :], v.rearrange("(o c) -> o c", o=1).broadcast_to([P, IDIM])
                             ).then_inc(dw_here, 16)
            load_tiles(N_IQ, 8, CUT["iq"])
            load_tile(N_Q, CUT["q"], N_Q % 2)
            sp.wait_ge(kv_ready, TILES)
            for t in range(4):
                for c, o in ((0, k_prompt), (1, v_prompt)):
                    sp.dma_start(o[0, t * P:(t + 1) * P].rearrange("t g d -> t (g d)"),
                                 kv[:, t, 256 * c:256 * c + 256]).then_inc(stored, 16)
                    stores[0] += 1
            for c, o, s in ((0, k_prompt, k_sample), (1, v_prompt, v_sample)):
                sp.dma_start(o[0, 4 * P:LP].rearrange("t g d -> t (g d)"),
                             kv[0:LAST, 4, 256 * c:256 * c + 256]).then_inc(stored, 16)
                sp.dma_start(s.rearrange("b t g d -> (b t) (g d)"),
                             kv[LAST:ROWS[4], 4, 256 * c:256 * c + 256]).then_inc(stored, 16)
                stores[0] += 2
            kv_stores = stores[0]
            sp.wait_ge(ikiw_ready, 1)
            sp.dma_start(iw_dram[:, :], ikiw[LAST:ROWS[4], 4, IDIM:]).then_inc(iw_stored, 16)
            sp.wait_ge(iw_stored, 16)
            for h in range(IH):
                p0 = 64 * (h % 2) + DS * (h // 2)
                sp.dma_start(wcol[p0:p0 + DS, :], iw_dram[:, h:h + 1].rearrange("(b t) o -> t (b o)", t=DS),
                             allow_slow_non_contiguous=True).then_inc(wcol_here, 16)
            sp.wait_ge(ik_ready, TILES)
            for t in range(4):
                sp.dma_start(idx_k_prompt[0, t * P:(t + 1) * P, :], ik_norm[:, t, 0, :]).then_inc(idx_stored, 16)
            sp.dma_start(idx_k_prompt[0, 4 * P:LP, :], ik_norm[0:LAST, 4, 0, :]).then_inc(idx_stored, 16)
            sp.dma_start(idx_k_sample.rearrange("b t d -> (b t) d"), ik_norm[LAST:ROWS[4], 4, 0, :]
                         ).then_inc(idx_stored, 16)

            sp.wait_ge(pages_here, 16)

            def page(b, n):
                return sp.value_load(pages[0:1, b * PAGES + n:b * PAGES + n + 1], min_val=0,
                                     max_val=cache_k.shape[0] - 1)

            def load_idx(b):
                if b >= 2:
                    sp.wait_ge(idx_turned, b - 1)
                for n in range(PAGES):
                    v = page(b, n)
                    for c in range(2):
                        sp.dma_start(idx_page[:, b % 2, n, c, :],
                                     cache_idx_k[ds(v, 1), :, :].rearrange("a t d -> (a t) d")
                                     ).then_inc(idx_here[b % 2], 16)

            for b in range(DB):
                load_idx(b)
            load_tile(N_Q + 1, CUT["q"] + P, (N_Q + 1) % 2)
            sp.wait_ge(idx_out, 72)
            sp.dma_start(dist_c[:, :], consts2[:, 0:2 * LP]).then_inc(consts2_here, 16)
            sp.dma_start(rep_c[:, :], consts2[:, E_REP:E_END]).then_inc(consts2_here, 16)
            load_tiles(N_Q + 2, 6, CUT["q"] + 2 * P)
            load_tiles(N_GT, 32, CUT["gt"])
            load_tile(N_ZA, CUT["za"], N_ZA % 2)
            load_tile(N_ZA + 1, CUT["za"] + P, (N_ZA + 1) % 2)

            sp.wait_ge(bias_ready, TILES)

            def load_v(b):
                for n in range(PAGES):
                    v = page(b, n)
                    sp.dma_start(vpage[:, b % 4, n, :], cache_v[ds(v, 1)].rearrange("a t g d -> (a t) (g d)")
                                 ).then_inc(vpage_here, 16)

            def load_k(b):
                if b:
                    sp.wait_ge(kTs_out, b)
                for n in range(PAGES):
                    v = page(b, n)
                    sp.dma_start(kpage[:, n, :], cache_k[ds(v, 1)].rearrange("a t g d -> (a t) (g d)")
                                 ).then_inc(kpage_here, 16)

            for half in range(2):
                load_k(4 * half)
                if half:
                    sp.wait_ge(s_o_out, 1)
                for b in range(4 * half, 4 * half + 4):
                    load_v(b)
                if not half:
                    sp.wait_ge(o_out, HEADS * TILES)
                    sp.wait_ge(stored, 16 * kv_stores)
                    sp.dma_start(v_new[:, :, :], v_sample.rearrange("b t g d -> t b (g d)")).then_inc(v_new_here, 16)
                for b in range(4 * half + 1, 4 * half + 4):
                    load_k(b)

            load_tiles(N_ZA + 2, 6, CUT["za"] + 2 * P)
            sp.wait_ge(s_logits, DB)
            for c in range(2):
                sp.dma_start(state[0:4 * TAIL, c, :], state_conv[4 * c:4 * c + 4].rearrange("b t c -> (b t) c")
                             ).then_inc(state_here, 16)
            sp.dma_start(conv_sample[:, 0:TAIL - DS, :], state_conv[:, DS:TAIL, :]).then_inc(stored, 16)
            stores[0] += 1
            load_tiles(N_CU, 16, CUT["ga"], CUT["gb"])
            load_tile(N_ZC, CUT["zc"], N_ZC % 2)
            load_tile(N_ZC + 1, CUT["zc"] + P, (N_ZC + 1) % 2)
            load_tiles(N_ZC + 2, 4, CUT["zc"] + 2 * P)
            sp.wait_ge(tail_ready, 1)
            sp.dma_start(conv_prompt[0], u_tail[0:TAIL, :]).then_inc(tail_stored, 16)
            for b in range(DB):
                sp.dma_start(conv_sample[b, TAIL - DS:TAIL, :], u_tail[TAIL + DS * b:TAIL + DS * b + DS, :]
                             ).then_inc(tail_stored, 16)
            load_tiles(N_ZC + 6, 2, CUT["zc"] + 6 * P)

            def branch_pair(i):
                for b in range(2):
                    n = N_BR + 2 * i + b
                    buffer_free(n)
                    for c, w in ((0, w_att_out), (1, w_conv_out)):
                        sp.dma_start(raw[:, n % 2, c * DC:(c + 1) * DC].rearrange("p (k c) -> p k c", k=8),
                                     w[:, (2 * i + b) * P:(2 * i + b + 1) * P].rearrange("(k p) c -> p k c", p=P)
                                     ).then_inc(raw_here[n % 2], 16)

            branch_pair(0)
            for s in gate_stored:
                sp.wait_ge(s, 16 * 16)
            sp.wait_ge(xhi_ready, 4 * TILES + KC)
            sp.wait_ge(xlo_ready, 4 * TILES + KC)
            for i in range(8):
                if i:
                    branch_pair(i)
                for g, dst in ((0, gate0), (1, gate1)):
                    sp.dma_start(dst[:, 2 * i:2 * i + 2, :],
                                 gates[16 * g + 2 * i:16 * g + 2 * i + 2].rearrange("j p t -> p j t")
                                 ).then_inc(gate_here[i], 16)
            for r in range(2):
                load_rows(N_WO + r, w_o, 4 * r, 0)
            sp.wait_ge(block_used, N_WO)
            sp.dma_start(y[0:META, 0, :], meta_tokens).then_inc(y_here, 16)
            sp.dma_start(y[META:P, 0, :], x_prompt[0, 0:P - META, :]).then_inc(y_here, 16)
            for t in range(1, 4):
                sp.dma_start(y[:, t, :], x_prompt[0, t * P - META:(t + 1) * P - META, :]).then_inc(y_here, 16)
            sp.dma_start(y[0:LAST, 4, :], x_prompt[0, SEQ - LAST:SEQ, :]).then_inc(y_here, 16)
            sp.dma_start(y[LAST:ROWS[4], 4, :], x_sample.rearrange("b t d -> (b t) d")).then_inc(y_here, 16)
            for v, dst in ((ln_post_g, post_g), (ln_post_b, post_b)):
                sp.dma_start(dst[:, :], v.rearrange("(o c) -> o c", o=1).broadcast_to([P, D])).then_inc(post_here, 16)
            for n in range(N_WO + 2, N_END):
                r = n - N_WO
                load_rows(n, w_o, 4 * (r % 4), 512 * (r // 4))
            for t in range(TILES):
                sp.wait_ge(y_final, t + 1)
                if t == 0:
                    sp.dma_start(y_prompt[0, 0:P - META, :], y[META:P, 0, :]).then_inc(stored, 16)
                elif t < 4:
                    sp.dma_start(y_prompt[0, t * P - META:(t + 1) * P - META, :], y[:, t, :]).then_inc(stored, 16)
                else:
                    sp.dma_start(y_prompt[0, SEQ - LAST:SEQ, :], y[0:LAST, 4, :]).then_inc(stored, 16)
                    sp.dma_start(y_sample.rearrange("b t d -> (b t) d"), y[LAST:ROWS[4], 4, :]).then_inc(stored, 16)
                    stores[0] += 1
                stores[0] += 1
            sp.wait_ge(tail_stored, 16 * (1 + DB))
            sp.wait_ge(idx_stored, 16 * 6)
            sp.wait_ge(stored, 16 * stores[0])

        @block.gpsimd
        def _(pool):
            steps = [0]

            def link(ins):
                steps[0] += 1
                ins.then_inc(pool_step, 1)
                pool.wait_ge(pool_step, steps[0])

            def split_lo(n, buf, width=KC * P):
                pool.wait_ge(hi_ready, n + 1)
                nc.gpsimd.tensor_tensor(wlo[:, buf, 0:width], raw[:, buf, 0:width],
                                        whi[:, buf, 0:width].bitcast(F32), ALU.subtract).then_inc(lo_ready, 1)

            for n in range(N_IK):
                split_lo(n, n % 2)
            split_lo(N_IK, 0, KC * 80)
            with pool.Fori(0, (N_ZA - N_IQ) // 2) as i:
                for b in range(2):
                    split_lo(N_IQ + b + i * 2, (N_IQ + b) % 2)
            split_lo(N_ZA, N_ZA % 2)
            for j in range(8):
                split_lo(N_ZA + j + 1, (N_ZA + j + 1) % 2)
                pool.wait_ge(tile_taken, N_ZA + j - C_OF + 3)
                s = j % 2
                link(nc.gpsimd.tensor_tensor(tmp_tanh[:, s, :], tmp_tanh[:, s, :], tmp_lin[:, s, :], ALU.mult))
                link(nc.gpsimd.tensor_tensor(tmp_tanh[:, s, :], tmp_tanh[:, s, :], tmp_lin[:, s, :], ALU.add))
                pool.wait_ge(s_o_taken, 2)
                nc.gpsimd.tensor_tensor(qT[:, j, :], qT[:, j, :], tmp_tanh[:, s, :], ALU.mult).then_inc(za_used, 1)
            with pool.Fori(0, (N_ZC - N_CU) // 2) as i:
                for b in range(2):
                    split_lo(N_CU + 1 + b + i * 2, (N_CU + 1 + b) % 2)
            for j in range(8):
                split_lo(N_ZC + j + 1, (N_ZC + j + 1) % 2)
                pool.wait_ge(tile_taken, N_ZC + j - C_OF + 3)
                s = j % 2
                link(nc.gpsimd.tensor_tensor(tmp_tanh[:, s, :], tmp_tanh[:, s, :], zc[:, j, :], ALU.mult))
                nc.gpsimd.tensor_tensor(zc[:, j, :], tmp_tanh[:, s, :], zc[:, j, :], ALU.add).then_inc(zc_done, 1)
            for n in range(N_BR + 1, N_END):
                split_lo(n, n % 2)

        @block.scalar
        def _(act):
            def split_hi(n, buf, landed, width=KC * P, first=False):
                act.wait_ge(raw_here[buf], landed)
                if not first:
                    act.wait_ge(block_used, n - 1)
                nc.scalar.activation(whi[:, buf, 0:width], raw[:, buf, 0:width], ACT.Copy).then_inc(hi_ready, 1)

            def tile_ps(b):
                return ps[:, 2 * b:2 * b + 2, 0:HALF]

            def pairs(a):
                return a.rearrange("p (h t) -> p h t", h=2)

            def flat(a, j):
                return pairs(a[:, j, :]) if isinstance(j, int) else \
                    a[:, ds(j, 1), :].rearrange("p a (h t) -> p (a h) t", h=2)

            def each_pair(n0, count, take):
                with act.Fori(0, count // 2) as i:
                    for b in range(2):
                        n = n0 + b
                        split_hi(n + 1 + i * 2, (n + 1) % 2, LANDED[n + 1] + i * 16)
                        act.wait_ge(block_used, n + 1 + i * 2)
                        take(i, b)

            for g in range(4 * TILES):
                t, q = g // 4, g % 4
                act.wait_ge(xT_out, g + 1)
                nc.scalar.activation(xhi[:, 4 * q:4 * q + 4, t * P:t * P + ROWS[t]],
                                     ps[:, g % 8, :].rearrange("p (k t) -> p k t", k=4)[:, :, 0:ROWS[t]],
                                     ACT.Copy).then_inc(xhi_ready, 1)
                if g == 3:
                    split_hi(0, 0, LANDED[0], first=True)
                if g == 7:
                    split_hi(1, 1, LANDED[1], first=True)
            split_hi(2, 0, LANDED[2])
            split_hi(3, 1, LANDED[3])
            split_hi(4, 0, LANDED[4], KC * 80)
            for t in range(TILES):
                if t < 4:
                    act.wait_ge(kv_out, t + 1)
                else:
                    act.wait_ge(block_used, N_IK)
                nc.scalar.activation(kv[0:ROWS[t], t, :], ps[0:ROWS[t], t, :], ACT.Copy).then_inc(kv_ready, 1)
            act.wait_ge(kv_ready, TILES)
            act.sem_inc(tile_taken, 2)
            split_hi(5, 1, LANDED[5])
            act.wait_ge(block_used, N_IK + 1)
            nc.scalar.activation(ikiw[:, 0:4, :], ps[:, 5, 0:320].rearrange("p (t c) -> p t c", t=4), ACT.Copy
                                 ).then_inc(ikiw_ready, 1)
            nc.scalar.activation(ikiw[0:ROWS[4], 4, :], ps[0:ROWS[4], 5, 320:400], ACT.Copy).then_inc(ikiw_ready, 1)

            act.wait_ge(ik_var, 1)
            nc.scalar.activation(rs, mv.rearrange("p (t c) -> p t c", c=2)[:, :, 1], ACT.Sqrt).then_inc(ik_std, 1)

            def take_iq(i, b):
                nc.scalar.activation(flat(iqT, i * 2 + b), tile_ps(b), ACT.Copy).then_inc(tile_taken, 1)

            each_pair(N_IQ, 8, take_iq)
            act.wait_ge(turned, 1)
            nc.scalar.activation(kT[:, :, 0:512], ps[:, 4:6, :], ACT.Copy).then_inc(turned_taken, 1)
            act.wait_ge(turned, 2)
            nc.scalar.activation(kT[:, :, 512:TOK], ps[:, 6, 0:160].rearrange("p (g t) -> p g t", g=2), ACT.Copy
                                 ).then_inc(turned_taken, 1)
            act.wait_ge(turned, 3)
            nc.scalar.activation(ikT[:, 0:512], ps[:, 7, :], ACT.Copy).then_inc(turned_taken, 1)
            act.wait_ge(turned, 4)
            nc.scalar.activation(ikT[:, 512:TOK], ps[:, 2, 0:80], ACT.Copy).then_inc(turned_taken, 1)
            act.wait_ge(turned, 5)
            nc.scalar.activation(dwT[:, :, :], ps[:, 3, 0:8 * (CW + 3)].rearrange("p (j r) -> p j r", j=8), ACT.Copy
                                 ).then_inc(turned_taken, 1)

            scale = (IDIM ** -0.5) * (IH ** -0.5)
            for u in range(64):
                i, rows = 1 + u // IH, P if u < 48 else LAST
                n = min((i + 1) * P, LP)
                act.wait_ge(idx_out, u + 1)
                if u >= 2:
                    act.wait_ge(relu_used, u - 1)
                nc.scalar.activation(scores[0:rows, u % 2, 0:n],
                                     ps_t[0:rows, 2048 + 1024 * (u % 2):2048 + 1024 * (u % 2) + n],
                                     ACT.Relu, scale=scale).then_inc(relu_ready, 1)
            for b in range(DB):
                act.wait_ge(idx_turned, b + 1)
                nc.scalar.activation(idx_kT[:, b % 2, :], ps[:, 2 + b % 2, :], ACT.Copy).then_inc(idx_kT_ready, 1)
                act.wait_ge(idx_out, 65 + b)
                act.wait_ge(relu_used, 64 if b < 2 else 64 + b - 1)
                nc.scalar.activation(scores[:, b % 2, 0:LS], ps_t[:, 2048 + 1024 * (b % 2):2048 + 1024 * (b % 2) + LS],
                                     ACT.Relu, scale=scale).then_inc(relu_ready, 1)

            def take_q(i, b):
                nc.scalar.activation(flat(qT, i * 2 + b), tile_ps(b), ACT.Copy, scale=DH ** -0.5
                                     ).then_inc(tile_taken, 1)

            act.wait_ge(idx_stored, 16 * 6)
            each_pair(N_Q, 8, take_q)

            def take_gate(i, b, first=False):
                if not first:
                    act.wait_ge(gate_stored[b], i * 16)
                nc.scalar.activation(pairs(tmp_lin[:, b, :]), tile_ps(b), ACT.Tanh, scale=0.5).then_inc(tile_taken, 1)
                act.wait_ge(tile_taken, N_GT - C_OF + b + 3 + i * 2)
                dst = gates[b] if first else gates[ds(i * 2 + b, 1)].rearrange("a p t -> (a p) t")
                act.dma_start(dst, tmp_lin[:, b, :]).then_inc(gate_stored[b], 16)

            for b in range(2):
                split_hi(N_GT + b + 1, (N_GT + b + 1) % 2, LANDED[N_GT + b + 1])
                act.wait_ge(block_used, N_GT + b + 1)
                take_gate(0, b, True)
            with act.Fori(1, 16) as i:
                for b in range(2):
                    n = N_GT + b
                    split_hi(n + 1 + i * 2, (n + 1) % 2, LANDED[n + 1] + i * 16)
                    act.wait_ge(block_used, n + 1 + i * 2)
                    take_gate(i, b)
            split_hi(N_ZA + 1, (N_ZA + 1) % 2, LANDED[N_ZA + 1])

            units = [(i, h) for i in range(TILES) for h in range(HEADS)]
            for s in range(len(units) + 1):
                if s < len(units):
                    i, h = units[s]
                    rows, n = (P if i < 4 else LAST), min((i + 1) * P, LP)
                    act.wait_ge(max_ready, s + 1)
                    nc.scalar.activation(scores[0:rows, s % 2, 0:n], scores[0:rows, s % 2, 0:n], ACT.Exp,
                                         bias=neg_max[0:rows, s % 2:s % 2 + 1],
                                         accum_out=exp_sum[0:rows, s % 2:s % 2 + 1]).then_inc(exp_ready, 1)
                if s >= 1:
                    u = s - 1
                    i, h = units[u]
                    cols = (i + 1) * P if i < 4 else 4 * LAST
                    act.wait_ge(pT_out, u + 1)
                    if u >= 2:
                        act.wait_ge(o_out, u - 1)
                    if i == 4:
                        nc.scalar.activation(pT[0:LAST, u % 2, cols:cols + LAST], ps[0:LAST, u % 2, cols:cols + LAST],
                                             ACT.Copy)
                    nc.scalar.activation(pT[:, u % 2, 0:cols], ps[:, u % 2, 0:cols], ACT.Copy).then_inc(pT_ready, 1)

            for half in range(2):
                for b4 in range(4):
                    b = 4 * half + b4
                    act.wait_ge(kTs_out, b + 1)
                    if b:
                        act.wait_ge(s_logits, b)
                    nc.scalar.activation(kTs[:, :, :], ps[:, 0:2, :], ACT.Copy).then_inc(kTs_ready, 1)
                for g in range(2):
                    act.wait_ge(s_max, 2 * half + g + 1)
                    nc.scalar.activation(scores[:, g, 0:LS], scores[:, g, 0:LS], ACT.Exp,
                                         bias=neg_max[:, g:g + 1], accum_out=exp_sum[:, g:g + 1]).then_inc(s_exp, 1)
                for g in range(2):
                    act.wait_ge(s_pT_out, 2 * half + g + 1)
                    if half:
                        act.wait_ge(s_o_out, half)
                    nc.scalar.activation(pT[:, g, :], ps[:, g, :], ACT.Copy)
                    nc.scalar.activation(pT_new[:, g, :], ps[0:DS, 2 + g, 0:P], ACT.Copy).then_inc(s_pT_ready, 1)

            for j in range(8):
                n = N_ZA + j
                if j:
                    split_hi(n + 1, (n + 1) % 2, LANDED[n + 1])
                act.wait_ge(block_used, n + 1)
                if j >= 2:
                    act.wait_ge(za_used, j - 1)
                b = j % 2
                nc.scalar.activation(pairs(tmp_lin[:, b, :]), tile_ps(b), ACT.Copy, scale=0.5)
                nc.scalar.activation(pairs(tmp_tanh[:, b, :]), tile_ps(b), ACT.Tanh, scale=0.5).then_inc(tile_taken, 1)

            act.wait_ge(state_taken, 16)
            with act.Fori(0, 8) as i:
                for b in range(2):
                    n = N_CU + b
                    split_hi(n + 1 + i * 2, (n + 1) % 2, LANDED[n + 1] + i * 16)
                    act.wait_ge(block_used, n + 1 + i * 2)
                    if b == 0:
                        row = U[:, ds(i, 1), :].rearrange("p a w -> p (a w)")
                        nc.scalar.activation(row[:, TAIL:TAIL + HALF], ps[:, 0, 0:HALF], ACT.Copy, scale=0.5)
                        nc.scalar.activation(row[:, TAIL + HALF:EXT], ps[:, 1, 0:LP - HALF], ACT.Copy, scale=0.5)
                        nc.scalar.activation(sample_cols(U, i)[:, :, TAIL:],
                                             ps[:, 1, LP - HALF:HALF].rearrange("p (b t) -> p b t", b=DB),
                                             ACT.Copy, scale=0.5).then_inc(tile_taken, 1)
                    else:
                        nc.scalar.activation(flat(zc, i), tile_ps(1), ACT.Tanh, scale=0.5).then_inc(tile_taken, 1)

            def normed(j):
                act.wait_ge(n_ready, j + 1)
                if j >= 2:
                    act.wait_ge(c_ready, j - 1)
                b = j % 2
                nc.scalar.activation(tmp_lin[:, b, 0:LP], U[:, j, TAIL:EXT], ACT.Identity,
                                     scale=half_g[:, j:j + 1], bias=half_b[:, j:j + 1])
                nc.scalar.activation(tmp_lin[:, b, LP:TOK].rearrange("p (b t) -> p b t", b=DB),
                                     sample_cols(U, j)[:, :, TAIL:], ACT.Identity,
                                     scale=half_g[:, j:j + 1], bias=half_b[:, j:j + 1]).then_inc(lin_ready, 1)
                act.wait_ge(lin_ready, j + 1)
                nc.scalar.activation(U[:, j, 0:TOK], tmp_lin[:, b, :], ACT.Tanh).then_inc(tanh_ready, 1)

            for j in range(8):
                n = N_ZC + j
                split_hi(n + 1, (n + 1) % 2, LANDED[n + 1])
                act.wait_ge(block_used, n + 1)
                act.wait_ge(tailT_ready, j + 1)
                if j >= 2:
                    act.wait_ge(zc_done, j - 1)
                b = j % 2
                nc.scalar.activation(flat(zc, j), tile_ps(b), ACT.Copy, scale=0.5)
                nc.scalar.activation(pairs(tmp_tanh[:, b, :]), tile_ps(b), ACT.Tanh, scale=0.5).then_inc(tile_taken, 1)
                if j == 3:
                    act.wait_ge(tail_out, 1)
                    nc.scalar.activation(u_tail[0:TAIL + DB * DS, :].rearrange("p (h c) -> p h c", h=2),
                                         ps[0:TAIL + DB * DS, 4:6, :], ACT.Copy).then_inc(tail_ready, 1)
                if j == 5:
                    act.wait_ge(std_in, 1)
                    nc.scalar.activation(c_rstd[:, :], c_sum[:, :], ACT.Sqrt).then_inc(std_ready, 1)
                    act.wait_ge(tail_stored, 16 * (1 + DB))
                if j >= 6:
                    for k in range(4 * (j - 6), 4 * (j - 6) + 4):
                        normed(k)
            act.wait_ge(block_used, N_BR)
            for k in range(KC):
                if k >= 8:
                    act.wait_ge(c_ready, k - 7)
                nc.scalar.activation(xhi[:, k, :], qT[:, k, :] if k < 8 else zc[:, k - 8, :], ACT.Copy
                                     ).then_inc(xhi_ready, 1)

            for j in range(KC):
                n = N_BR + j
                split_hi(n + 1, (n + 1) % 2, LANDED[n + 1])
                act.wait_ge(m_ready, j + 1)
                nc.scalar.activation(mhi[:, j, :], m_tmp[:, j % 2, :], ACT.Copy).then_inc(mhi_ready, 1)
            act.wait_ge(y_here, 16 * 7)
            for r in range(16):
                n = N_WO + r
                if r < 5:
                    rows = ROWS[r]
                    nc.scalar.mul(y[0:rows, r, :], y[0:rows, r, :], ALPHA).then_inc(y_scaled, 1)
                if n + 1 < N_END:
                    split_hi(n + 1, (n + 1) % 2, LANDED[n + 1])
            for t in range(TILES):
                rows = ROWS[t]
                act.wait_ge(y_var, t + 1)
                nc.scalar.activation(y_rstd[0:rows, t:t + 1], ymv[0:rows, 1:2], ACT.Sqrt).then_inc(y_std, 1)
                act.wait_ge(y_norm_in, t + 1)
                nc.scalar.activation(y[0:rows, t, :], y[0:rows, t, :], ACT.Identity,
                                     scale=y_rstd[0:rows, t:t + 1], bias=y_shift[0:rows, t:t + 1]).then_inc(y_norm, 1)

        @block.vector
        def _(dve):
            steps = [0]

            def link(ins):
                steps[0] += 1
                ins.then_inc(dve_step, 1)
                dve.wait_ge(dve_step, steps[0])

            link(nc.vector.memset(ones[:, :], 1.0 / DC))
            link(nc.vector.memset(mv, 1.0))
            for g in range(4 * TILES):
                t, q = g // 4, g % 4
                dve.wait_ge(xhi_ready, g + 1)
                cols = slice(t * P, t * P + ROWS[t])
                nc.vector.tensor_tensor(xlo[:, 4 * q:4 * q + 4, cols],
                                        ps[:, g % 8, :].rearrange("p (k t) -> p k t", k=4)[:, :, 0:ROWS[t]],
                                        xhi[:, 4 * q:4 * q + 4, cols].bitcast(F32), ALU.subtract
                                        ).then_inc(xlo_ready, 1)

            dve.wait_ge(ikiw_ready, 2)
            dve.wait_ge(dw_here, 16 * 6)
            for t in range(TILES):
                r = ROWS[t]
                link(nc.vector.bn_stats(st[0:r, 6 * t:6 * t + 6], ikiw[0:r, t, 0:IDIM]))
                link(nc.vector.bn_aggr(mv[0:r, 2 * t:2 * t + 2], st[0:r, 6 * t:6 * t + 6]))
            var = mv.rearrange("p (t c) -> p t c", c=2)[:, :, 1]
            nc.vector.tensor_scalar(var, var, EPS, None, ALU.add).then_inc(ik_var, 1)
            dve.wait_ge(ik_std, 1)
            link(nc.vector.reciprocal(rs, rs))
            for t in range(TILES):
                r = ROWS[t]
                a = ik_norm[0:r, t, 0, :]
                link(nc.vector.tensor_scalar(a, ikiw[0:r, t, 0:IDIM], mv[0:r, 2 * t:2 * t + 1], rs[0:r, t:t + 1],
                                             ALU.subtract, ALU.mult))
                link(nc.vector.tensor_tensor(a, a, idx_gb[0:r, 0, :], ALU.mult))
                link(nc.vector.tensor_tensor(a, a, idx_gb[0:r, 1, :], ALU.add))
                nc.vector.tensor_copy(ik_norm[0:r, t, 1, :], a).then_inc(ik_ready, 1)

            dve.wait_ge(tile_taken, 8 + 2)
            for j in range(IH // 2):
                nc.vector.tensor_copy(iq_new[:, :, DS * j:DS * j + DS],
                                      iqT[:, j, LP:TOK].rearrange("p (b t) -> p b t", b=DB)).then_inc(iq_new_ready, 1)

            link(nc.vector.memset(w_sel[:, :, :], 0.0))
            dve.wait_ge(wcol_here, 16 * IH)
            for b in range(DB):
                nc.vector.tensor_scalar(w_sel[:, b, LAST + DS * b:LAST + DS * b + DS], cst[:, C_DIV:C_DIV + DS],
                                        wcol[:, b:b + 1], None, ALU.mult).then_inc(wsel_ready, 1)

            def sc(i):
                rows = P if i < 4 else ROWS[4]
                return bias[0:rows, bias_at[i]:bias_at[i] + bias_w[i]]

            link(nc.vector.memset(sc(4), 0.0))
            for u in range(64):
                i, h = 1 + u // IH, u % IH
                rows, n = (P if i < 4 else LAST), min((i + 1) * P, LP)
                dst = sc(i)[0:rows, (PAD if i == 4 else 0):][:, 0:n]
                w = ikiw[0:rows, i, IDIM + h:IDIM + h + 1]
                dve.wait_ge(relu_ready, u + 1)
                if h == 0:
                    nc.vector.tensor_scalar(dst, scores[0:rows, u % 2, 0:n], w, None, ALU.mult).then_inc(relu_used, 1)
                else:
                    dve.wait_ge(relu_used, u)
                    nc.vector.scalar_tensor_tensor(dst, scores[0:rows, u % 2, 0:n], w, dst, ALU.mult, ALU.add
                                                   ).then_inc(relu_used, 1)
            dve.wait_ge(relu_used, 64)
            for i in range(1, 4):
                link(nc.vector.tensor_tensor(sc(i)[:, i * P:(i + 1) * P], sc(i)[:, i * P:(i + 1) * P],
                                             cst[:, C_TRI:C_TRI + P], ALU.add))
            last = sc(4)
            dve.wait_ge(sample_scored, 1)
            link(nc.vector.tensor_tensor(last[:, PAD:PAD + LS], last[:, PAD:PAD + LS], ps_t[0:ROWS[4], 0:LS], ALU.add))
            nc.vector.tensor_copy(last[:, 0:PAD], cst[0:ROWS[4], C_PAD:C_PAD + PAD]).then_inc(scores_done, 1)
            dve.wait_ge(scores_done, 1)
            link(nc.vector.tensor_tensor(last[:, PAD + 4 * P:], last[:, PAD + 4 * P:],
                                         cst[0:ROWS[4], C_NEW:C_NEW + META], ALU.add))

            done = 0
            for i, rounds in ((1, TOP_P // 8), (2, TOP_P // 8), (3, TOP_P // 8), (4, (TOP_S + 6) // 8)):
                rows = P if i < 4 else ROWS[4]
                with dve.Fori(0, rounds) as r:
                    nc.vector.max(top8[0:rows, :], sc(i)).then_inc(topk_step, 1)
                    dve.wait_ge(topk_step, done + 1 + r * 2)
                    nc.vector.memset(wait_carrier, 0.0)
                    nc.vector.match_replace(sc(i), top8[0:rows, :], sc(i), TAKEN).then_inc(topk_step, 1)
                    dve.wait_ge(topk_step, done + 2 + r * 2)
                done += 2 * rounds

            dve.wait_ge(consts2_here, 32)
            for i in range(1, 5):
                rows = P if i < 4 else ROWS[4]
                s = sc(i) if i < 4 else sc(4)[:, PAD:]
                n = bias_w[i] if i < 4 else LP
                link(nc.vector.tensor_scalar(s, s, BETWEEN, FAR, ALU.is_ge, ALU.mult))
                dist = dist_c[0:rows, 0:n] if i < 4 else dist_c[0:rows, LP:LP + n]
                nc.vector.scalar_tensor_tensor(s, dist, float(-i * P) if i < 4 else 0.0, s, ALU.add, ALU.add
                                               ).then_inc(bias_ready, 1)
            link(nc.vector.tensor_scalar(sc(0), cst[:, C_TRI:C_TRI + P], 1e-6, None, ALU.mult))
            nc.vector.tensor_tensor(sc(0), sc(0), dist_c[:, 0:P], ALU.add).then_inc(bias_ready, 1)
            dve.wait_ge(bias_ready, TILES)
            for s in gate_stored:
                dve.wait_ge(s, 16 * 16)
            units = [(i, h) for i in range(TILES) for h in range(HEADS)]
            for s in range(len(units) + 3):
                if s < len(units):
                    i, h = units[s]
                    rows, n = (P if i < 4 else LAST), min((i + 1) * P, LP)
                    b = s % 2
                    t = scores[0:rows, b, 0:n]
                    dist = sc(i)[0:rows, 0:n] if i < 4 else sc(4)[0:rows, PAD:PAD + n]
                    dve.wait_ge(logits_out, s + 1)
                    if s >= 2:
                        dve.wait_ge(pT_out, s - 1)
                    nc.vector.scalar_tensor_tensor(t, dist, 2.0 ** -(h + 1.0),
                                                   ps_t[0:rows, 2048 + 1024 * b:2048 + 1024 * b + n],
                                                   ALU.mult, ALU.add).then_inc(logits_taken, 1)
                    dve.wait_ge(logits_taken, s + 1)
                    nc.vector.tensor_reduce(neg_max[0:rows, b:b + 1], t, AX_X, ALU.max, negate=True
                                            ).then_inc(max_ready, 1)
                if 1 <= s <= len(units):
                    u = s - 1
                    i, h = units[u]
                    rows, n = (P if i < 4 else LAST), min((i + 1) * P, LP)
                    b = u % 2
                    t = scores[0:rows, b, 0:n]
                    dve.wait_ge(exp_ready, u + 1)
                    link(nc.vector.reciprocal(inv_sum[0:rows, b:b + 1], exp_sum[0:rows, b:b + 1]))
                    nc.vector.tensor_scalar(t, t, inv_sum[0:rows, b:b + 1], None, ALU.mult).then_inc(probs_ready, 1)
                if s >= 3:
                    u = s - 3
                    i, h = units[u]
                    rows = P if i < 4 else LAST
                    dve.wait_ge(o_out, u + 1)
                    nc.vector.tensor_copy(qT[:, h, i * P:i * P + rows], ps[:, 2 + u % 2, 0:rows]).then_inc(o_taken, 1)

            for h in range(HEADS):
                r = h % GROUP
                nc.vector.tensor_copy(q_new[:, h // GROUP, :, DS * r:DS * r + DS],
                                      qT[:, h, LP:TOK].rearrange("p (b t) -> p b t", b=DB)).then_inc(q_new_ready, 1)
            for half in range(2):
                dve.wait_ge(rep_out, half + 1)
                nc.vector.tensor_copy(bias_s[:, :], ps_t[:, 2048:2048 + LS]).then_inc(rep_taken, 1)
                dve.wait_ge(rep_taken, half + 1)
                for g in range(2):
                    dve.wait_ge(s_logits, 4 * half + 4)
                    t = scores[:, g, 0:LS]
                    link(nc.vector.scalar_tensor_tensor(t, bias_s[:, :], cst[:, C_SLOPE + g:C_SLOPE + g + 1],
                                                        ps_t[:, 2048 + 1024 * g:2048 + 1024 * g + LS],
                                                        ALU.mult, ALU.add))
                    nc.vector.tensor_reduce(neg_max[:, g:g + 1], t, AX_X, ALU.max, negate=True).then_inc(s_max, 1)
                for g in range(2):
                    t = scores[:, g, 0:LS]
                    dve.wait_ge(s_exp, 2 * half + g + 1)
                    link(nc.vector.reciprocal(inv_sum[:, g:g + 1], exp_sum[:, g:g + 1]))
                    nc.vector.tensor_scalar(t, t, inv_sum[:, g:g + 1], None, ALU.mult).then_inc(s_probs, 1)
                dve.wait_ge(s_o_out, half + 1)
                for g in range(2):
                    at0 = LP + 32 * half
                    ins = nc.vector.tensor_copy(
                        qT[:, 4 * g:4 * g + 4, at0:at0 + 32].rearrange("p r (b t) -> p r b t", b=4),
                        ps[:, 4 + 2 * g, 0:P].rearrange("p (b r t) -> p r b t", b=4, r=4))
                    link(ins)
                dve.sem_inc(s_o_taken, 1)

            for c in range(16):
                j, part = c // 2, c % 2
                dve.wait_ge(state_out, c + 1)
                if c == 0:
                    link(nc.vector.memset(U[:, :, 0:TAIL], 0.0))
                nc.vector.tensor_copy(sample_cols(U, j)[:, 4 * part:4 * part + 4, 0:TAIL],
                                      ps[:, 4 + c % 4, 0:4 * TAIL].rearrange("p (b t) -> p b t", b=4)
                                      ).then_inc(state_taken, 1)
            link(nc.vector.tensor_scalar(half_g, dwT[:, :, CW + 1], 0.5, None, ALU.mult))
            link(nc.vector.tensor_scalar(half_b, dwT[:, :, CW + 2], 0.5, None, ALU.mult))

            link(nc.vector.memset(c_sum[:, :], 0.0))
            TAPS = 4
            ENDS = TAPS + 2 * CW
            PER = ENDS + 2
            with dve.Fori(0, 8) as j:
                row = U[:, ds(j, 1), :].rearrange("p a w -> p (a w)")
                new = sample_cols(U, j)
                t = zc[:, ds(j, 1), :].rearrange("p a w -> p (a w)")
                accs = c_acc[:, LP:TOK].rearrange("p (b t) -> p b t", b=DB)
                tail = tailT[:, ds(j, 1), :].rearrange("p a w -> p (a w)")
                dve.wait_ge(tile_taken, N_CU + 2 - C_OF + 2 + j * 2)
                nc.vector.scalar_tensor_tensor(row[:, TAIL:EXT], t[:, 0:LP], 1.0, row[:, TAIL:EXT], ALU.add, ALU.mult
                                               ).then_inc(conv_step, 1)
                nc.vector.scalar_tensor_tensor(new[:, :, TAIL:], t[:, LP:TOK].rearrange("p (b t) -> p b t", b=DB),
                                               1.0, new[:, :, TAIL:], ALU.add, ALU.mult).then_inc(conv_step, 1)
                dve.wait_ge(conv_step, 2 + j * PER)
                nc.vector.tensor_copy(tail[:, 0:TAIL], row[:, EXT - TAIL:EXT]).then_inc(conv_step, 1)
                nc.vector.tensor_copy(tail[:, TAIL:].rearrange("p (b t) -> p b t", b=DB), new[:, :, TAIL:]
                                      ).then_inc(conv_step, 1)
                dve.wait_ge(conv_step, TAPS + j * PER)
                dve.sem_inc(tailT_ready, 1)
                for k in range(CW):
                    w = dwT[:, ds(j, 1), k:k + 1].rearrange("p a k -> p (a k)")
                    out_p = c_acc[:, 0:LP] if k < CW - 1 else row[:, TAIL:EXT]
                    out_s = accs if k < CW - 1 else new[:, :, TAIL:]
                    if k == 0:
                        bd = dwT[:, ds(j, 1), CW:CW + 1].rearrange("p a k -> p (a k)")
                        nc.vector.tensor_scalar(out_p, row[:, 0:LP], w, bd, ALU.mult, ALU.add).then_inc(conv_step, 1)
                        nc.vector.tensor_scalar(out_s, new[:, :, 0:DS], w, bd, ALU.mult, ALU.add
                                                ).then_inc(conv_step, 1)
                    else:
                        dve.wait_ge(conv_step, TAPS + 2 * k - 1 + j * PER)
                        nc.vector.scalar_tensor_tensor(out_p, row[:, k:k + LP], w, c_acc[:, 0:LP], ALU.mult, ALU.add
                                                       ).then_inc(conv_step, 1)
                        dve.wait_ge(conv_step, TAPS + 2 * k + j * PER)
                        nc.vector.scalar_tensor_tensor(out_s, new[:, :, k:k + DS], w, accs, ALU.mult, ALU.add
                                                       ).then_inc(conv_step, 1)
                dve.wait_ge(conv_step, ENDS + j * PER)
                sums = c_sum[:, LP:TOK].rearrange("p (b t) -> p b t", b=DB)
                nc.vector.tensor_tensor(c_sum[:, 0:LP], c_sum[:, 0:LP], row[:, TAIL:EXT], ALU.add
                                        ).then_inc(conv_step, 1)
                nc.vector.tensor_tensor(sums, sums, new[:, :, TAIL:], ALU.add).then_inc(conv_step, 1)
                dve.wait_ge(conv_step, PER + j * PER)
            dve.sem_inc(conv_done, 1)

            def dev(j):
                row = U[:, j, :]
                link(nc.vector.tensor_tensor(row[:, TAIL:TAIL + HALF], row[:, TAIL:TAIL + HALF], ps[:, 6, 0:HALF],
                                             ALU.subtract))
                link(nc.vector.tensor_tensor(row[:, TAIL + HALF:EXT], row[:, TAIL + HALF:EXT],
                                             ps[:, 7, 0:LP - HALF], ALU.subtract))
                link(nc.vector.tensor_tensor(sample_cols(U, j)[:, :, TAIL:], sample_cols(U, j)[:, :, TAIL:],
                                             ps[:, 7, LP - HALF:HALF].rearrange("p (b t) -> p b t", b=DB),
                                             ALU.subtract))

            def branch_input(j):
                dve.wait_ge(tanh_ready, j + 1)
                link(nc.vector.scalar_tensor_tensor(U[:, j, 0:TOK], U[:, j, 0:TOK], 1.0, tmp_lin[:, j % 2, :],
                                                    ALU.add, ALU.mult))
                dve.wait_ge(zc_done, j + 1)
                nc.vector.tensor_tensor(zc[:, j, :], zc[:, j, :], U[:, j, 0:TOK], ALU.mult).then_inc(c_ready, 1)

            dve.wait_ge(mean_out, 1)
            for j in range(8):
                row, new = U[:, j, :], sample_cols(U, j)[:, :, TAIL:]
                dev(j)
                accs = c_acc[:, LP:TOK].rearrange("p (b t) -> p b t", b=DB)
                dst, dsts = (c_sum, c_sum[:, LP:TOK].rearrange("p (b t) -> p b t", b=DB)) if j == 0 else (c_acc, accs)
                link(nc.vector.tensor_tensor(dst[:, 0:LP], row[:, TAIL:EXT], row[:, TAIL:EXT], ALU.mult))
                link(nc.vector.tensor_tensor(dsts, new, new, ALU.mult))
                if j:
                    link(nc.vector.tensor_tensor(c_sum[:, :], c_sum[:, :], c_acc[:, :], ALU.add))
            dve.sem_inc(sq_ready, 1)
            dve.wait_ge(var_out, 1)
            nc.vector.tensor_scalar(c_sum[:, :].rearrange("p (h t) -> p h t", h=2), ps[:, 4:6, 0:HALF], EPS, None,
                                    ALU.add).then_inc(std_in, 1)
            dve.wait_ge(std_ready, 1)
            link(nc.vector.reciprocal(c_rstd[:, :], c_rstd[:, :]))
            for j in range(8):
                row, new = U[:, j, :], sample_cols(U, j)[:, :, TAIL:]
                link(nc.vector.tensor_tensor(row[:, TAIL:EXT], row[:, TAIL:EXT], c_rstd[:, 0:LP], ALU.mult))
                nc.vector.tensor_tensor(new, new, c_rstd[:, LP:TOK].rearrange("p (b t) -> p b t", b=DB), ALU.mult
                                        ).then_inc(n_ready, 1)
                if j >= 1:
                    branch_input(j - 1)
            branch_input(7)
            for k in range(KC):
                dve.wait_ge(xhi_ready, 4 * TILES + k + 1)
                src = qT[:, k, :] if k < 8 else zc[:, k - 8, :]
                nc.vector.tensor_tensor(xlo[:, k, :], src, xhi[:, k, :].bitcast(F32), ALU.subtract
                                        ).then_inc(xlo_ready, 1)

            def low_mixed(j):
                dve.wait_ge(mhi_ready, j + 1)
                nc.vector.tensor_tensor(mlo[:, j, :], m_tmp[:, j % 2, :], mhi[:, j, :].bitcast(F32), ALU.subtract
                                        ).then_inc(mlo_ready, 1)

            for j in range(KC):
                o = 4 * (j % 2)
                dve.wait_ge(gate_here[j // 2], 32)
                dve.wait_ge(block_used, N_BR + j + 1)
                for c, g in ((0, gate0), (1, gate1)):
                    gv = g[:, j, :].rearrange("p (h t) -> p h t", h=2)
                    ins = nc.vector.scalar_tensor_tensor(gv, gv, 1.0, ps[:, o + 2 * c:o + 2 * c + 2, 0:HALF],
                                                         ALU.add, ALU.mult)
                    link(ins)
                dve.sem_inc(br_taken, 1)
                nc.vector.tensor_tensor(m_tmp[:, j % 2, :], gate0[:, j, :], gate1[:, j, :], ALU.add
                                        ).then_inc(m_ready, 1)
                low_mixed(j)
                if j == KC - 2:
                    dve.sem_inc(y_taken, 4)
            dve.sem_inc(y_taken, 1)

            def scaled(t):
                r = ROWS[t]
                dve.wait_ge(y_norm, t + 1)
                dve.wait_ge(post_here, 32)
                link(nc.vector.tensor_tensor(y[0:r, t, :], y[0:r, t, :], post_g[0:r, :], ALU.mult))
                nc.vector.tensor_tensor(y[0:r, t, :], y[0:r, t, :], post_b[0:r, :], ALU.add).then_inc(y_final, 1)

            for n in range(4):
                for t in range(TILES):
                    r = ROWS[t]
                    if n == 0:
                        dve.wait_ge(y_scaled, t + 1)
                    if t < 4:
                        dve.wait_ge(y_out, 4 * n + t + 1)
                    else:
                        dve.wait_ge(block_used, N_WO + 4 * n + 4)
                    dst = y[0:r, t, 512 * n:512 * n + 512]
                    nc.vector.scalar_tensor_tensor(dst, ps[0:r, t, :], 0.5, dst, ALU.mult, ALU.add
                                                   ).then_inc(y_taken, 1)
                    if n == 3:
                        dve.wait_ge(y_taken, TILES * (n + 1) + t + 1)
                        for c in range(4):
                            link(nc.vector.bn_stats(yst[0:r, 6 * c:6 * c + 6], y[0:r, t, 512 * c:512 * c + 512]))
                        if t:
                            dve.wait_ge(y_norm, t)
                        link(nc.vector.bn_aggr(ymv[0:r, :], yst[0:r, :]))
                        nc.vector.tensor_scalar(ymv[0:r, 1:2], ymv[0:r, 1:2], EPS, None, ALU.add).then_inc(y_var, 1)
                        dve.wait_ge(y_std, t + 1)
                        link(nc.vector.reciprocal(y_rstd[0:r, t:t + 1], y_rstd[0:r, t:t + 1]))
                        nc.vector.scalar_tensor_tensor(y_shift[0:r, t:t + 1], ymv[0:r, 0:1], -1.0,
                                                       y_rstd[0:r, t:t + 1], ALU.mult, ALU.mult
                                                       ).then_inc(y_norm_in, 1)
                        if t >= 1:
                            scaled(t - 1)
            scaled(TILES - 1)

        @block.tensor
        def _(pe):
            mm = nc.tensor.matmul

            def block_ready(n):
                pe.wait_ge(lo_ready, n + 1)

            def rows_block(n, buf, act_hi, act_lo, k0, first, last, out_sem, empty=None):
                block_ready(n)
                w = [t[:, buf, :].rearrange("p (k c) -> p k c", k=4) for t in (whi, wlo)]
                for t in range(TILES):
                    r = ROWS[t]
                    cols = slice(t * P, t * P + r)
                    if empty is not None:
                        pe.wait_ge(y_taken, empty + t + 1)
                    for k in range(4):
                        for m, (a, b) in enumerate(((act_hi, 0), (act_lo, 0), (act_hi, 1))):
                            ins = mm(ps[0:r, t, :], a[:, k0 + k, cols], w[b][:, k, :],
                                     start=(first and k == 0 and m == 0), stop=(last and k == 3 and m == 2))
                    if t == TILES - 1:
                        ins.then_inc(block_used, 1)
                    elif last:
                        ins.then_inc(out_sem, 1)

            def tile_block(buf, bank, k0=0, kn=KC):
                w = [t[:, buf, :].rearrange("p (k c) -> p k c", k=KC) for t in (whi, wlo)]
                for k in range(k0, k0 + kn):
                    for m, (b, x) in enumerate(((0, xhi), (0, xlo), (1, xhi))):
                        for half in range(2):
                            ins = mm(ps[:, bank + half, 0:HALF], w[b][:, k, :],
                                     x[:, k, half * HALF:(half + 1) * HALF],
                                     start=(k == k0 and m == 0), stop=(k == k0 + kn - 1 and m == 2))
                return ins

            def tile_pair(n0, i):
                for b in range(2):
                    n = n0 + b
                    block_ready(n + i * 2)
                    pe.wait_ge(tile_taken, n - C_OF + 1 + i * 2)
                    tile_block(n % 2, 2 * b).then_inc(block_used, 1)

            def tiles(n0, count):
                with pe.Fori(0, count // 2) as i:
                    tile_pair(n0, i)

            pe.wait_ge(consts_here, 16)
            for g in range(4 * TILES):
                t, q = g // 4, g % 4
                if q == 0:
                    pe.wait_ge(x_here[t], 32 if t in (0, 4) else 16)
                if g >= 8:
                    pe.wait_ge(xlo_ready, g - 7)
                r = ROWS[t]
                for k in range(4):
                    ins = nc.tensor.transpose(ps[:, g % 8, k * P:k * P + r],
                                              xn[0:r, t, (4 * q + k) * P:(4 * q + k + 1) * P], cst[0:r, C_ID:C_ID + r])
                ins.then_inc(xT_out, 1)
            pe.wait_ge(xlo_ready, 4 * TILES)
            for n in range(4):
                rows_block(n, n % 2, xhi, xlo, 4 * n, n == 0, n == 3, kv_out)
            block_ready(N_IK)
            w = [t[:, 0, 0:KC * 80].rearrange("p (k c) -> p k c", k=KC) for t in (whi, wlo)]
            for t in range(TILES):
                for k in range(KC):
                    for m, (a, b) in enumerate(((xhi, 0), (xlo, 0), (xhi, 1))):
                        ins = mm(ps[0:ROWS[t], 5, 80 * t:80 * t + 80], a[:, k, t * P:t * P + ROWS[t]], w[b][:, k, :],
                                 start=(k == 0 and m == 0), stop=(k == KC - 1 and m == 2))
            ins.then_inc(block_used, 1)
            tiles(N_IQ, 8)
            pe.wait_ge(tile_taken, 8 + 2)
            pe.wait_ge(kv_ready, TILES)
            pe.wait_ge(ikiw_ready, 2)
            for g in range(2):
                for t in range(4):
                    ins = nc.tensor.transpose(ps[:, 4 + g, t * P:t * P + P], kv[:, t, g * P:g * P + P], ident)
            ins.then_inc(turned, 1)
            r = ROWS[4]
            for g in range(2):
                ins = nc.tensor.transpose(ps[:, 6, 80 * g:80 * g + 80], kv[0:r, 4, g * P:g * P + P],
                                          cst[0:r, C_ID:C_ID + r])
            ins.then_inc(turned, 1)
            pe.wait_ge(ik_ready, TILES)
            for t in range(4):
                ins = nc.tensor.transpose(ps[:, 7, t * P:t * P + P],
                                          ik_norm[:, t, :, :].rearrange("p c d -> p (c d)"), ident)
            ins.then_inc(turned, 1)
            nc.tensor.transpose(ps[:, 2, 0:80], ik_norm[0:r, 4, :, :].rearrange("p c d -> p (c d)"),
                                cst[0:r, C_ID:C_ID + r]).then_inc(turned, 1)
            pe.wait_ge(dw_here, 16 * 6)
            for j in range(8):
                ins = nc.tensor.transpose(ps[:, 3, j * (CW + 3):(j + 1) * (CW + 3)], dw_rows[:, j * P:(j + 1) * P],
                                          cst[0:CW + 3, C_ID:C_ID + CW + 3])
            ins.then_inc(turned, 1)
            pe.wait_ge(turned_taken, 5)

            for u in range(64):
                i, h = 1 + u // IH, u % IH
                rows, n = (P if i < 4 else LAST), min((i + 1) * P, LP)
                half = slice(64 * (h % 2), 64 * (h % 2) + 64)
                if u >= 2:
                    pe.wait_ge(relu_ready, u - 1)
                o = 2048 + 1024 * (u % 2)
                lhs = iqT[half, h // 2, i * P:i * P + rows]
                ins = mm(ps_t[0:rows, o:o + min(n, 512)], lhs, ikT[half, 0:min(n, 512)], start=True, stop=True)
                if n > 512:
                    ins = mm(ps_t[0:rows, o + 512:o + n], lhs, ikT[half, 512:n], start=True, stop=True)
                ins.then_inc(idx_out, 1)

            def turn_idx(b):
                pe.wait_ge(idx_here[b % 2], 16 * 8 * (b // 2 + 1))
                if b >= 2:
                    pe.wait_ge(idx_kT_ready, b - 1)
                for n in range(PAGES):
                    ins = nc.tensor.transpose(ps[:, 2 + b % 2, n * P:n * P + P],
                                              idx_page[:, b % 2, n, :, :].rearrange("p c d -> p (c d)"), ident)
                ins.then_inc(idx_turned, 1)

            turn_idx(0)
            pe.wait_ge(wsel_ready, DB)
            pe.wait_ge(iq_new_ready, IH // 2)
            for b in range(DB):
                if b + 1 < DB:
                    turn_idx(b + 1)
                pe.wait_ge(idx_kT_ready, b + 1)
                pe.wait_ge(relu_ready, 64 if b < 2 else 63 + b)
                o = 2048 + 1024 * (b % 2)
                at0 = LP + DS * b
                for par in range(2):
                    half = slice(64 * par, 64 * par + 64)
                    lhs = iq_new[half, b, :]
                    mm(ps_t[half, o:o + PAST], lhs, idx_kT[half, b % 2, :], start=True, stop=True)
                    ins = mm(ps_t[half, o + PAST:o + LS], lhs, ikT[half, at0:at0 + DS], start=True, stop=True)
                ins.then_inc(idx_out, 1)
                pe.wait_ge(relu_ready, 65 + b)
                r = ROWS[4]
                mm(ps[0:r, 0, :], w_sel[:, b, :], scores[:, b % 2, 0:PAST], start=(b == 0), stop=(b == DB - 1))
                ins = mm(ps[0:r, 1, 0:DS], w_sel[:, b, :], scores[:, b % 2, PAST:LS], start=(b == 0),
                         stop=(b == DB - 1))
                ins.then_inc(relu_used, 1) if b < DB - 1 else ins.then_inc(sample_scored, 1)
            pe.wait_ge(scores_done, 1)

            tiles(N_Q, 8)
            tiles(N_GT, 32)
            pe.wait_ge(tile_taken, N_ZA - C_OF + 2)

            pe.wait_ge(bias_ready, TILES)
            units = [(i, h) for i in range(TILES) for h in range(HEADS)]
            for s in range(len(units) + 2):
                if s < len(units):
                    i, h = units[s]
                    rows, n = (P if i < 4 else LAST), min((i + 1) * P, LP)
                    o = 2048 + 1024 * (s % 2)
                    if s >= 2:
                        pe.wait_ge(logits_taken, s - 1)
                    lhs = qT[:, h, i * P:i * P + rows]
                    ins = mm(ps_t[0:rows, o:o + min(n, 512)], lhs, kT[:, h // GROUP, 0:min(n, 512)],
                             start=True, stop=True)
                    if n > 512:
                        ins = mm(ps_t[0:rows, o + 512:o + n], lhs, kT[:, h // GROUP, 512:n], start=True, stop=True)
                    ins.then_inc(logits_out, 1)
                if 1 <= s <= len(units):
                    u = s - 1
                    i, h = units[u]
                    rows = P if i < 4 else LAST
                    pe.wait_ge(probs_ready, u + 1)
                    if u >= 2:
                        pe.wait_ge(pT_ready, u - 1)
                    for c in range(i + 1):
                        w = P if c < 4 else LAST
                        ins = nc.tensor.transpose(ps[0:w, u % 2, c * rows:(c + 1) * rows],
                                                  scores[0:rows, u % 2, c * P:c * P + w], cst[0:rows, C_ID:C_ID + rows])
                    ins.then_inc(pT_out, 1)
                if s >= 2:
                    u = s - 2
                    i, h = units[u]
                    rows = P if i < 4 else LAST
                    pe.wait_ge(pT_ready, u + 1)
                    if u >= 2:
                        pe.wait_ge(o_taken, u - 1)
                    g0 = KVH * DH + (h // GROUP) * DH
                    for c in range(i + 1):
                        w = P if c < 4 else LAST
                        ins = mm(ps[:, 2 + u % 2, 0:rows], kv[0:w, c, g0:g0 + DH], pT[0:w, u % 2, c * rows:(c + 1) * rows],
                                 start=(c == 0), stop=(c == i))
                    ins.then_inc(o_out, 1)

            pe.wait_ge(logits_taken, len(units))
            pe.wait_ge(pT_ready, len(units))
            pe.wait_ge(o_taken, len(units))
            pe.wait_ge(v_new_here, 16)
            pe.wait_ge(q_new_ready, HEADS)
            for half in range(2):
                if half:
                    pe.wait_ge(s_o_taken, 1)
                r = ROWS[4]
                s4 = bias[0:r, bias_at[4] + PAD:bias_at[4] + PAD + LS]
                rep = rep_c[0:r, half * P:(half + 1) * P]
                mm(ps[:, 4, :], rep, s4[:, 0:512], start=True, stop=True)
                mm(ps[:, 5, 0:DS], rep, s4[:, 512:LS], start=True, stop=True).then_inc(rep_out, 1)
                for b4 in range(4):
                    b = 4 * half + b4
                    pe.wait_ge(kpage_here, 16 * PAGES * (b + 1))
                    if b:
                        pe.wait_ge(kTs_ready, b)
                    for g in range(2):
                        for n in range(PAGES):
                            ins = nc.tensor.transpose(ps[:, g, n * P:n * P + P], kpage[:, n, g * DH:(g + 1) * DH], ident)
                    ins.then_inc(kTs_out, 1)
                    pe.wait_ge(kTs_ready, b + 1)
                    if b4 == 0:
                        pe.wait_ge(rep_taken, half + 1)
                    at0 = LP + DS * b
                    for g in range(2):
                        o = 2048 + 1024 * g
                        lhs = q_new[:, g, b, :]
                        rows = slice(32 * b4, 32 * b4 + 32)
                        mm(ps_t[rows, o:o + PAST], lhs, kTs[:, g, :], start=True, stop=True)
                        ins = mm(ps_t[rows, o + PAST:o + LS], lhs, kT[:, g, at0:at0 + DS], start=True, stop=True)
                    ins.then_inc(s_logits, 1)
                for g in range(2):
                    pe.wait_ge(s_probs, 2 * half + g + 1)
                    for n in range(PAGES):
                        nc.tensor.transpose(ps[:, g, n * P:n * P + P], scores[:, g, n * P:n * P + P], ident)
                    nc.tensor.transpose(ps[0:DS, 2 + g, 0:P], scores[:, g, PAST:LS], ident).then_inc(s_pT_out, 1)
                pe.wait_ge(vpage_here, 16 * PAGES * 4 * (half + 1))
                for g in range(2):
                    pe.wait_ge(s_pT_ready, 2 * half + g + 1)
                    for b4 in range(4):
                        cols = slice(32 * b4, 32 * b4 + 32)
                        for n in range(PAGES):
                            mm(ps[:, 4 + 2 * g, cols], vpage[:, b4, n, g * DH:(g + 1) * DH],
                               pT[:, g, n * P + 32 * b4:n * P + 32 * b4 + 32], start=(n == 0), stop=False)
                        ins = mm(ps[:, 4 + 2 * g, cols], v_new[:, 4 * half + b4, g * DH:(g + 1) * DH],
                                 pT_new[:, g, cols], start=False, stop=True)
                ins.then_inc(s_o_out, 1)
            pe.wait_ge(s_o_taken, 2)

            tiles(N_ZA, 8)
            pe.wait_ge(state_here, 32)
            for c in range(16):
                j, part = c // 2, c % 2
                if c >= 4:
                    pe.wait_ge(state_taken, c - 3)
                nc.tensor.transpose(ps[:, 4 + c % 4, 0:4 * TAIL], state[0:4 * TAIL, part, j * P:(j + 1) * P],
                                    cst[0:4 * TAIL, C_ID:C_ID + 4 * TAIL]).then_inc(state_out, 1)
            pe.wait_ge(state_taken, 16)
            tiles(N_CU, 16)
            tiles(N_ZC, 4)
            pe.wait_ge(tailT_ready, 8)
            for j in range(8):
                ins = nc.tensor.transpose(ps[0:TAIL + DB * DS, 4 + j // 4, (j % 4) * P:(j % 4 + 1) * P],
                                          tailT[:, j, :], ident)
            ins.then_inc(tail_out, 1)
            pe.wait_ge(conv_done, 1)
            for half in range(2):
                ins = mm(ps[:, 6 + half, 0:HALF], ones[:, :], c_sum[:, half * HALF:(half + 1) * HALF],
                         start=True, stop=True)
            ins.then_inc(mean_out, 1)
            tile_pair(N_ZC + 4, 0)
            pe.wait_ge(sq_ready, 1)
            pe.wait_ge(tail_ready, 1)
            for half in range(2):
                ins = mm(ps[:, 4 + half, 0:HALF], ones[:, :], c_sum[:, half * HALF:(half + 1) * HALF],
                         start=True, stop=True)
            ins.then_inc(var_out, 1)
            tile_pair(N_ZC + 6, 0)

            pe.wait_ge(tile_taken, N_BR - C_OF + 2)
            block_ready(N_BR)
            for k in range(KC):
                pe.wait_ge(xlo_ready, 4 * TILES + k + 1)
                for m, (b, x) in enumerate(((whi, xhi), (whi, xlo), (wlo, xhi))):
                    for half in range(2):
                        ins = mm(ps[:, 2 * (k // 8) + half, 0:HALF], b[:, 1, k * P:(k + 1) * P],
                                 x[:, k, half * HALF:(half + 1) * HALF],
                                 start=(k % 8 == 0 and m == 0), stop=(k % 8 == 7 and m == 2))
            ins.then_inc(block_used, 1)

            def branch(n, buf, o):
                block_ready(n)
                tile_block(buf, o, 0, 8)
                tile_block(buf, o + 2, 8, 8).then_inc(block_used, 1)

            branch(N_BR + 1, 0, 4)
            with pe.Fori(0, 7) as i:
                for b in range(2):
                    pe.wait_ge(br_taken, 1 + b + i * 2)
                    branch(N_BR + 2 + b + i * 2, (1 + b) % 2, 4 * b)

            with pe.Fori(0, 4) as i:
                for r in range(4):
                    pe.wait_ge(mlo_ready, 4 * r + 4)
                    rows_block(N_WO + r + i * 4, (N_WO + r) % 2, mhi, mlo, 4 * r, r == 0, r == 3, y_out,
                               i * TILES if r == 0 else None)

    return nc


INS = ["x_prompt", "x_sample", "cache_k", "cache_v", "cache_idx_k", "state_conv", "page_table", "meta_tokens",
       "w_in", "ln_idx_g", "ln_idx_b", "w_dw", "b_dw", "ln_conv_g", "ln_conv_b", "w_att_out", "w_conv_out", "w_o",
       "ln_post_g", "ln_post_b"]
OUTS = [(1, SEQ, D), (DB, DS, D), (1, LP, KVH, DH), (1, LP, KVH, DH), (1, LP, IDIM), (1, TAIL, DC),
        (DB, DS, KVH, DH), (DB, DS, KVH, DH), (DB, DS, IDIM), (DB, TAIL, DC)]


def kernel(**inputs):
    import numpy as _np
    import concourse.bacc as _bacc
    from concourse import mybir as _mybir
    from concourse.bass_utils import run_bass_kernel_spmd as _run

    nc = _bacc.Bacc("TRN2", target_bir_lowering=False, num_devices=1)
    arrays, args = {}, []
    for name in INS:
        arrays[f"in_{name}_dram"] = _np.ascontiguousarray(inputs[name])
    for name, a in zip(("consts", "consts2"), shape_constants()):
        arrays[f"in_{name}_dram"] = a
    for name, a in arrays.items():
        args.append(nc.dram_tensor(name, a.shape, _mybir.dt.from_np(a.dtype), kind="ExternalInput").ap())
    for i, shape in enumerate(OUTS):
        args.append(nc.dram_tensor(f"out_{i}_dram", shape, _mybir.dt.float32, kind="ExternalOutput").ap())
    build(nc, *args)
    r = _run(nc, [arrays], core_ids=[0])
    return tuple(r.results[0][f"out_{i}_dram"] for i in range(len(OUTS)))
```

```python
from contextlib import ExitStack

import concourse.bass as bass
import numpy as np
from concourse import mybir

F32 = mybir.dt.float32
F32R = mybir.dt.float32r
I32 = mybir.dt.int32
ALU = mybir.AluOpType
ACT = mybir.ActivationFunctionType
AX_X = mybir.AxisListType.X
ds = bass.ds

P = 128
D = 2048
SEQ = 512
META = 16
LP = SEQ + META
DB = 8
DS = 8
PAST = 512
PAGES = PAST // P
HEADS, DH, KVH = 8, 128, 2
GROUP = HEADS // KVH
IH, IDIM = 16, 64
DC = 1024
CW = 31
TAIL = CW - 1
ALPHA = 2.0 ** 0.25
EPS = 1e-5
TOK = LP + DB * DS
HALF = TOK // 2
KC = D // P
TILES = 5
ROWS = [P, P, P, P, TOK - 4 * P]
LAST = LP - 4 * P
LS = PAST + DS
CUT = dict(q=0, kv=1024, iq=1536, ik=2560, za=2640, ga=3664, gb=4688, zc=5712, gt=6736)

MASKED = -3.0e38
TAKEN = -3.4e38
BETWEEN = -3.2e38
FAR = -1.0e32
PAD = 8
TOP_P = 128
TOP_S = 130
EXT = TAIL + LP
UW = EXT + DB * (TAIL + DS)

N_KV, N_IK, N_IQ, N_Q, N_GT, N_ZA, N_CU, N_ZC, N_G2, N_BR, N_WO = 0, 4, 5, 13, 21, 45, 53, 69, 77, 85, 101
N_END = 117
C_OF = N_IQ
GT1 = N_ZA - N_GT

C_ID, C_TRI, C_DIV, C_SLOPE, C_PAD, C_NEW, C_END = 0, 128, 256, 264, 267, 275, 291
E_DIST, E_DIST4, E_REP, E_END = 0, LP, 2 * LP, 2 * LP + 3 * P


def shape_constants():
    c = np.zeros((P, C_END), np.float32)
    p = np.arange(P)
    c[:, C_ID:C_ID + P] = np.eye(P)
    c[:, C_TRI:C_TRI + P] = np.where(p[None, :] > p[:, None], MASKED, 0.0)
    c[:, C_DIV:C_DIV + DS] = (p[:, None] % DS) == np.arange(DS)[None, :]
    for g in range(KVH):
        c[:, C_SLOPE + g] = 2.0 ** -(1.0 + g * GROUP + (p // DS) % GROUP)
    c[:, C_SLOPE + KVH] = 2.0 ** -(1.0 + p // LAST)
    c[:, C_PAD:C_PAD + PAD] = -MASKED
    c[LAST:, C_PAD + PAD - (TOP_S - TOP_P):C_PAD + PAD] = MASKED
    new = np.zeros((P, META), np.float32)
    for r in range(ROWS[4]):
        seen = r + 1 if r < LAST else (r - LAST) % DS + 1
        new[r, seen:] = MASKED
    c[:, C_NEW:C_NEW + META] = new
    e = np.zeros((P, E_END), np.float32)
    k = np.arange(LP)
    e[:, E_DIST:E_DIST + LP] = k[None, :] - p[:, None]
    for r in range(ROWS[4]):
        at = 4 * P + r if r < LAST else PAST + (r - LAST) % DS
        e[r, E_DIST4:E_DIST4 + LP] = k - at
    for half in range(2):
        for m in range(P):
            b, t = m // (GROUP * DS), m % DS
            e[LAST + DS * (4 * half + b) + t, E_REP + half * P + m] = 1.0
    e[p % LAST, E_REP + 2 * P + p] = 1.0
    return c, e


def landed_after():
    total, out = [0, 0], []
    for n in range(N_END):
        total[n % 2] += 32 if N_BR <= n < N_WO else 16
        out.append(total[n % 2])
    return out


LANDED = landed_after()


def build(nc, x_prompt, x_sample, cache_k, cache_v, cache_idx_k, state_conv, page_table, meta_tokens,
          w_in, ln_idx_g, ln_idx_b, w_dw, b_dw, ln_conv_g, ln_conv_b, w_att_out, w_conv_out, w_o,
          ln_post_g, ln_post_b, consts, consts2,
          y_prompt, y_sample, k_prompt, v_prompt, idx_k_prompt, conv_prompt,
          k_sample, v_sample, idx_k_sample, conv_sample):
    gates = nc.dram_tensor("gates_dram", [32, P, TOK], F32)
    iw_dram = nc.dram_tensor("iw_dram", [DB * DS, IH], F32)

    base = -(-nc.sbuf_base // 32) * 32

    def at(name, shape, dt, offset):
        return nc.alloc_sbuf_tensor_at(name, shape, dt, offset=base + offset)

    XB = KC * TOK * 4
    xhi = at("xhi", [P, KC, TOK], F32R, 0)
    xlo = at("xlo", [P, KC, TOK], F32R, XB)
    y = at("y", [P, TILES, D], F32, 0)
    post_g = at("post_g", [P, D], F32, TILES * D * 4)
    post_b = at("post_b", [P, D], F32, (TILES + 1) * D * 4)
    W0 = 2 * XB
    BL = KC * P * 4
    raw = at("raw", [P, 2, KC * P], F32, W0)
    whi = at("whi", [P, 2, KC * P], F32R, W0 + 2 * BL)
    wlo = at("wlo", [P, 2, KC * P], F32R, W0 + 4 * BL)
    B0 = W0 + 6 * BL
    HB = 8 * TOK * 4
    xn = at("xn", [P, TILES, D], F32, B0)
    qT = at("qT", [P, 8, TOK], F32, B0)
    iqT = at("iqT", [P, 8, TOK], F32, B0 + HB)
    zc = at("zc", [P, 8, TOK], F32, B0 + HB)
    vpage = at("vpage", [P, 4, PAGES, 2 * DH], F32, B0 + HB)
    dist_c = at("dist_c", [P, 2 * LP], F32, B0 + HB)
    rep_c = at("rep_c", [P, 3 * P], F32, B0 + HB + 16384)
    idx_page = at("idx_page", [P, 2, PAGES, 2, IDIM], F32, B0)
    idx_kT = at("idx_kT", [P, 2, PAST], F32, B0 + 4096)
    w_sel = at("w_sel", [P, DB, ROWS[4]], F32, B0 + 8192)
    ik_norm = at("ik_norm", [P, TILES, 2, IDIM], F32, B0 + 10752)
    dw_rows = at("dw_rows", [CW + 3, DC], F32, B0 + 13312)
    idx_gb = at("idx_gb", [P, 2, IDIM], F32, B0 + 17408)
    R0 = B0 + 2 * HB
    kT = at("kT", [P, KVH, TOK], F32, R0)
    ikT = at("ikT", [P, TOK], F32, R0 + 4736)
    kv = at("kv", [P, TILES, 2 * KVH * DH], F32, R0 + 7104)
    v_new = at("v_new", [DS, DB, KVH * DH], F32, R0 + 7104)
    S0 = R0 + 17344
    bias_w = [P, 2 * P, 3 * P, 4 * P, PAD + LP]
    bias_at = [0, P, 3 * P, 6 * P, 10 * P]
    bias = at("bias", [P, sum(bias_w)], F32, S0)
    scores = at("scores", [P, 2, LP], F32, S0 + 7264)
    ikiw = at("ikiw", [P, TILES, IDIM + IH], F32, S0 + 11488)
    tmp_gate = at("tmp_gate", [P, 2, TOK], F32, S0 + 7264)
    pT = at("pT", [P, GROUP, 4 * P], F32, S0 + 12000)
    bias_s = at("bias_s", [P, LP], F32, S0 + 17184)
    q_last = at("q_last", [P, HEADS * LAST], F32, R0 + 4736)
    iq_new = at("iq_new", [P, DB, IH // 2 * DS], F32, S0 + 13088)
    q_new = at("q_new", [P, KVH, DB, GROUP * DS], F32, S0)
    pT_new = at("pT_new", [DS, 2, P], F32, S0 + 19328)
    U = at("U", [P, 8, UW], F32, R0)
    tmp_lin = at("tmp_lin", [P, 2, TOK], F32, R0 + 27584)
    tmp_tanh = at("tmp_tanh", [P, 2, TOK], F32, R0 + 27584 + 4736)
    u_tail = at("u_tail", [P, DC], F32, R0 + 27584)
    mhi = at("mhi", [P, KC, TOK], F32R, B0)
    mlo = at("mlo", [P, KC, TOK], F32R, B0 + XB)
    gate0 = at("gate0", [P, KC, TOK], F32, B0)
    gate1 = at("gate1", [P, KC, TOK], F32, B0 + XB)
    M0 = B0 + 2 * XB
    cst = at("cst", [P, C_END], F32, M0)
    ones = at("ones", [P, P], F32, M0 + 1184)
    dwT = at("dwT", [P, 8, CW + 3], F32, M0 + 1696)
    small = at("small", [P, 128], F32, M0 + 2784)
    pages = at("pages", [1, DB * PAGES], I32, M0 + 3296)
    probs = at("probs", [P, GROUP, 4 * P], F32, M0 + 3424)
    probs_last = at("probs_last", [P, LP], F32, M0 + 3424)
    kpage = at("kpage", [P, PAGES, 2 * DH], F32, M0 + 3424)
    kTs = at("kTs", [P, KVH, PAST], F32, M0 + 3424 + 4096)
    state = at("state", [P, 2, DC], F32, M0 + 3424)
    c_acc = at("c_acc", [P, TOK], F32, M0 + 3424)
    c_sum = at("c_sum", [P, TOK], F32, M0 + 3424 + 2368)
    c_rstd = at("c_rstd", [P, TOK], F32, M0 + 3424 + 4736)
    tailT = at("tailT", [P, 8, TAIL + DB * DS], F32, M0 + 3424 + 4736)
    yst = at("yst", [P, TILES, 24], F32, M0 + 3424 + 4736)
    m_tmp = at("m_tmp", [P, 2, TOK], F32, M0 + 3424)
    ident = cst[:, C_ID:C_ID + P]

    st = small[:, 0:30]
    mv = small[:, 30:40]
    rs = small[:, 40:45]
    wcol = small[:, 48:56]
    top8 = small[:, 56:64]
    neg_max = small[:, 88:92]
    exp_sum = small[:, 92:96]
    inv_sum = small[:, 96:100]
    half_g = small[:, 72:80]
    half_b = small[:, 80:88]
    ymv = small[:, 112:114]
    y_rstd = small[:, 114:119]
    y_shift = small[:, 119:124]
    wait_carrier = small[:, 124:125]

    with ExitStack() as ctx:
        ps_t = ctx.enter_context(nc.psum_tensor("ps", [P, 8 * 512], F32))
        ps = ps_t[:, :].rearrange("p (b n) -> p b n", b=8)

        def sem(name):
            return ctx.enter_context(nc.semaphore(name))

        x_here = [sem(f"x_here{i}") for i in range(TILES)]
        consts_here = sem("consts_here")
        consts2_here = sem("consts2_here")
        dw_here = sem("dw_here")
        pages_here = sem("pages_here")
        raw_here = [sem("raw_here0"), sem("raw_here1")]
        hi_ready = sem("hi_ready")
        lo_ready = sem("lo_ready")
        block_used = sem("block_used")
        xT_out = sem("xT_out")
        xhi_ready = sem("xhi_ready")
        xlo_ready = sem("xlo_ready")
        kv_out = sem("kv_out")
        kv_ready = sem("kv_ready")
        ikiw_ready = sem("ikiw_ready")
        ik_var = sem("ik_var")
        ik_std = sem("ik_std")
        ik_ready = sem("ik_ready")
        tile_taken = sem("tile_taken")
        turned = sem("turned")
        turned_taken = sem("turned_taken")
        iw_stored = sem("iw_stored")
        wcol_here = sem("wcol_here")
        wsel_ready = sem("wsel_ready")
        idx_here = [sem("idx_here0"), sem("idx_here1")]
        idx_turned = sem("idx_turned")
        idx_kT_ready = sem("idx_kT_ready")
        idx_out = sem("idx_out")
        relu_ready = sem("relu_ready")
        relu_used = sem("relu_used")
        sample_scored = sem("sample_scored")
        scores_done = sem("scores_done")
        bias_ready = sem("bias_ready")
        gate_stored = [sem("gate_stored0"), sem("gate_stored1")]
        logits_out = sem("logits_out")
        max_ready = sem("max_ready")
        exp_ready = sem("exp_ready")
        probs_ready = sem("probs_ready")
        pT_out = sem("pT_out")
        pT_ready = sem("pT_ready")
        o_out = sem("o_out")
        o_taken = sem("o_taken")
        q_last_ready = sem("q_last_ready")
        last_logits = sem("last_logits")
        last_max = sem("last_max")
        last_exp = sem("last_exp")
        last_probs = sem("last_probs")
        last_pT_out = sem("last_pT_out")
        last_pT_ready = sem("last_pT_ready")
        last_o_out = sem("last_o_out")
        last_o_taken = sem("last_o_taken")
        rep_out = sem("rep_out")
        rep_taken = sem("rep_taken")
        kpage_here = sem("kpage_here")
        vpage_here = sem("vpage_here")
        v_new_here = sem("v_new_here")
        kTs_out = sem("kTs_out")
        kTs_ready = sem("kTs_ready")
        s_logits = sem("s_logits")
        s_max = sem("s_max")
        s_exp = sem("s_exp")
        s_probs = sem("s_probs")
        s_pT_out = sem("s_pT_out")
        s_pT_ready = sem("s_pT_ready")
        s_o_out = sem("s_o_out")
        s_o_taken = sem("s_o_taken")
        za_used = sem("za_used")
        state_here = sem("state_here")
        state_out = sem("state_out")
        state_taken = sem("state_taken")
        conv_done = sem("conv_done")
        tail_out = sem("tail_out")
        tail_ready = sem("tail_ready")
        tail_stored = sem("tail_stored")
        zc_done = sem("zc_done")
        mean_out = sem("mean_out")
        sq_ready = sem("sq_ready")
        var_out = sem("var_out")
        std_in = sem("std_in")
        std_ready = sem("std_ready")
        n_ready = sem("n_ready")
        lin_ready = sem("lin_ready")
        tanh_ready = sem("tanh_ready")
        c_ready = sem("c_ready")
        gate_here = [sem(f"gate_here{i}") for i in range(8)]
        br_taken = sem("br_taken")
        m_ready = sem("m_ready")
        mhi_ready = sem("mhi_ready")
        mlo_ready = sem("mlo_ready")
        y_here = sem("y_here")
        post_here = sem("post_here")
        y_scaled = sem("y_scaled")
        y_out = sem("y_out")
        y_taken = sem("y_taken")
        y_var = sem("y_var")
        y_std = sem("y_std")
        y_norm_in = sem("y_norm_in")
        y_norm = sem("y_norm")
        y_times_g = sem("y_times_g")
        y_final = sem("y_final")
        y_final_last = sem("y_final_last")
        dve_step = sem("dve_step")
        pool_step = sem("pool_step")
        topk_step = sem("topk_step")
        conv_step = sem("conv_step")
        stored = sem("stored")
        idx_stored = sem("idx_stored")
        iq_new_ready = sem("iq_new_ready")
        q_new_ready = sem("q_new_ready")
        tailT_ready = sem("tailT_ready")

        stores = [0]

        def w_cols(c0, k0=0, kn=KC, width=P, w=w_in):
            return w[k0 * P:(k0 + kn) * P, c0:c0 + width] if isinstance(c0, int) else \
                w[k0 * P:(k0 + kn) * P, ds(c0, width)]

        groups = [(i, g) for i in range(4) for g in range(KVH)]
        GROUPS = len(groups)
        BURSTS = GROUPS + 2

        def sample_cols(a, j):
            v = a[:, j, EXT:UW] if isinstance(j, int) else a[:, ds(j, 1), EXT:UW].rearrange("p a w -> p (a w)")
            return v.rearrange("p (b w) -> p b w", b=DB)

        block = ctx.enter_context(nc.Block())

        @block.sync
        def _(sp):
            def buffer_free(n):
                sp.wait_ge(hi_ready, n - 1)
                sp.wait_ge(lo_ready, n - 1)

            def load_rows(n, w, k0, c0):
                if n >= 2:
                    buffer_free(n)
                sp.dma_start(raw[:, n % 2, :].rearrange("p (k c) -> p k c", k=4),
                             w[k0 * P:(k0 + 4) * P, c0:c0 + 512].rearrange("(k p) c -> p k c", p=P)
                             ).then_inc(raw_here[n % 2], 16)

            def load_tile(n, c0, buf):
                buffer_free(n)
                sp.dma_start(raw[:, buf, :].rearrange("p (k c) -> p k c", k=KC),
                             w_cols(c0).rearrange("(k p) c -> p k c", p=P)).then_inc(raw_here[buf], 16)

            def load_tiles(n0, count, c0, c1=None):
                with sp.Fori(0, count // 2) as i:
                    if c1 is None:
                        load_tile(n0 + i * 2, c0 + i * 256, n0 % 2)
                        load_tile(n0 + 1 + i * 2, c0 + P + i * 256, (n0 + 1) % 2)
                    else:
                        load_tile(n0 + i * 2, c0 + i * P, n0 % 2)
                        load_tile(n0 + 1 + i * 2, c1 + i * P, (n0 + 1) % 2)

            sp.dma_start(cst[:, :], consts).then_inc(consts_here, 16)
            sp.dma_start(xn[0:META, 0, :], meta_tokens).then_inc(x_here[0], 16)
            sp.dma_start(xn[META:P, 0, :], x_prompt[0, 0:P - META, :]).then_inc(x_here[0], 16)
            for t in range(1, 4):
                sp.dma_start(xn[:, t, :], x_prompt[0, t * P - META:(t + 1) * P - META, :]).then_inc(x_here[t], 16)
            sp.dma_start(xn[0:LAST, 4, :], x_prompt[0, SEQ - LAST:SEQ, :]).then_inc(x_here[4], 16)
            sp.dma_start(xn[LAST:ROWS[4], 4, :], x_sample.rearrange("b t d -> (b t) d")).then_inc(x_here[4], 16)
            sp.dma_start(pages[:, :], page_table.rearrange("(o b) n -> o (b n)", o=1)).then_inc(pages_here, 16)
            for n in range(4):
                load_rows(n, w_in, 4 * n, CUT["kv"])
            buffer_free(N_IK)
            sp.dma_start(raw[:, 0, 0:KC * 80].rearrange("p (k c) -> p k c", k=KC),
                         w_cols(CUT["ik"], width=80).rearrange("(k p) c -> p k c", p=P)).then_inc(raw_here[0], 16)
            sp.wait_ge(xT_out, 4 * TILES)
            sp.dma_start(dw_rows[0:CW, :], w_dw).then_inc(dw_here, 16)
            for r, v in enumerate((b_dw, ln_conv_g, ln_conv_b)):
                sp.dma_start(dw_rows[CW + r:CW + r + 1, :], v.rearrange("(o c) -> o c", o=1)).then_inc(dw_here, 16)
            for r, v in enumerate((ln_idx_g, ln_idx_b)):
                sp.dma_start(idx_gb[:, r, :], v.rearrange("(o c) -> o c", o=1).broadcast_to([P, IDIM])
                             ).then_inc(dw_here, 16)
            load_tiles(N_IQ, 8, CUT["iq"])
            load_tile(N_Q, CUT["q"], N_Q % 2)
            sp.wait_ge(kv_ready, TILES)
            for t in range(4):
                for c, o in ((0, k_prompt), (1, v_prompt)):
                    sp.dma_start(o[0, t * P:(t + 1) * P].rearrange("t g d -> t (g d)"),
                                 kv[:, t, 256 * c:256 * c + 256]).then_inc(stored, 16)
                    stores[0] += 1
            for c, o, s in ((0, k_prompt, k_sample), (1, v_prompt, v_sample)):
                sp.dma_start(o[0, 4 * P:LP].rearrange("t g d -> t (g d)"),
                             kv[0:LAST, 4, 256 * c:256 * c + 256]).then_inc(stored, 16)
                sp.dma_start(s.rearrange("b t g d -> (b t) (g d)"),
                             kv[LAST:ROWS[4], 4, 256 * c:256 * c + 256]).then_inc(stored, 16)
                stores[0] += 2
            kv_stores = stores[0]
            sp.wait_ge(ikiw_ready, 2)
            sp.dma_start(iw_dram[:, :], ikiw[LAST:ROWS[4], 4, IDIM:]).then_inc(iw_stored, 16)
            sp.wait_ge(iw_stored, 16)
            for h in range(IH):
                p0 = 64 * (h % 2) + DS * (h // 2)
                sp.dma_start(wcol[p0:p0 + DS, :], iw_dram[:, h:h + 1].rearrange("(b t) o -> t (b o)", t=DS),
                             allow_slow_non_contiguous=True).then_inc(wcol_here, 16)
            sp.wait_ge(ik_ready, TILES)
            for t in range(4):
                sp.dma_start(idx_k_prompt[0, t * P:(t + 1) * P, :], ik_norm[:, t, 0, :]).then_inc(idx_stored, 16)
            sp.dma_start(idx_k_prompt[0, 4 * P:LP, :], ik_norm[0:LAST, 4, 0, :]).then_inc(idx_stored, 16)
            sp.dma_start(idx_k_sample.rearrange("b t d -> (b t) d"), ik_norm[LAST:ROWS[4], 4, 0, :]
                         ).then_inc(idx_stored, 16)

            sp.wait_ge(pages_here, 16)

            def page(b, n):
                return sp.value_load(pages[0:1, b * PAGES + n:b * PAGES + n + 1], min_val=0,
                                     max_val=cache_k.shape[0] - 1)

            def load_idx(b):
                if b >= 2:
                    sp.wait_ge(idx_turned, b - 1)
                for n in range(PAGES):
                    v = page(b, n)
                    for c in range(2):
                        sp.dma_start(idx_page[:, b % 2, n, c, :],
                                     cache_idx_k[ds(v, 1), :, :].rearrange("a t d -> (a t) d")
                                     ).then_inc(idx_here[b % 2], 16)

            for b in range(DB):
                load_idx(b)
            load_tile(N_Q + 1, CUT["q"] + P, (N_Q + 1) % 2)
            sp.wait_ge(idx_out, 72)
            sp.dma_start(dist_c[:, :], consts2[:, 0:2 * LP]).then_inc(consts2_here, 16)
            sp.dma_start(rep_c[:, :], consts2[:, E_REP:E_END]).then_inc(consts2_here, 16)
            load_tiles(N_Q + 2, 6, CUT["q"] + 2 * P)
            load_tiles(N_GT, GT1, CUT["gt"])
            load_tile(N_ZA, CUT["za"], N_ZA % 2)
            load_tile(N_ZA + 1, CUT["za"] + P, (N_ZA + 1) % 2)

            sp.wait_ge(bias_ready, TILES)
            sp.wait_ge(last_pT_out, 1)

            def load_v(b):
                for n in range(PAGES):
                    v = page(b, n)
                    sp.dma_start(vpage[:, b % 4, n, :], cache_v[ds(v, 1)].rearrange("a t g d -> (a t) (g d)")
                                 ).then_inc(vpage_here, 16)

            def load_k(b):
                if b:
                    sp.wait_ge(kTs_out, b)
                for n in range(PAGES):
                    v = page(b, n)
                    sp.dma_start(kpage[:, n, :], cache_k[ds(v, 1)].rearrange("a t g d -> (a t) (g d)")
                                 ).then_inc(kpage_here, 16)

            for half in range(2):
                load_k(4 * half)
                if half:
                    sp.wait_ge(s_o_out, 1)
                for b in range(4 * half, 4 * half + 4):
                    load_v(b)
                if not half:
                    sp.wait_ge(last_o_out, 1)
                    sp.wait_ge(stored, 16 * kv_stores)
                    sp.dma_start(v_new[:, :, :], v_sample.rearrange("b t g d -> t b (g d)")).then_inc(v_new_here, 16)
                for b in range(4 * half + 1, 4 * half + 4):
                    load_k(b)

            load_tiles(N_ZA + 2, 6, CUT["za"] + 2 * P)
            sp.wait_ge(s_logits, DB)
            for c in range(2):
                sp.dma_start(state[0:4 * TAIL, c, :], state_conv[4 * c:4 * c + 4].rearrange("b t c -> (b t) c")
                             ).then_inc(state_here, 16)
            sp.dma_start(conv_sample[:, 0:TAIL - DS, :], state_conv[:, DS:TAIL, :]).then_inc(stored, 16)
            stores[0] += 1
            load_tiles(N_CU, 16, CUT["ga"], CUT["gb"])
            load_tile(N_ZC, CUT["zc"], N_ZC % 2)
            load_tile(N_ZC + 1, CUT["zc"] + P, (N_ZC + 1) % 2)
            load_tiles(N_ZC + 2, 6, CUT["zc"] + 2 * P)
            sp.wait_ge(tail_ready, 1)
            sp.dma_start(conv_prompt[0], u_tail[0:TAIL, :]).then_inc(tail_stored, 16)
            for b in range(DB):
                sp.dma_start(conv_sample[b, TAIL - DS:TAIL, :], u_tail[TAIL + DS * b:TAIL + DS * b + DS, :]
                             ).then_inc(tail_stored, 16)
            load_tiles(N_G2, N_BR - N_G2, CUT["gt"] + GT1 * P)

            def branch_pair(i):
                for b in range(2):
                    n = N_BR + 2 * i + b
                    buffer_free(n)
                    for c, w in ((0, w_att_out), (1, w_conv_out)):
                        sp.dma_start(raw[:, n % 2, c * DC:(c + 1) * DC].rearrange("p (k c) -> p k c", k=8),
                                     w[:, (2 * i + b) * P:(2 * i + b + 1) * P].rearrange("(k p) c -> p k c", p=P)
                                     ).then_inc(raw_here[n % 2], 16)

            branch_pair(0)
            for s in gate_stored:
                sp.wait_ge(s, 16 * 16)
            sp.wait_ge(xhi_ready, 4 * TILES + KC)
            sp.wait_ge(xlo_ready, 4 * TILES + KC)
            for i in range(8):
                if i:
                    branch_pair(i)
                for g, dst in ((0, gate0), (1, gate1)):
                    sp.dma_start(dst[:, 2 * i:2 * i + 2, :],
                                 gates[16 * g + 2 * i:16 * g + 2 * i + 2].rearrange("j p t -> p j t")
                                 ).then_inc(gate_here[i], 16)
            for r in range(2):
                load_rows(N_WO + r, w_o, 4 * r, 0)
            load_rows(N_WO + 2, w_o, 8, 0)
            sp.wait_ge(block_used, N_WO)
            sp.dma_start(y[0:META, 0, :], meta_tokens).then_inc(y_here, 16)
            sp.dma_start(y[META:P, 0, :], x_prompt[0, 0:P - META, :]).then_inc(y_here, 16)
            for t in range(1, 4):
                sp.dma_start(y[:, t, :], x_prompt[0, t * P - META:(t + 1) * P - META, :]).then_inc(y_here, 16)
            sp.dma_start(y[0:LAST, 4, :], x_prompt[0, SEQ - LAST:SEQ, :]).then_inc(y_here, 16)
            sp.dma_start(y[LAST:ROWS[4], 4, :], x_sample.rearrange("b t d -> (b t) d")).then_inc(y_here, 16)
            for v, dst in ((ln_post_g, post_g), (ln_post_b, post_b)):
                sp.dma_start(dst[:, :], v.rearrange("(o c) -> o c", o=1).broadcast_to([P, D])).then_inc(post_here, 16)
            for n in range(N_WO + 3, N_END):
                r = n - N_WO
                load_rows(n, w_o, 4 * (r % 4), 512 * (r // 4))
            for t in range(TILES):
                if t < 4:
                    sp.wait_ge(y_final, t + 1)
                else:
                    sp.wait_ge(y_final_last, 1)
                if t == 0:
                    sp.dma_start(y_prompt[0, 0:P - META, :], y[META:P, 0, :]).then_inc(stored, 16)
                elif t < 4:
                    sp.dma_start(y_prompt[0, t * P - META:(t + 1) * P - META, :], y[:, t, :]).then_inc(stored, 16)
                else:
                    sp.dma_start(y_prompt[0, SEQ - LAST:SEQ, :], y[0:LAST, 4, :]).then_inc(stored, 16)
                    sp.dma_start(y_sample.rearrange("b t d -> (b t) d"), y[LAST:ROWS[4], 4, :]).then_inc(stored, 16)
                    stores[0] += 1
                stores[0] += 1
            sp.wait_ge(tail_stored, 16 * (1 + DB))
            sp.wait_ge(idx_stored, 16 * 6)
            sp.wait_ge(stored, 16 * stores[0])

        @block.gpsimd
        def _(pool):
            steps = [0]

            def link(ins):
                steps[0] += 1
                ins.then_inc(pool_step, 1)
                pool.wait_ge(pool_step, steps[0])

            def split_lo(n, buf, width=KC * P):
                pool.wait_ge(hi_ready, n + 1)
                nc.gpsimd.tensor_tensor(wlo[:, buf, 0:width], raw[:, buf, 0:width],
                                        whi[:, buf, 0:width].bitcast(F32), ALU.subtract).then_inc(lo_ready, 1)

            for n in range(N_IK):
                split_lo(n, n % 2)
            split_lo(N_IK, 0, KC * 80)
            with pool.Fori(0, (N_ZA - N_IQ) // 2) as i:
                for b in range(2):
                    split_lo(N_IQ + b + i * 2, (N_IQ + b) % 2)
            split_lo(N_ZA, N_ZA % 2)
            for j in range(8):
                split_lo(N_ZA + j + 1, (N_ZA + j + 1) % 2)
                pool.wait_ge(tile_taken, N_ZA + j - C_OF + 3)
                s = j % 2
                link(nc.gpsimd.tensor_tensor(tmp_tanh[:, s, :], tmp_tanh[:, s, :], tmp_lin[:, s, :], ALU.mult))
                link(nc.gpsimd.tensor_tensor(tmp_tanh[:, s, :], tmp_tanh[:, s, :], tmp_lin[:, s, :], ALU.add))
                pool.wait_ge(s_o_taken, 2)
                nc.gpsimd.tensor_tensor(qT[:, j, :], qT[:, j, :], tmp_tanh[:, s, :], ALU.mult).then_inc(za_used, 1)
            with pool.Fori(0, (N_ZC - N_CU) // 2) as i:
                for b in range(2):
                    split_lo(N_CU + 1 + b + i * 2, (N_CU + 1 + b) % 2)
            for j in range(8):
                split_lo(N_ZC + j + 1, (N_ZC + j + 1) % 2)
                pool.wait_ge(tile_taken, N_ZC + j - C_OF + 3)
                s = j % 2
                link(nc.gpsimd.tensor_tensor(tmp_tanh[:, s, :], tmp_tanh[:, s, :], zc[:, j, :], ALU.mult))
                nc.gpsimd.tensor_tensor(zc[:, j, :], tmp_tanh[:, s, :], zc[:, j, :], ALU.add).then_inc(zc_done, 1)
            with pool.Fori(0, (N_BR - N_G2) // 2) as i:
                for b in range(2):
                    split_lo(N_G2 + 1 + b + i * 2, (N_G2 + 1 + b) % 2)
            for n in range(N_BR + 1, N_END):
                split_lo(n, n % 2)
            pool.wait_ge(post_here, 32)
            for t in range(4):
                pool.wait_ge(y_times_g, t + 1)
                nc.gpsimd.tensor_tensor(y[:, t, :], y[:, t, :], post_b[:, :], ALU.add).then_inc(y_final, 1)

        @block.scalar
        def _(act):
            def split_hi(n, buf, landed, width=KC * P, first=False):
                act.wait_ge(raw_here[buf], landed)
                if not first:
                    act.wait_ge(block_used, n - 1)
                nc.scalar.activation(whi[:, buf, 0:width], raw[:, buf, 0:width], ACT.Copy).then_inc(hi_ready, 1)

            def tile_ps(b):
                return ps[:, 2 * b:2 * b + 2, 0:HALF]

            def pairs(a):
                return a.rearrange("p (h t) -> p h t", h=2)

            def flat(a, j):
                return pairs(a[:, j, :]) if isinstance(j, int) else \
                    a[:, ds(j, 1), :].rearrange("p a (h t) -> p (a h) t", h=2)

            def each_pair(n0, count, take):
                with act.Fori(0, count // 2) as i:
                    for b in range(2):
                        n = n0 + b
                        split_hi(n + 1 + i * 2, (n + 1) % 2, LANDED[n + 1] + i * 16)
                        act.wait_ge(block_used, n + 1 + i * 2)
                        take(i, b)

            for g in range(4 * TILES):
                t, q = g // 4, g % 4
                act.wait_ge(xT_out, g + 1)
                nc.scalar.activation(xhi[:, 4 * q:4 * q + 4, t * P:t * P + ROWS[t]],
                                     ps[:, g % 8, :].rearrange("p (k t) -> p k t", k=4)[:, :, 0:ROWS[t]],
                                     ACT.Copy).then_inc(xhi_ready, 1)
                if g == 3:
                    split_hi(0, 0, LANDED[0], first=True)
                if g == 7:
                    split_hi(1, 1, LANDED[1], first=True)
            split_hi(2, 0, LANDED[2])
            split_hi(3, 1, LANDED[3])
            split_hi(4, 0, LANDED[4], KC * 80)
            for t in range(TILES):
                if t < 4:
                    act.wait_ge(kv_out, t + 1)
                else:
                    act.wait_ge(block_used, N_IK)
                nc.scalar.activation(kv[0:ROWS[t], t, :], ps[0:ROWS[t], t, :], ACT.Copy).then_inc(kv_ready, 1)
            act.wait_ge(kv_ready, TILES)
            act.sem_inc(tile_taken, 2)
            split_hi(5, 1, LANDED[5])
            act.wait_ge(block_used, N_IK + 1)
            nc.scalar.activation(ikiw[:, 0:4, :], ps[:, 5, 0:320].rearrange("p (t c) -> p t c", t=4), ACT.Copy
                                 ).then_inc(ikiw_ready, 1)
            nc.scalar.activation(ikiw[0:ROWS[4], 4, :], ps[0:ROWS[4], 5, 320:400], ACT.Copy).then_inc(ikiw_ready, 1)

            act.wait_ge(ik_var, 1)
            nc.scalar.activation(rs, mv.rearrange("p (t c) -> p t c", c=2)[:, :, 1], ACT.Sqrt).then_inc(ik_std, 1)

            def take_iq(i, b):
                nc.scalar.activation(flat(iqT, i * 2 + b), tile_ps(b), ACT.Copy).then_inc(tile_taken, 1)

            each_pair(N_IQ, 8, take_iq)
            act.wait_ge(turned, 1)
            nc.scalar.activation(kT[:, :, 0:512], ps[:, 4:6, :], ACT.Copy).then_inc(turned_taken, 1)
            act.wait_ge(turned, 2)
            nc.scalar.activation(kT[:, :, 512:TOK], ps[:, 6, 0:160].rearrange("p (g t) -> p g t", g=2), ACT.Copy
                                 ).then_inc(turned_taken, 1)
            act.wait_ge(turned, 3)
            nc.scalar.activation(ikT[:, 0:512], ps[:, 7, :], ACT.Copy).then_inc(turned_taken, 1)
            act.wait_ge(turned, 4)
            nc.scalar.activation(ikT[:, 512:TOK], ps[:, 2, 0:80], ACT.Copy).then_inc(turned_taken, 1)
            act.wait_ge(turned, 5)
            nc.scalar.activation(dwT[:, :, :], ps[:, 3, 0:8 * (CW + 3)].rearrange("p (j r) -> p j r", j=8), ACT.Copy
                                 ).then_inc(turned_taken, 1)

            scale = (IDIM ** -0.5) * (IH ** -0.5)
            for u in range(64):
                i, rows = 1 + u // IH, P if u < 48 else LAST
                n = min((i + 1) * P, LP)
                act.wait_ge(idx_out, u + 1)
                if u >= 2:
                    act.wait_ge(relu_used, u - 1)
                nc.scalar.activation(scores[0:rows, u % 2, 0:n],
                                     ps_t[0:rows, 2048 + 1024 * (u % 2):2048 + 1024 * (u % 2) + n],
                                     ACT.Relu, scale=scale).then_inc(relu_ready, 1)
            for b in range(DB):
                act.wait_ge(idx_turned, b + 1)
                nc.scalar.activation(idx_kT[:, b % 2, :], ps[:, 2 + b % 2, :], ACT.Copy).then_inc(idx_kT_ready, 1)
                act.wait_ge(idx_out, 65 + b)
                act.wait_ge(relu_used, 64 if b < 2 else 64 + b - 1)
                nc.scalar.activation(scores[:, b % 2, 0:LS], ps_t[:, 2048 + 1024 * (b % 2):2048 + 1024 * (b % 2) + LS],
                                     ACT.Relu, scale=scale).then_inc(relu_ready, 1)

            def take_q(i, b):
                nc.scalar.activation(flat(qT, i * 2 + b), tile_ps(b), ACT.Copy, scale=DH ** -0.5
                                     ).then_inc(tile_taken, 1)

            act.wait_ge(idx_stored, 16 * 6)
            each_pair(N_Q, 8, take_q)

            def take_gate(i, b):
                if not isinstance(i, int) or i:
                    act.wait_ge(gate_stored[b], i * 16)
                nc.scalar.activation(pairs(tmp_gate[:, b, :]), tile_ps(b), ACT.Tanh, scale=0.5).then_inc(tile_taken, 1)
                act.wait_ge(tile_taken, N_GT - C_OF + b + 3 + i * 2)
                dst = gates[i * 2 + b] if isinstance(i, int) else gates[ds(i * 2 + b, 1)].rearrange("a p t -> (a p) t")
                act.dma_start(dst, tmp_gate[:, b, :]).then_inc(gate_stored[b], 16)

            def burst(s):
                if 1 <= s <= GROUPS:
                    cols = (groups[s - 1][0] + 1) * P
                    if s >= 2:
                        act.wait_ge(o_out, s - 1)
                    for r in range(GROUP):
                        act.wait_ge(pT_out, GROUP * (s - 1) + r + 1)
                        nc.scalar.activation(pT[:, r, 0:cols], ps[:, 4 + r, 0:cols], ACT.Copy).then_inc(pT_ready, 1)
                if s == GROUPS + 1:
                    act.wait_ge(last_pT_out, 1)
                    nc.scalar.activation(pT[:, 0, :], ps[:, 5, :], ACT.Copy)
                    nc.scalar.activation(pT[0:LAST, 1, 0:P], ps[0:LAST, 6, 0:P], ACT.Copy).then_inc(last_pT_ready, 1)

            def exps(s):
                if s < GROUPS:
                    n = (groups[s][0] + 1) * P
                    for r in range(GROUP):
                        act.wait_ge(max_ready, GROUP * s + r + 1)
                        nc.scalar.activation(probs[:, r, 0:n], probs[:, r, 0:n], ACT.Exp, bias=neg_max[:, r:r + 1],
                                             accum_out=exp_sum[:, r:r + 1]).then_inc(exp_ready, 1)
                if s == GROUPS:
                    act.wait_ge(last_max, 1)
                    nc.scalar.activation(probs_last[:, :], probs_last[:, :], ACT.Exp, bias=neg_max[:, 0:1],
                                         accum_out=exp_sum[:, 0:1]).then_inc(last_exp, 1)

            for s in range(BURSTS):
                burst(s)
                for b in range(2):
                    n = N_GT + 2 * s + b
                    split_hi(n + 1, (n + 1) % 2, LANDED[n + 1])
                    if b == 0:
                        exps(s)
                    act.wait_ge(block_used, n + 1)
                    take_gate(s, b)
            with act.Fori(BURSTS, GT1 // 2) as i:
                for b in range(2):
                    n = N_GT + b
                    split_hi(n + 1 + i * 2, (n + 1) % 2, LANDED[n + 1] + i * 16)
                    act.wait_ge(block_used, n + 1 + i * 2)
                    take_gate(i, b)
            split_hi(N_ZA + 1, (N_ZA + 1) % 2, LANDED[N_ZA + 1])

            for half in range(2):
                for b4 in range(4):
                    b = 4 * half + b4
                    act.wait_ge(kTs_out, b + 1)
                    if b:
                        act.wait_ge(s_logits, b)
                    nc.scalar.activation(kTs[:, :, :], ps[:, 0:2, :], ACT.Copy).then_inc(kTs_ready, 1)
                for g in range(2):
                    act.wait_ge(s_max, 2 * half + g + 1)
                    nc.scalar.activation(scores[:, g, 0:LS], scores[:, g, 0:LS], ACT.Exp,
                                         bias=neg_max[:, g:g + 1], accum_out=exp_sum[:, g:g + 1]).then_inc(s_exp, 1)
                for g in range(2):
                    act.wait_ge(s_pT_out, 2 * half + g + 1)
                    if half:
                        act.wait_ge(s_o_out, half)
                    nc.scalar.activation(pT[:, g, :], ps[:, g, :], ACT.Copy)
                    nc.scalar.activation(pT_new[:, g, :], ps[0:DS, 2 + g, 0:P], ACT.Copy).then_inc(s_pT_ready, 1)

            for j in range(8):
                n = N_ZA + j
                if j:
                    split_hi(n + 1, (n + 1) % 2, LANDED[n + 1])
                act.wait_ge(block_used, n + 1)
                if j >= 2:
                    act.wait_ge(za_used, j - 1)
                b = j % 2
                nc.scalar.activation(pairs(tmp_lin[:, b, :]), tile_ps(b), ACT.Copy, scale=0.5)
                nc.scalar.activation(pairs(tmp_tanh[:, b, :]), tile_ps(b), ACT.Tanh, scale=0.5).then_inc(tile_taken, 1)

            act.wait_ge(state_taken, 16)
            with act.Fori(0, 8) as i:
                for b in range(2):
                    n = N_CU + b
                    split_hi(n + 1 + i * 2, (n + 1) % 2, LANDED[n + 1] + i * 16)
                    act.wait_ge(block_used, n + 1 + i * 2)
                    if b == 0:
                        row = U[:, ds(i, 1), :].rearrange("p a w -> p (a w)")
                        nc.scalar.activation(row[:, TAIL:TAIL + HALF], ps[:, 0, 0:HALF], ACT.Copy, scale=0.5)
                        nc.scalar.activation(row[:, TAIL + HALF:EXT], ps[:, 1, 0:LP - HALF], ACT.Copy, scale=0.5)
                        nc.scalar.activation(sample_cols(U, i)[:, :, TAIL:],
                                             ps[:, 1, LP - HALF:HALF].rearrange("p (b t) -> p b t", b=DB),
                                             ACT.Copy, scale=0.5).then_inc(tile_taken, 1)
                    else:
                        nc.scalar.activation(flat(zc, i), tile_ps(1), ACT.Tanh, scale=0.5).then_inc(tile_taken, 1)

            def normed(j):
                act.wait_ge(n_ready, j + 1)
                if j >= 2:
                    act.wait_ge(c_ready, j - 1)
                b = j % 2
                nc.scalar.activation(tmp_lin[:, b, 0:LP], U[:, j, TAIL:EXT], ACT.Identity,
                                     scale=half_g[:, j:j + 1], bias=half_b[:, j:j + 1])
                nc.scalar.activation(tmp_lin[:, b, LP:TOK].rearrange("p (b t) -> p b t", b=DB),
                                     sample_cols(U, j)[:, :, TAIL:], ACT.Identity,
                                     scale=half_g[:, j:j + 1], bias=half_b[:, j:j + 1]).then_inc(lin_ready, 1)
                act.wait_ge(lin_ready, j + 1)
                nc.scalar.activation(U[:, j, 0:TOK], tmp_lin[:, b, :], ACT.Tanh).then_inc(tanh_ready, 1)

            for j in range(8):
                n = N_ZC + j
                split_hi(n + 1, (n + 1) % 2, LANDED[n + 1])
                act.wait_ge(block_used, n + 1)
                act.wait_ge(tailT_ready, j + 1)
                if j >= 2:
                    act.wait_ge(zc_done, j - 1)
                b = j % 2
                nc.scalar.activation(flat(zc, j), tile_ps(b), ACT.Copy, scale=0.5)
                nc.scalar.activation(pairs(tmp_tanh[:, b, :]), tile_ps(b), ACT.Tanh, scale=0.5).then_inc(tile_taken, 1)
                if j == 5:
                    act.wait_ge(tail_out, 1)
                    nc.scalar.activation(u_tail[0:TAIL + DB * DS, :].rearrange("p (h c) -> p h c", h=2),
                                         ps[0:TAIL + DB * DS, 4:6, :], ACT.Copy).then_inc(tail_ready, 1)
            act.wait_ge(zc_done, 8)
            for j in range(N_BR - N_G2):
                n = N_G2 + j
                split_hi(n + 1, (n + 1) % 2, LANDED[n + 1])
                act.wait_ge(block_used, n + 1)
                b = j % 2
                if j >= 2:
                    act.wait_ge(gate_stored[b], (GT1 + j) // 2 * 16)
                nc.scalar.activation(pairs(tmp_tanh[:, b, :]), tile_ps(b), ACT.Tanh, scale=0.5).then_inc(tile_taken, 1)
                act.wait_ge(tile_taken, n - C_OF + 3)
                act.dma_start(gates[GT1 + j], tmp_tanh[:, b, :]).then_inc(gate_stored[b], 16)
                if j == 3:
                    act.wait_ge(std_in, 1)
                    nc.scalar.activation(c_rstd[:, :], c_sum[:, :], ACT.Sqrt).then_inc(std_ready, 1)
                    act.wait_ge(tail_stored, 16 * (1 + DB))
                if j >= 4:
                    for k in range(2 * (j - 4), 2 * (j - 4) + 2):
                        normed(k)
            act.wait_ge(block_used, N_BR)
            for k in range(KC):
                if k >= 8:
                    act.wait_ge(c_ready, k - 7)
                nc.scalar.activation(xhi[:, k, :], qT[:, k, :] if k < 8 else zc[:, k - 8, :], ACT.Copy
                                     ).then_inc(xhi_ready, 1)

            for j in range(KC):
                n = N_BR + j
                split_hi(n + 1, (n + 1) % 2, LANDED[n + 1])
                act.wait_ge(m_ready, j + 1)
                nc.scalar.activation(mhi[:, j, :], m_tmp[:, j % 2, :], ACT.Copy).then_inc(mhi_ready, 1)
            for r in range(16):
                n = N_WO + r
                if n + 1 < N_END:
                    split_hi(n + 1, (n + 1) % 2, LANDED[n + 1])
                if r == 1:
                    act.wait_ge(y_here, 16 * 7)
                for t in {1: (0, 1), 2: (2, 3), 3: (4,)}.get(r, ()):
                    rows = ROWS[t]
                    nc.scalar.mul(y[0:rows, t, :], y[0:rows, t, :], ALPHA).then_inc(y_scaled, 1)
            for t in range(TILES):
                rows = ROWS[t]
                act.wait_ge(y_var, t + 1)
                nc.scalar.activation(y_rstd[0:rows, t:t + 1], ymv[0:rows, 1:2], ACT.Sqrt).then_inc(y_std, 1)
                act.wait_ge(y_norm_in, t + 1)
                nc.scalar.activation(y[0:rows, t, :], y[0:rows, t, :], ACT.Identity,
                                     scale=y_rstd[0:rows, t:t + 1], bias=y_shift[0:rows, t:t + 1]).then_inc(y_norm, 1)

        @block.vector
        def _(dve):
            steps = [0]

            def link(ins):
                steps[0] += 1
                ins.then_inc(dve_step, 1)
                dve.wait_ge(dve_step, steps[0])

            link(nc.vector.memset(ones[:, :], 1.0 / DC))
            link(nc.vector.memset(mv, 1.0))
            for g in range(4 * TILES):
                t, q = g // 4, g % 4
                dve.wait_ge(xhi_ready, g + 1)
                cols = slice(t * P, t * P + ROWS[t])
                nc.vector.tensor_tensor(xlo[:, 4 * q:4 * q + 4, cols],
                                        ps[:, g % 8, :].rearrange("p (k t) -> p k t", k=4)[:, :, 0:ROWS[t]],
                                        xhi[:, 4 * q:4 * q + 4, cols].bitcast(F32), ALU.subtract
                                        ).then_inc(xlo_ready, 1)

            dve.wait_ge(ikiw_ready, 2)
            dve.wait_ge(dw_here, 16 * 6)
            for t in range(TILES):
                r = ROWS[t]
                link(nc.vector.bn_stats(st[0:r, 6 * t:6 * t + 6], ikiw[0:r, t, 0:IDIM]))
                link(nc.vector.bn_aggr(mv[0:r, 2 * t:2 * t + 2], st[0:r, 6 * t:6 * t + 6]))
            var = mv.rearrange("p (t c) -> p t c", c=2)[:, :, 1]
            nc.vector.tensor_scalar(var, var, EPS, None, ALU.add).then_inc(ik_var, 1)
            dve.wait_ge(ik_std, 1)
            link(nc.vector.reciprocal(rs, rs))
            for t in range(TILES):
                r = ROWS[t]
                a = ik_norm[0:r, t, 0, :]
                link(nc.vector.tensor_scalar(a, ikiw[0:r, t, 0:IDIM], mv[0:r, 2 * t:2 * t + 1], rs[0:r, t:t + 1],
                                             ALU.subtract, ALU.mult))
                link(nc.vector.tensor_tensor(a, a, idx_gb[0:r, 0, :], ALU.mult))
                link(nc.vector.tensor_tensor(a, a, idx_gb[0:r, 1, :], ALU.add))
                nc.vector.tensor_copy(ik_norm[0:r, t, 1, :], a).then_inc(ik_ready, 1)

            dve.wait_ge(tile_taken, 8 + 2)
            for j in range(IH // 2):
                nc.vector.tensor_copy(iq_new[:, :, DS * j:DS * j + DS],
                                      iqT[:, j, LP:TOK].rearrange("p (b t) -> p b t", b=DB)).then_inc(iq_new_ready, 1)

            link(nc.vector.memset(w_sel[:, :, :], 0.0))
            dve.wait_ge(wcol_here, 16 * IH)
            for b in range(DB):
                nc.vector.tensor_scalar(w_sel[:, b, LAST + DS * b:LAST + DS * b + DS], cst[:, C_DIV:C_DIV + DS],
                                        wcol[:, b:b + 1], None, ALU.mult).then_inc(wsel_ready, 1)

            def sc(i):
                rows = P if i < 4 else ROWS[4]
                return bias[0:rows, bias_at[i]:bias_at[i] + bias_w[i]]

            link(nc.vector.memset(sc(4), 0.0))
            for u in range(64):
                i, h = 1 + u // IH, u % IH
                rows, n = (P if i < 4 else LAST), min((i + 1) * P, LP)
                dst = sc(i)[0:rows, (PAD if i == 4 else 0):][:, 0:n]
                w = ikiw[0:rows, i, IDIM + h:IDIM + h + 1]
                dve.wait_ge(relu_ready, u + 1)
                if h == 0:
                    nc.vector.tensor_scalar(dst, scores[0:rows, u % 2, 0:n], w, None, ALU.mult).then_inc(relu_used, 1)
                else:
                    dve.wait_ge(relu_used, u)
                    nc.vector.scalar_tensor_tensor(dst, scores[0:rows, u % 2, 0:n], w, dst, ALU.mult, ALU.add
                                                   ).then_inc(relu_used, 1)
            dve.wait_ge(relu_used, 64)
            for i in range(1, 4):
                link(nc.vector.tensor_tensor(sc(i)[:, i * P:(i + 1) * P], sc(i)[:, i * P:(i + 1) * P],
                                             cst[:, C_TRI:C_TRI + P], ALU.add))
            last = sc(4)
            dve.wait_ge(sample_scored, 1)
            link(nc.vector.tensor_tensor(last[:, PAD:PAD + LS], last[:, PAD:PAD + LS], ps_t[0:ROWS[4], 0:LS], ALU.add))
            nc.vector.tensor_copy(last[:, 0:PAD], cst[0:ROWS[4], C_PAD:C_PAD + PAD]).then_inc(scores_done, 1)
            dve.wait_ge(scores_done, 1)
            link(nc.vector.tensor_tensor(last[:, PAD + 4 * P:], last[:, PAD + 4 * P:],
                                         cst[0:ROWS[4], C_NEW:C_NEW + META], ALU.add))

            done = 0
            for i, rounds in ((1, TOP_P // 8), (2, TOP_P // 8), (3, TOP_P // 8), (4, (TOP_S + 6) // 8)):
                rows = P if i < 4 else ROWS[4]
                with dve.Fori(0, rounds) as r:
                    nc.vector.max(top8[0:rows, :], sc(i)).then_inc(topk_step, 1)
                    dve.wait_ge(topk_step, done + 1 + r * 2)
                    nc.vector.memset(wait_carrier, 0.0)
                    nc.vector.match_replace(sc(i), top8[0:rows, :], sc(i), TAKEN).then_inc(topk_step, 1)
                    dve.wait_ge(topk_step, done + 2 + r * 2)
                done += 2 * rounds

            dve.wait_ge(consts2_here, 32)
            for i in range(1, 5):
                rows = P if i < 4 else ROWS[4]
                s = sc(i) if i < 4 else sc(4)[:, PAD:]
                n = bias_w[i] if i < 4 else LP
                link(nc.vector.tensor_scalar(s, s, BETWEEN, FAR, ALU.is_ge, ALU.mult))
                dist = dist_c[0:rows, 0:n] if i < 4 else dist_c[0:rows, LP:LP + n]
                nc.vector.scalar_tensor_tensor(s, dist, float(-i * P) if i < 4 else 0.0, s, ALU.add, ALU.add
                                               ).then_inc(bias_ready, 1)
            link(nc.vector.tensor_scalar(sc(0), cst[:, C_TRI:C_TRI + P], 1e-6, None, ALU.mult))
            nc.vector.tensor_tensor(sc(0), sc(0), dist_c[:, 0:P], ALU.add).then_inc(bias_ready, 1)
            dve.wait_ge(bias_ready, TILES)
            dve.wait_ge(tile_taken, N_GT - C_OF + 2)
            nc.vector.tensor_copy(q_last[:, :].rearrange("p (h t) -> p h t", h=HEADS), qT[:, :, 4 * P:LP]
                                  ).then_inc(q_last_ready, 1)
            for s in range(GROUPS + 1):
                if s >= 1:
                    i, g = groups[s - 1]
                    dve.wait_ge(o_out, s)
                    nc.vector.tensor_copy(qT[:, GROUP * g:GROUP * (g + 1), i * P:(i + 1) * P],
                                          ps[:, 4, :].rearrange("p (r t) -> p r t", r=GROUP)).then_inc(o_taken, 1)
                if s == GROUPS:
                    break
                i, g = groups[s]
                n = (i + 1) * P
                for r in range(GROUP):
                    dve.wait_ge(logits_out, GROUP * s + r + 1)
                    link(nc.vector.scalar_tensor_tensor(probs[:, r, 0:n], sc(i)[:, 0:n], 2.0 ** -(GROUP * g + r + 1.0),
                                                        ps[:, 4 + (r + 1) % 4, 0:n], ALU.mult, ALU.add))
                    nc.vector.tensor_reduce(neg_max[:, r:r + 1], probs[:, r, 0:n], AX_X, ALU.max, negate=True
                                            ).then_inc(max_ready, 1)
                for r in range(GROUP):
                    dve.wait_ge(exp_ready, GROUP * s + r + 1)
                    link(nc.vector.reciprocal(inv_sum[:, r:r + 1], exp_sum[:, r:r + 1]))
                    nc.vector.tensor_scalar(probs[:, r, 0:n], probs[:, r, 0:n], inv_sum[:, r:r + 1], None, ALU.mult
                                            ).then_inc(probs_ready, 1)
            dve.wait_ge(last_logits, 1)
            nc.vector.tensor_copy(bias_s[:, 0:512], ps[:, 7, :])
            link(nc.vector.tensor_copy(bias_s[:, 512:LP], ps[:, 6, 64:64 + LAST]))
            link(nc.vector.scalar_tensor_tensor(probs_last[:, :], bias_s[:, :],
                                                cst[:, C_SLOPE + KVH:C_SLOPE + KVH + 1],
                                                ps_t[:, 5 * 512:5 * 512 + LP], ALU.mult, ALU.add))
            nc.vector.tensor_reduce(neg_max[:, 0:1], probs_last[:, :], AX_X, ALU.max, negate=True
                                    ).then_inc(last_max, 1)
            dve.wait_ge(last_exp, 1)
            link(nc.vector.reciprocal(inv_sum[:, 0:1], exp_sum[:, 0:1]))
            nc.vector.tensor_scalar(probs_last[:, :], probs_last[:, :], inv_sum[:, 0:1], None, ALU.mult
                                    ).then_inc(last_probs, 1)
            dve.wait_ge(last_o_out, 1)
            nc.vector.tensor_copy(qT[:, :, 4 * P:LP], ps[:, 7, 0:P].rearrange("p (h t) -> p h t", h=HEADS)
                                  ).then_inc(last_o_taken, 1)

            for s in gate_stored:
                dve.wait_ge(s, 16 * (GT1 // 2))
            for h in range(HEADS):
                r = h % GROUP
                nc.vector.tensor_copy(q_new[:, h // GROUP, :, DS * r:DS * r + DS],
                                      qT[:, h, LP:TOK].rearrange("p (b t) -> p b t", b=DB)).then_inc(q_new_ready, 1)
            for half in range(2):
                dve.wait_ge(rep_out, half + 1)
                nc.vector.tensor_copy(bias_s[:, 0:LS], ps_t[:, 2048:2048 + LS]).then_inc(rep_taken, 1)
                dve.wait_ge(rep_taken, half + 1)
                for g in range(2):
                    dve.wait_ge(s_logits, 4 * half + 4)
                    t = scores[:, g, 0:LS]
                    link(nc.vector.scalar_tensor_tensor(t, bias_s[:, 0:LS], cst[:, C_SLOPE + g:C_SLOPE + g + 1],
                                                        ps_t[:, 2048 + 1024 * g:2048 + 1024 * g + LS],
                                                        ALU.mult, ALU.add))
                    nc.vector.tensor_reduce(neg_max[:, g:g + 1], t, AX_X, ALU.max, negate=True).then_inc(s_max, 1)
                for g in range(2):
                    t = scores[:, g, 0:LS]
                    dve.wait_ge(s_exp, 2 * half + g + 1)
                    link(nc.vector.reciprocal(inv_sum[:, g:g + 1], exp_sum[:, g:g + 1]))
                    nc.vector.tensor_scalar(t, t, inv_sum[:, g:g + 1], None, ALU.mult).then_inc(s_probs, 1)
                dve.wait_ge(s_o_out, half + 1)
                for g in range(2):
                    at0 = LP + 32 * half
                    ins = nc.vector.tensor_copy(
                        qT[:, 4 * g:4 * g + 4, at0:at0 + 32].rearrange("p r (b t) -> p r b t", b=4),
                        ps[:, 4 + 2 * g, 0:P].rearrange("p (b r t) -> p r b t", b=4, r=4))
                    link(ins)
                dve.sem_inc(s_o_taken, 1)

            for c in range(16):
                j, part = c // 2, c % 2
                dve.wait_ge(state_out, c + 1)
                if c == 0:
                    link(nc.vector.memset(U[:, :, 0:TAIL], 0.0))
                nc.vector.tensor_copy(sample_cols(U, j)[:, 4 * part:4 * part + 4, 0:TAIL],
                                      ps[:, 4 + c % 4, 0:4 * TAIL].rearrange("p (b t) -> p b t", b=4)
                                      ).then_inc(state_taken, 1)
            link(nc.vector.tensor_scalar(half_g, dwT[:, :, CW + 1], 0.5, None, ALU.mult))
            link(nc.vector.tensor_scalar(half_b, dwT[:, :, CW + 2], 0.5, None, ALU.mult))

            link(nc.vector.memset(c_sum[:, :], 0.0))
            TAPS = 4
            ENDS = TAPS + 2 * CW
            PER = ENDS + 2
            with dve.Fori(0, 8) as j:
                row = U[:, ds(j, 1), :].rearrange("p a w -> p (a w)")
                new = sample_cols(U, j)
                t = zc[:, ds(j, 1), :].rearrange("p a w -> p (a w)")
                accs = c_acc[:, LP:TOK].rearrange("p (b t) -> p b t", b=DB)
                tail = tailT[:, ds(j, 1), :].rearrange("p a w -> p (a w)")
                dve.wait_ge(tile_taken, N_CU + 2 - C_OF + 2 + j * 2)
                nc.vector.scalar_tensor_tensor(row[:, TAIL:EXT], t[:, 0:LP], 1.0, row[:, TAIL:EXT], ALU.add, ALU.mult
                                               ).then_inc(conv_step, 1)
                nc.vector.scalar_tensor_tensor(new[:, :, TAIL:], t[:, LP:TOK].rearrange("p (b t) -> p b t", b=DB),
                                               1.0, new[:, :, TAIL:], ALU.add, ALU.mult).then_inc(conv_step, 1)
                dve.wait_ge(conv_step, 2 + j * PER)
                nc.vector.tensor_copy(tail[:, 0:TAIL], row[:, EXT - TAIL:EXT]).then_inc(conv_step, 1)
                nc.vector.tensor_copy(tail[:, TAIL:].rearrange("p (b t) -> p b t", b=DB), new[:, :, TAIL:]
                                      ).then_inc(conv_step, 1)
                dve.wait_ge(conv_step, TAPS + j * PER)
                dve.sem_inc(tailT_ready, 1)
                for k in range(CW):
                    w = dwT[:, ds(j, 1), k:k + 1].rearrange("p a k -> p (a k)")
                    out_p = c_acc[:, 0:LP] if k < CW - 1 else row[:, TAIL:EXT]
                    out_s = accs if k < CW - 1 else new[:, :, TAIL:]
                    if k == 0:
                        bd = dwT[:, ds(j, 1), CW:CW + 1].rearrange("p a k -> p (a k)")
                        nc.vector.tensor_scalar(out_p, row[:, 0:LP], w, bd, ALU.mult, ALU.add).then_inc(conv_step, 1)
                        nc.vector.tensor_scalar(out_s, new[:, :, 0:DS], w, bd, ALU.mult, ALU.add
                                                ).then_inc(conv_step, 1)
                    else:
                        dve.wait_ge(conv_step, TAPS + 2 * k - 1 + j * PER)
                        nc.vector.scalar_tensor_tensor(out_p, row[:, k:k + LP], w, c_acc[:, 0:LP], ALU.mult, ALU.add
                                                       ).then_inc(conv_step, 1)
                        dve.wait_ge(conv_step, TAPS + 2 * k + j * PER)
                        nc.vector.scalar_tensor_tensor(out_s, new[:, :, k:k + DS], w, accs, ALU.mult, ALU.add
                                                       ).then_inc(conv_step, 1)
                dve.wait_ge(conv_step, ENDS + j * PER)
                sums = c_sum[:, LP:TOK].rearrange("p (b t) -> p b t", b=DB)
                nc.vector.tensor_tensor(c_sum[:, 0:LP], c_sum[:, 0:LP], row[:, TAIL:EXT], ALU.add
                                        ).then_inc(conv_step, 1)
                nc.vector.tensor_tensor(sums, sums, new[:, :, TAIL:], ALU.add).then_inc(conv_step, 1)
                dve.wait_ge(conv_step, PER + j * PER)
            dve.sem_inc(conv_done, 1)

            def dev(j):
                row = U[:, j, :]
                link(nc.vector.tensor_tensor(row[:, TAIL:TAIL + HALF], row[:, TAIL:TAIL + HALF], ps[:, 6, 0:HALF],
                                             ALU.subtract))
                link(nc.vector.tensor_tensor(row[:, TAIL + HALF:EXT], row[:, TAIL + HALF:EXT],
                                             ps[:, 7, 0:LP - HALF], ALU.subtract))
                link(nc.vector.tensor_tensor(sample_cols(U, j)[:, :, TAIL:], sample_cols(U, j)[:, :, TAIL:],
                                             ps[:, 7, LP - HALF:HALF].rearrange("p (b t) -> p b t", b=DB),
                                             ALU.subtract))

            def branch_input(j):
                dve.wait_ge(tanh_ready, j + 1)
                link(nc.vector.scalar_tensor_tensor(U[:, j, 0:TOK], U[:, j, 0:TOK], 1.0, tmp_lin[:, j % 2, :],
                                                    ALU.add, ALU.mult))
                dve.wait_ge(zc_done, j + 1)
                nc.vector.tensor_tensor(zc[:, j, :], zc[:, j, :], U[:, j, 0:TOK], ALU.mult).then_inc(c_ready, 1)

            dve.wait_ge(mean_out, 1)
            for j in range(8):
                row, new = U[:, j, :], sample_cols(U, j)[:, :, TAIL:]
                dev(j)
                accs = c_acc[:, LP:TOK].rearrange("p (b t) -> p b t", b=DB)
                dst, dsts = (c_sum, c_sum[:, LP:TOK].rearrange("p (b t) -> p b t", b=DB)) if j == 0 else (c_acc, accs)
                link(nc.vector.tensor_tensor(dst[:, 0:LP], row[:, TAIL:EXT], row[:, TAIL:EXT], ALU.mult))
                link(nc.vector.tensor_tensor(dsts, new, new, ALU.mult))
                if j:
                    link(nc.vector.tensor_tensor(c_sum[:, :], c_sum[:, :], c_acc[:, :], ALU.add))
            dve.sem_inc(sq_ready, 1)
            dve.wait_ge(var_out, 1)
            nc.vector.tensor_scalar(c_sum[:, :].rearrange("p (h t) -> p h t", h=2), ps[:, 4:6, 0:HALF], EPS, None,
                                    ALU.add).then_inc(std_in, 1)
            dve.wait_ge(std_ready, 1)
            link(nc.vector.reciprocal(c_rstd[:, :], c_rstd[:, :]))
            for j in range(8):
                row, new = U[:, j, :], sample_cols(U, j)[:, :, TAIL:]
                link(nc.vector.tensor_tensor(row[:, TAIL:EXT], row[:, TAIL:EXT], c_rstd[:, 0:LP], ALU.mult))
                nc.vector.tensor_tensor(new, new, c_rstd[:, LP:TOK].rearrange("p (b t) -> p b t", b=DB), ALU.mult
                                        ).then_inc(n_ready, 1)
                if j >= 1:
                    branch_input(j - 1)
            branch_input(7)
            for k in range(KC):
                dve.wait_ge(xhi_ready, 4 * TILES + k + 1)
                src = qT[:, k, :] if k < 8 else zc[:, k - 8, :]
                nc.vector.tensor_tensor(xlo[:, k, :], src, xhi[:, k, :].bitcast(F32), ALU.subtract
                                        ).then_inc(xlo_ready, 1)

            def low_mixed(j):
                dve.wait_ge(mhi_ready, j + 1)
                nc.vector.tensor_tensor(mlo[:, j, :], m_tmp[:, j % 2, :], mhi[:, j, :].bitcast(F32), ALU.subtract
                                        ).then_inc(mlo_ready, 1)

            for j in range(KC):
                o = 4 * (j % 2)
                dve.wait_ge(gate_here[j // 2], 32)
                dve.wait_ge(block_used, N_BR + j + 1)
                for c, g in ((0, gate0), (1, gate1)):
                    gv = g[:, j, :].rearrange("p (h t) -> p h t", h=2)
                    ins = nc.vector.scalar_tensor_tensor(gv, gv, 1.0, ps[:, o + 2 * c:o + 2 * c + 2, 0:HALF],
                                                         ALU.add, ALU.mult)
                    link(ins)
                dve.sem_inc(br_taken, 1)
                nc.vector.tensor_tensor(m_tmp[:, j % 2, :], gate0[:, j, :], gate1[:, j, :], ALU.add
                                        ).then_inc(m_ready, 1)
                low_mixed(j)
                if j == KC - 2:
                    dve.sem_inc(y_taken, 4)
            dve.sem_inc(y_taken, 1)

            def scaled(t):
                r = ROWS[t]
                dve.wait_ge(y_norm, t + 1)
                dve.wait_ge(post_here, 32)
                nc.vector.tensor_tensor(y[0:r, t, :], y[0:r, t, :], post_g[0:r, :], ALU.mult).then_inc(y_times_g, 1)

            for n in range(4):
                for t in range(TILES):
                    r = ROWS[t]
                    if n == 0:
                        dve.wait_ge(y_scaled, t + 1)
                    if t < 4:
                        dve.wait_ge(y_out, 4 * n + t + 1)
                    else:
                        dve.wait_ge(block_used, N_WO + 4 * n + 4)
                    dst = y[0:r, t, 512 * n:512 * n + 512]
                    nc.vector.scalar_tensor_tensor(dst, ps[0:r, t, :], 0.5, dst, ALU.mult, ALU.add
                                                   ).then_inc(y_taken, 1)
                    dve.wait_ge(y_taken, TILES * (n + 1) + t + 1)
                    link(nc.vector.bn_stats(yst[0:r, t, 6 * n:6 * n + 6], dst))
                    if n == 3:
                        if t:
                            dve.wait_ge(y_norm, t)
                        link(nc.vector.bn_aggr(ymv[0:r, :], yst[0:r, t, :]))
                        nc.vector.tensor_scalar(ymv[0:r, 1:2], ymv[0:r, 1:2], EPS, None, ALU.add).then_inc(y_var, 1)
                        dve.wait_ge(y_std, t + 1)
                        link(nc.vector.reciprocal(y_rstd[0:r, t:t + 1], y_rstd[0:r, t:t + 1]))
                        nc.vector.scalar_tensor_tensor(y_shift[0:r, t:t + 1], ymv[0:r, 0:1], -1.0,
                                                       y_rstd[0:r, t:t + 1], ALU.mult, ALU.mult
                                                       ).then_inc(y_norm_in, 1)
                        if t >= 1:
                            scaled(t - 1)
            scaled(TILES - 1)
            r = ROWS[4]
            dve.wait_ge(y_times_g, TILES)
            nc.vector.tensor_tensor(y[0:r, 4, :], y[0:r, 4, :], post_b[0:r, :], ALU.add).then_inc(y_final_last, 1)

        @block.tensor
        def _(pe):
            mm = nc.tensor.matmul

            def block_ready(n):
                pe.wait_ge(lo_ready, n + 1)

            def rows_block(n, buf, act_hi, act_lo, k0, first, last, out_sem, empty=None):
                block_ready(n)
                w = [t[:, buf, :].rearrange("p (k c) -> p k c", k=4) for t in (whi, wlo)]
                for t in range(TILES):
                    r = ROWS[t]
                    cols = slice(t * P, t * P + r)
                    if empty is not None:
                        pe.wait_ge(y_taken, empty + t + 1)
                    for k in range(4):
                        for m, (a, b) in enumerate(((act_hi, 0), (act_lo, 0), (act_hi, 1))):
                            ins = mm(ps[0:r, t, :], a[:, k0 + k, cols], w[b][:, k, :],
                                     start=(first and k == 0 and m == 0), stop=(last and k == 3 and m == 2))
                    if t == TILES - 1:
                        ins.then_inc(block_used, 1)
                    elif last:
                        ins.then_inc(out_sem, 1)

            def tile_block(buf, bank, k0=0, kn=KC):
                w = [t[:, buf, :].rearrange("p (k c) -> p k c", k=KC) for t in (whi, wlo)]
                for k in range(k0, k0 + kn):
                    for m, (b, x) in enumerate(((0, xhi), (0, xlo), (1, xhi))):
                        for half in range(2):
                            ins = mm(ps[:, bank + half, 0:HALF], w[b][:, k, :],
                                     x[:, k, half * HALF:(half + 1) * HALF],
                                     start=(k == k0 and m == 0), stop=(k == k0 + kn - 1 and m == 2))
                return ins

            def tile_pair(n0, i):
                for b in range(2):
                    n = n0 + b
                    block_ready(n + i * 2)
                    pe.wait_ge(tile_taken, n - C_OF + 1 + i * 2)
                    tile_block(n % 2, 2 * b).then_inc(block_used, 1)

            def tiles(n0, count):
                with pe.Fori(0, count // 2) as i:
                    tile_pair(n0, i)

            pe.wait_ge(consts_here, 16)
            for g in range(4 * TILES):
                t, q = g // 4, g % 4
                if q == 0:
                    pe.wait_ge(x_here[t], 32 if t in (0, 4) else 16)
                if g >= 8:
                    pe.wait_ge(xlo_ready, g - 7)
                r = ROWS[t]
                for k in range(4):
                    ins = nc.tensor.transpose(ps[:, g % 8, k * P:k * P + r],
                                              xn[0:r, t, (4 * q + k) * P:(4 * q + k + 1) * P], cst[0:r, C_ID:C_ID + r])
                ins.then_inc(xT_out, 1)
            pe.wait_ge(xlo_ready, 4 * TILES)
            for n in range(4):
                rows_block(n, n % 2, xhi, xlo, 4 * n, n == 0, n == 3, kv_out)
            block_ready(N_IK)
            w = [t[:, 0, 0:KC * 80].rearrange("p (k c) -> p k c", k=KC) for t in (whi, wlo)]
            for t in range(TILES):
                for k in range(KC):
                    for m, (a, b) in enumerate(((xhi, 0), (xlo, 0), (xhi, 1))):
                        ins = mm(ps[0:ROWS[t], 5, 80 * t:80 * t + 80], a[:, k, t * P:t * P + ROWS[t]], w[b][:, k, :],
                                 start=(k == 0 and m == 0), stop=(k == KC - 1 and m == 2))
            ins.then_inc(block_used, 1)
            tiles(N_IQ, 8)
            pe.wait_ge(tile_taken, 8 + 2)
            pe.wait_ge(kv_ready, TILES)
            pe.wait_ge(ikiw_ready, 2)
            for g in range(2):
                for t in range(4):
                    ins = nc.tensor.transpose(ps[:, 4 + g, t * P:t * P + P], kv[:, t, g * P:g * P + P], ident)
            ins.then_inc(turned, 1)
            r = ROWS[4]
            for g in range(2):
                ins = nc.tensor.transpose(ps[:, 6, 80 * g:80 * g + 80], kv[0:r, 4, g * P:g * P + P],
                                          cst[0:r, C_ID:C_ID + r])
            ins.then_inc(turned, 1)
            pe.wait_ge(ik_ready, TILES)
            for t in range(4):
                ins = nc.tensor.transpose(ps[:, 7, t * P:t * P + P],
                                          ik_norm[:, t, :, :].rearrange("p c d -> p (c d)"), ident)
            ins.then_inc(turned, 1)
            nc.tensor.transpose(ps[:, 2, 0:80], ik_norm[0:r, 4, :, :].rearrange("p c d -> p (c d)"),
                                cst[0:r, C_ID:C_ID + r]).then_inc(turned, 1)
            pe.wait_ge(dw_here, 16 * 6)
            for j in range(8):
                ins = nc.tensor.transpose(ps[:, 3, j * (CW + 3):(j + 1) * (CW + 3)], dw_rows[:, j * P:(j + 1) * P],
                                          cst[0:CW + 3, C_ID:C_ID + CW + 3])
            ins.then_inc(turned, 1)
            pe.wait_ge(turned_taken, 5)

            for u in range(64):
                i, h = 1 + u // IH, u % IH
                rows, n = (P if i < 4 else LAST), min((i + 1) * P, LP)
                half = slice(64 * (h % 2), 64 * (h % 2) + 64)
                if u >= 2:
                    pe.wait_ge(relu_ready, u - 1)
                o = 2048 + 1024 * (u % 2)
                lhs = iqT[half, h // 2, i * P:i * P + rows]
                ins = mm(ps_t[0:rows, o:o + min(n, 512)], lhs, ikT[half, 0:min(n, 512)], start=True, stop=True)
                if n > 512:
                    ins = mm(ps_t[0:rows, o + 512:o + n], lhs, ikT[half, 512:n], start=True, stop=True)
                ins.then_inc(idx_out, 1)

            def turn_idx(b):
                pe.wait_ge(idx_here[b % 2], 16 * 8 * (b // 2 + 1))
                if b >= 2:
                    pe.wait_ge(idx_kT_ready, b - 1)
                for n in range(PAGES):
                    ins = nc.tensor.transpose(ps[:, 2 + b % 2, n * P:n * P + P],
                                              idx_page[:, b % 2, n, :, :].rearrange("p c d -> p (c d)"), ident)
                ins.then_inc(idx_turned, 1)

            turn_idx(0)
            pe.wait_ge(wsel_ready, DB)
            pe.wait_ge(iq_new_ready, IH // 2)
            for b in range(DB):
                if b + 1 < DB:
                    turn_idx(b + 1)
                pe.wait_ge(idx_kT_ready, b + 1)
                pe.wait_ge(relu_ready, 64 if b < 2 else 63 + b)
                o = 2048 + 1024 * (b % 2)
                at0 = LP + DS * b
                for par in range(2):
                    half = slice(64 * par, 64 * par + 64)
                    lhs = iq_new[half, b, :]
                    mm(ps_t[half, o:o + PAST], lhs, idx_kT[half, b % 2, :], start=True, stop=True)
                    ins = mm(ps_t[half, o + PAST:o + LS], lhs, ikT[half, at0:at0 + DS], start=True, stop=True)
                ins.then_inc(idx_out, 1)
                pe.wait_ge(relu_ready, 65 + b)
                r = ROWS[4]
                mm(ps[0:r, 0, :], w_sel[:, b, :], scores[:, b % 2, 0:PAST], start=(b == 0), stop=(b == DB - 1))
                ins = mm(ps[0:r, 1, 0:DS], w_sel[:, b, :], scores[:, b % 2, PAST:LS], start=(b == 0),
                         stop=(b == DB - 1))
                ins.then_inc(relu_used, 1) if b < DB - 1 else ins.then_inc(sample_scored, 1)
            pe.wait_ge(scores_done, 1)

            tiles(N_Q, 8)

            def burst(s):
                if 1 <= s <= GROUPS:
                    i, g = groups[s - 1]
                    pe.wait_ge(probs_ready, GROUP * s)
                    for r in range(GROUP):
                        for c in range(i + 1):
                            ins = nc.tensor.transpose(ps[:, 4 + r, c * P:(c + 1) * P],
                                                      probs[:, r, c * P:(c + 1) * P], ident)
                        ins.then_inc(pT_out, 1)
                    g0 = KVH * DH + g * DH
                    for r in range(GROUP):
                        pe.wait_ge(pT_ready, GROUP * (s - 1) + r + 1)
                        for c in range(i + 1):
                            ins = mm(ps[:, 4, r * P:(r + 1) * P], kv[:, c, g0:g0 + DH], pT[:, r, c * P:(c + 1) * P],
                                     start=(c == 0), stop=(c == i))
                    ins.then_inc(o_out, 1)
                if s < GROUPS:
                    i, g = groups[s]
                    for r in range(GROUP):
                        if s and r == GROUP - 1:
                            pe.wait_ge(o_taken, s)
                        mm(ps[:, 4 + (r + 1) % 4, 0:(i + 1) * P], qT[:, GROUP * g + r, i * P:(i + 1) * P],
                           kT[:, g, 0:(i + 1) * P], start=True, stop=True).then_inc(logits_out, 1)
                if s == GROUPS:
                    pe.wait_ge(q_last_ready, 1)
                    for g in range(KVH):
                        rows = slice(64 * g, 64 * g + 64)
                        mm(ps[rows, 5, :], q_last[:, rows], kT[:, g, 0:512], start=True, stop=True)
                        mm(ps[rows, 6, 0:LAST], q_last[:, rows], kT[:, g, 512:LP], start=True, stop=True)
                    r = ROWS[4]
                    s4 = bias[0:r, bias_at[4] + PAD:bias_at[4] + PAD + LP]
                    mm(ps[:, 7, :], rep_c[0:r, 2 * P:3 * P], s4[:, 0:512], start=True, stop=True)
                    mm(ps[:, 6, 64:64 + LAST], rep_c[0:r, 2 * P:3 * P], s4[:, 512:LP], start=True, stop=True
                       ).then_inc(last_logits, 1)
                if s == GROUPS + 1:
                    pe.wait_ge(last_probs, 1)
                    for c in range(4):
                        nc.tensor.transpose(ps[:, 5, c * P:(c + 1) * P], probs_last[:, c * P:(c + 1) * P], ident)
                    nc.tensor.transpose(ps[0:LAST, 6, 0:P], probs_last[:, 4 * P:LP], ident).then_inc(last_pT_out, 1)
                    pe.wait_ge(last_pT_ready, 1)
                    for g in range(KVH):
                        g0 = KVH * DH + g * DH
                        cols = slice(64 * g, 64 * g + 64)
                        for c in range(4):
                            mm(ps[:, 7, cols], kv[:, c, g0:g0 + DH], pT[:, 0, c * P + 64 * g:c * P + 64 * g + 64],
                               start=(c == 0), stop=False)
                        ins = mm(ps[:, 7, cols], kv[0:LAST, 4, g0:g0 + DH], pT[0:LAST, 1, cols], start=False, stop=True)
                    ins.then_inc(last_o_out, 1)

            pe.wait_ge(tile_taken, N_GT - C_OF + 2)
            for s in range(BURSTS):
                burst(s)
                tile_pair(N_GT + 2 * s, 0)
            tiles(N_GT + 2 * BURSTS, GT1 - 2 * BURSTS)
            pe.wait_ge(tile_taken, N_ZA - C_OF + 2)

            pe.wait_ge(last_o_taken, 1)
            pe.wait_ge(v_new_here, 16)
            pe.wait_ge(q_new_ready, HEADS)
            for half in range(2):
                if half:
                    pe.wait_ge(s_o_taken, 1)
                r = ROWS[4]
                s4 = bias[0:r, bias_at[4] + PAD:bias_at[4] + PAD + LS]
                rep = rep_c[0:r, half * P:(half + 1) * P]
                mm(ps[:, 4, :], rep, s4[:, 0:512], start=True, stop=True)
                mm(ps[:, 5, 0:DS], rep, s4[:, 512:LS], start=True, stop=True).then_inc(rep_out, 1)
                for b4 in range(4):
                    b = 4 * half + b4
                    pe.wait_ge(kpage_here, 16 * PAGES * (b + 1))
                    if b:
                        pe.wait_ge(kTs_ready, b)
                    for g in range(2):
                        for n in range(PAGES):
                            ins = nc.tensor.transpose(ps[:, g, n * P:n * P + P], kpage[:, n, g * DH:(g + 1) * DH], ident)
                    ins.then_inc(kTs_out, 1)
                    pe.wait_ge(kTs_ready, b + 1)
                    if b4 == 0:
                        pe.wait_ge(rep_taken, half + 1)
                    at0 = LP + DS * b
                    for g in range(2):
                        o = 2048 + 1024 * g
                        lhs = q_new[:, g, b, :]
                        rows = slice(32 * b4, 32 * b4 + 32)
                        mm(ps_t[rows, o:o + PAST], lhs, kTs[:, g, :], start=True, stop=True)
                        ins = mm(ps_t[rows, o + PAST:o + LS], lhs, kT[:, g, at0:at0 + DS], start=True, stop=True)
                    ins.then_inc(s_logits, 1)
                for g in range(2):
                    pe.wait_ge(s_probs, 2 * half + g + 1)
                    for n in range(PAGES):
                        nc.tensor.transpose(ps[:, g, n * P:n * P + P], scores[:, g, n * P:n * P + P], ident)
                    nc.tensor.transpose(ps[0:DS, 2 + g, 0:P], scores[:, g, PAST:LS], ident).then_inc(s_pT_out, 1)
                pe.wait_ge(vpage_here, 16 * PAGES * 4 * (half + 1))
                for g in range(2):
                    pe.wait_ge(s_pT_ready, 2 * half + g + 1)
                    for b4 in range(4):
                        cols = slice(32 * b4, 32 * b4 + 32)
                        for n in range(PAGES):
                            mm(ps[:, 4 + 2 * g, cols], vpage[:, b4, n, g * DH:(g + 1) * DH],
                               pT[:, g, n * P + 32 * b4:n * P + 32 * b4 + 32], start=(n == 0), stop=False)
                        ins = mm(ps[:, 4 + 2 * g, cols], v_new[:, 4 * half + b4, g * DH:(g + 1) * DH],
                                 pT_new[:, g, cols], start=False, stop=True)
                ins.then_inc(s_o_out, 1)
            pe.wait_ge(s_o_taken, 2)

            tiles(N_ZA, 8)
            pe.wait_ge(state_here, 32)
            for c in range(16):
                j, part = c // 2, c % 2
                if c >= 4:
                    pe.wait_ge(state_taken, c - 3)
                nc.tensor.transpose(ps[:, 4 + c % 4, 0:4 * TAIL], state[0:4 * TAIL, part, j * P:(j + 1) * P],
                                    cst[0:4 * TAIL, C_ID:C_ID + 4 * TAIL]).then_inc(state_out, 1)
            pe.wait_ge(state_taken, 16)
            tiles(N_CU, 16)
            tiles(N_ZC, 6)
            pe.wait_ge(tailT_ready, 8)
            for j in range(8):
                ins = nc.tensor.transpose(ps[0:TAIL + DB * DS, 4 + j // 4, (j % 4) * P:(j % 4 + 1) * P],
                                          tailT[:, j, :], ident)
            ins.then_inc(tail_out, 1)
            tile_pair(N_ZC + 6, 0)
            pe.wait_ge(conv_done, 1)
            for half in range(2):
                ins = mm(ps[:, 6 + half, 0:HALF], ones[:, :], c_sum[:, half * HALF:(half + 1) * HALF],
                         start=True, stop=True)
            ins.then_inc(mean_out, 1)
            tiles(N_G2, 4)
            pe.wait_ge(sq_ready, 1)
            pe.wait_ge(tail_ready, 1)
            for half in range(2):
                ins = mm(ps[:, 4 + half, 0:HALF], ones[:, :], c_sum[:, half * HALF:(half + 1) * HALF],
                         start=True, stop=True)
            ins.then_inc(var_out, 1)
            tiles(N_G2 + 4, 4)

            pe.wait_ge(tile_taken, N_BR - C_OF + 2)
            block_ready(N_BR)
            for k in range(KC):
                pe.wait_ge(xlo_ready, 4 * TILES + k + 1)
                for m, (b, x) in enumerate(((whi, xhi), (whi, xlo), (wlo, xhi))):
                    for half in range(2):
                        ins = mm(ps[:, 2 * (k // 8) + half, 0:HALF], b[:, 1, k * P:(k + 1) * P],
                                 x[:, k, half * HALF:(half + 1) * HALF],
                                 start=(k % 8 == 0 and m == 0), stop=(k % 8 == 7 and m == 2))
            ins.then_inc(block_used, 1)

            def branch(n, buf, o):
                block_ready(n)
                tile_block(buf, o, 0, 8)
                tile_block(buf, o + 2, 8, 8).then_inc(block_used, 1)

            branch(N_BR + 1, 0, 4)
            with pe.Fori(0, 7) as i:
                for b in range(2):
                    pe.wait_ge(br_taken, 1 + b + i * 2)
                    branch(N_BR + 2 + b + i * 2, (1 + b) % 2, 4 * b)

            with pe.Fori(0, 4) as i:
                for r in range(4):
                    pe.wait_ge(mlo_ready, 4 * r + 4)
                    rows_block(N_WO + r + i * 4, (N_WO + r) % 2, mhi, mlo, 4 * r, r == 0, r == 3, y_out,
                               i * TILES if r == 0 else None)

    return nc


INS = ["x_prompt", "x_sample", "cache_k", "cache_v", "cache_idx_k", "state_conv", "page_table", "meta_tokens",
       "w_in", "ln_idx_g", "ln_idx_b", "w_dw", "b_dw", "ln_conv_g", "ln_conv_b", "w_att_out", "w_conv_out", "w_o",
       "ln_post_g", "ln_post_b"]
OUTS = [(1, SEQ, D), (DB, DS, D), (1, LP, KVH, DH), (1, LP, KVH, DH), (1, LP, IDIM), (1, TAIL, DC),
        (DB, DS, KVH, DH), (DB, DS, KVH, DH), (DB, DS, IDIM), (DB, TAIL, DC)]


def kernel(**inputs):
    import numpy as _np
    import concourse.bacc as _bacc
    from concourse import mybir as _mybir
    from concourse.bass_utils import run_bass_kernel_spmd as _run

    nc = _bacc.Bacc("TRN2", target_bir_lowering=False, num_devices=1)
    arrays, args = {}, []
    for name in INS:
        arrays[f"in_{name}_dram"] = _np.ascontiguousarray(inputs[name])
    for name, a in zip(("consts", "consts2"), shape_constants()):
        arrays[f"in_{name}_dram"] = a
    for name, a in arrays.items():
        args.append(nc.dram_tensor(name, a.shape, _mybir.dt.from_np(a.dtype), kind="ExternalInput").ap())
    for i, shape in enumerate(OUTS):
        args.append(nc.dram_tensor(f"out_{i}_dram", shape, _mybir.dt.float32, kind="ExternalOutput").ap())
    build(nc, *args)
    r = _run(nc, [arrays], core_ids=[0])
    return tuple(r.results[0][f"out_{i}_dram"] for i in range(len(OUTS)))
```

```python
from contextlib import ExitStack

import concourse.bass as bass
import numpy as np
from concourse import mybir

F32 = mybir.dt.float32
F32R = mybir.dt.float32r
I32 = mybir.dt.int32
ALU = mybir.AluOpType
ACT = mybir.ActivationFunctionType
AX_X = mybir.AxisListType.X
ds = bass.ds

P = 128
D = 2048
SEQ = 512
META = 16
LP = SEQ + META
DB = 8
DS = 8
PAST = 512
PAGES = PAST // P
HEADS, DH, KVH = 8, 128, 2
GROUP = HEADS // KVH
IH, IDIM = 16, 64
DC = 1024
CW = 31
TAIL = CW - 1
ALPHA = 2.0 ** 0.25
EPS = 1e-5
TOK = LP + DB * DS
HALF = TOK // 2
KC = D // P
TILES = 5
ROWS = [P, P, P, P, TOK - 4 * P]
LAST = LP - 4 * P
LS = PAST + DS
CUT = dict(q=0, kv=1024, iq=1536, ik=2560, za=2640, ga=3664, gb=4688, zc=5712, gt=6736)

MASKED = -3.0e38
TAKEN = -3.4e38
BETWEEN = -3.2e38
FAR = -1.0e32
PAD = 8
TOP_P = min(256, SEQ // 4)
TOP_S = min(256, LS // 4)
EXT = TAIL + LP
UW = EXT + DB * (TAIL + DS)

N_KV, N_IK, N_IQ, N_Q, N_GT, N_ZA, N_CU, N_ZC, N_G2, N_BR, N_WO = 0, 4, 5, 13, 21, 45, 53, 69, 77, 85, 101
N_END = 117
C_OF = N_IQ
GT1 = N_ZA - N_GT

C_ID, C_TRI, C_DIV, C_SLOPE, C_PAD, C_NEW, C_DIV2, C_END = 0, 128, 256, 264, 267, 275, 291, 307
E_DIST, E_DIST4, E_REP, E_END = 0, LP, 2 * LP, 2 * LP + 3 * P


def shape_constants():
    c = np.zeros((P, C_END), np.float32)
    p = np.arange(P)
    c[:, C_ID:C_ID + P] = np.eye(P)
    c[:, C_TRI:C_TRI + P] = np.where(p[None, :] > p[:, None], MASKED, 0.0)
    c[:, C_DIV:C_DIV + DS] = (p[:, None] % DS) == np.arange(DS)[None, :]
    c[:, C_DIV2:C_DIV2 + LAST] = (p[:, None] % LAST) == np.arange(LAST)[None, :]
    for g in range(KVH):
        c[:, C_SLOPE + g] = 2.0 ** -(1.0 + g * GROUP + (p // DS) % GROUP)
    c[:, C_SLOPE + KVH] = 2.0 ** -(1.0 + p // LAST)
    c[:, C_PAD:C_PAD + PAD] = -MASKED
    c[LAST:, C_PAD + PAD - (TOP_S - TOP_P):C_PAD + PAD] = MASKED
    new = np.zeros((P, META), np.float32)
    for r in range(ROWS[4]):
        seen = r + 1 if r < LAST else (r - LAST) % DS + 1
        new[r, seen:] = MASKED
    c[:, C_NEW:C_NEW + META] = new
    e = np.zeros((P, E_END), np.float32)
    k = np.arange(LP)
    e[:, E_DIST:E_DIST + LP] = k[None, :] - p[:, None]
    for r in range(ROWS[4]):
        at = 4 * P + r if r < LAST else PAST + (r - LAST) % DS
        e[r, E_DIST4:E_DIST4 + LP] = k - at
    for half in range(2):
        for m in range(P):
            b, t = m // (GROUP * DS), m % DS
            e[LAST + DS * (4 * half + b) + t, E_REP + half * P + m] = 1.0
    e[p % LAST, E_REP + 2 * P + p] = 1.0
    return c, e


def landed_after():
    total, out = [0, 0], []
    for n in range(N_END):
        total[n % 2] += 32 if N_BR <= n < N_WO else 16
        out.append(total[n % 2])
    return out


LANDED = landed_after()


def build(nc, x_prompt, x_sample, cache_k, cache_v, cache_idx_k, state_conv, page_table, meta_tokens,
          w_in, ln_idx_g, ln_idx_b, w_dw, b_dw, ln_conv_g, ln_conv_b, w_att_out, w_conv_out, w_o,
          ln_post_g, ln_post_b, consts, consts2,
          y_prompt, y_sample, k_prompt, v_prompt, idx_k_prompt, conv_prompt,
          k_sample, v_sample, idx_k_sample, conv_sample):
    gates = nc.dram_tensor("gates_dram", [32, P, TOK], F32)
    iw_dram = nc.dram_tensor("iw_dram", [ROWS[4], IH], F32)

    base = -(-nc.sbuf_base // 32) * 32

    def at(name, shape, dt, offset):
        return nc.alloc_sbuf_tensor_at(name, shape, dt, offset=base + offset)

    XB = KC * TOK * 4
    xhi = at("xhi", [P, KC, TOK], F32R, 0)
    xlo = at("xlo", [P, KC, TOK], F32R, XB)
    y = at("y", [P, TILES, D], F32, 0)
    post_g = at("post_g", [P, D], F32, TILES * D * 4)
    post_b = at("post_b", [P, D], F32, (TILES + 1) * D * 4)
    W0 = 2 * XB
    BL = KC * P * 4
    raw = at("raw", [P, 2, KC * P], F32, W0)
    whi = at("whi", [P, 2, KC * P], F32R, W0 + 2 * BL)
    wlo = at("wlo", [P, 2, KC * P], F32R, W0 + 4 * BL)
    B0 = W0 + 6 * BL
    HB = 8 * TOK * 4
    xn = at("xn", [P, TILES, D], F32, B0)
    qT = at("qT", [P, 8, TOK], F32, B0)
    iqT = at("iqT", [P, 8, TOK], F32, B0 + HB)
    zc = at("zc", [P, 8, TOK], F32, B0 + HB)
    vpage = at("vpage", [P, 4, PAGES, 2 * DH], F32, B0 + HB)
    dist_c = at("dist_c", [P, 2 * LP], F32, B0 + HB)
    rep_c = at("rep_c", [P, 3 * P], F32, B0 + HB + 16384)
    idx_page = at("idx_page", [P, 4, PAGES, 2, IDIM], F32, B0)
    w_sel = at("w_sel", [P, DB, ROWS[4]], F32, B0 + 8192)
    ik_norm = at("ik_norm", [P, TILES, 2, IDIM], F32, B0 + 10752)
    dw_rows = at("dw_rows", [CW + 3, DC], F32, B0 + 13312)
    idx_gb = at("idx_gb", [P, 2, IDIM], F32, B0 + 17408)
    R0 = B0 + 2 * HB
    kT = at("kT", [P, KVH, TOK], F32, R0)
    ikZ = at("ikZ", [P, 2, LP], F32, B0 + 13312)
    ik_new = at("ik_new", [P, DB * DS], F32, R0 + 4736)
    iq_last = at("iq_last", [P, IH // 2 * LAST], F32, R0 + 5248)
    w_last = at("w_last", [P, 2, ROWS[4]], F32, R0 + 5760)
    kv = at("kv", [P, TILES, 2 * KVH * DH], F32, R0 + 7104)
    v_new = at("v_new", [DS, DB // 2, KVH * DH], F32, R0 + 7104)
    scores_s = at("scores_s", [P, KVH, LP], F32, R0 + 13120)
    S0 = R0 + 17344
    bias_w = [P, 2 * P, 3 * P, 4 * P, PAD + LP]
    bias_at = [0, P, 3 * P, 6 * P, 10 * P]
    bias = at("bias", [P, sum(bias_w)], F32, S0)
    scores = at("scores", [P, 2, LP], F32, S0 + 7264)
    ikiw = at("ikiw", [P, TILES, IDIM + IH], F32, S0 + 11488)
    tmp_gate = at("tmp_gate", [P, 2, TOK], F32, S0 + 7264)
    pT = at("pT", [P, GROUP, 4 * P], F32, S0 + 12000)
    kTs = at("kTs", [P, 2, PAST], F32, S0 + 12000 + 4096)
    bias_s = at("bias_s", [P, LP], F32, S0 + 2048)
    ikiwT = at("ikiwT", [IDIM + IH, TOK], F32, S0 + 17184)
    o_rows = at("o_rows", [P, KVH * DH], F32, R0 + 13120)
    q_last = at("q_last", [P, HEADS * LAST], F32, R0 + 4736)
    iq_new = at("iq_new", [P, DB, 2, IH // 2 * DS], F32, S0 + 13088)
    q_new = at("q_new", [P, KVH, DB, GROUP * DS], F32, S0)
    pT_new = at("pT_new", [DS, 2, P], F32, R0 + 5248)
    U = at("U", [P, 8, UW], F32, R0)
    tmp_lin = at("tmp_lin", [P, 2, TOK], F32, R0 + 27584)
    tmp_tanh = at("tmp_tanh", [P, 2, TOK], F32, R0 + 27584 + 4736)
    u_tail = at("u_tail", [P, DC], F32, R0 + 27584)
    mhi = at("mhi", [P, KC, TOK], F32R, B0)
    mlo = at("mlo", [P, KC, TOK], F32R, B0 + XB)
    gate0 = at("gate0", [P, KC, TOK], F32, B0)
    gate1 = at("gate1", [P, KC, TOK], F32, B0 + XB)
    M0 = B0 + 2 * XB
    cst = at("cst", [P, C_END], F32, M0)
    ones = at("ones", [P, P], F32, M0 + 1248)
    dwT = at("dwT", [P, 8, CW + 3], F32, M0 + 1760)
    small = at("small", [P, 128], F32, M0 + 2848)
    pages = at("pages", [1, DB * PAGES], I32, M0 + 3360)
    relus = at("relus", [P, 4, 4 * P], F32, M0 + 3488)
    idx_kT = at("idx_kT", [P, 2, PAST], F32, M0 + 3488)
    probs = at("probs", [P, GROUP, 4 * P], F32, M0 + 3488)
    probs_last = at("probs_last", [P, LP], F32, M0 + 3488)
    kpage = at("kpage", [P, 2, PAGES, 2 * DH], F32, M0 + 3488)
    state = at("state", [P, 2, DC], F32, M0 + 3488)
    c_acc = at("c_acc", [P, TOK], F32, M0 + 3488)
    c_sum = at("c_sum", [P, TOK], F32, M0 + 3488 + 2368)
    c_rstd = at("c_rstd", [P, TOK], F32, M0 + 3488 + 4736)
    tailT = at("tailT", [P, 8, TAIL + DB * DS], F32, M0 + 3488 + 4736)
    yst = at("yst", [P, TILES, 24], F32, M0 + 3488 + 4736)
    m_tmp = at("m_tmp", [P, 2, TOK], F32, M0 + 3488)
    ident = cst[:, C_ID:C_ID + P]

    st = small[:, 0:30]
    mv = small[:, 30:40]
    rs = small[:, 40:45]
    wcol = small[:, 48:56]
    top8 = small[:, 56:64]
    neg_max = small[:, 88:96]
    exp_sum = small[:, 96:104]
    inv_sum = small[:, 104:112]
    half_g = small[:, 72:80]
    half_b = small[:, 80:88]
    ymv = small[:, 112:114]
    y_rstd = small[:, 114:119]
    y_shift = small[:, 119:124]
    wait_carrier = small[:, 124:125]
    wcol_last = small[:, 125:127]

    with ExitStack() as ctx:
        ps_t = ctx.enter_context(nc.psum_tensor("ps", [P, 8 * 512], F32))
        ps = ps_t[:, :].rearrange("p (b n) -> p b n", b=8)

        def sem(name):
            return ctx.enter_context(nc.semaphore(name))

        x_here = [sem(f"x_here{i}") for i in range(TILES)]
        consts_here = sem("consts_here")
        consts2_here = sem("consts2_here")
        dw_here = sem("dw_here")
        pages_here = sem("pages_here")
        raw_here = [sem("raw_here0"), sem("raw_here1")]
        hi_ready = sem("hi_ready")
        lo_ready = sem("lo_ready")
        block_used = sem("block_used")
        xT_out = sem("xT_out")
        xhi_ready = sem("xhi_ready")
        xlo_ready = sem("xlo_ready")
        kv_out = sem("kv_out")
        kv_ready = sem("kv_ready")
        ikiwT_ready = sem("ikiwT_ready")
        ikiw_out = sem("ikiw_out")
        ikiw_ready = sem("ikiw_ready")
        ik_var = sem("ik_var")
        ik_std = sem("ik_std")
        ik_ready = sem("ik_ready")
        tile_taken = sem("tile_taken")
        turned = sem("turned")
        turned_taken = sem("turned_taken")
        iw_stored = sem("iw_stored")
        wcol_here = sem("wcol_here")
        wsel_ready = sem("wsel_ready")
        idx_here = [sem(f"idx_here{i}") for i in range(4)]
        idx_turned = sem("idx_turned")
        idx_kT_ready = sem("idx_kT_ready")
        idx_out = sem("idx_out")
        relu_ready = sem("relu_ready")
        relu_used = sem("relu_used")
        sums_out = sem("sums_out")
        last_scored = sem("last_scored")
        dw_out = sem("dw_out")
        dwT_ready = sem("dwT_ready")
        ikZ_clear = sem("ikZ_clear")
        bias_ready = sem("bias_ready")
        gate_stored = [sem("gate_stored0"), sem("gate_stored1")]
        logits_out = sem("logits_out")
        max_ready = sem("max_ready")
        exp_ready = sem("exp_ready")
        probs_ready = sem("probs_ready")
        pT_out = sem("pT_out")
        pT_ready = sem("pT_ready")
        o_out = sem("o_out")
        o_taken = sem("o_taken")
        q_last_ready = sem("q_last_ready")
        last_logits = sem("last_logits")
        last_max = sem("last_max")
        last_exp = sem("last_exp")
        last_probs = sem("last_probs")
        last_pT_out = sem("last_pT_out")
        last_pT_ready = sem("last_pT_ready")
        last_o_out = sem("last_o_out")
        last_o_taken = sem("last_o_taken")
        rep_out = sem("rep_out")
        rep_taken = sem("rep_taken")
        kpage_here = [sem("kpage_here0"), sem("kpage_here1")]
        vpage_here = sem("vpage_here")
        v_new_here = sem("v_new_here")
        kTs_out = sem("kTs_out")
        kTs_ready = sem("kTs_ready")
        s_logits = sem("s_logits")
        s_max = sem("s_max")
        s_exp = sem("s_exp")
        s_probs = sem("s_probs")
        s_pT_out = sem("s_pT_out")
        s_pT_ready = sem("s_pT_ready")
        s_o_out = sem("s_o_out")
        s_o_rows = sem("s_o_rows")
        s_o_turned = sem("s_o_turned")
        s_o_taken = sem("s_o_taken")
        za_used = sem("za_used")
        state_here = sem("state_here")
        state_out = sem("state_out")
        state_taken = sem("state_taken")
        conv_done = sem("conv_done")
        conv_summed = sem("conv_summed")
        tail_out = sem("tail_out")
        tail_ready = sem("tail_ready")
        tail_stored = sem("tail_stored")
        zc_done = sem("zc_done")
        mean_out = sem("mean_out")
        sq_ready = sem("sq_ready")
        var_out = sem("var_out")
        std_in = sem("std_in")
        std_ready = sem("std_ready")
        n_ready = sem("n_ready")
        lin_ready = sem("lin_ready")
        tanh_ready = sem("tanh_ready")
        c_ready = sem("c_ready")
        gate_here = [sem(f"gate_here{i}") for i in range(8)]
        br_taken = sem("br_taken")
        m_ready = sem("m_ready")
        mhi_ready = sem("mhi_ready")
        mlo_ready = sem("mlo_ready")
        y_here = sem("y_here")
        post_here = sem("post_here")
        y_scaled = sem("y_scaled")
        y_out = sem("y_out")
        y_taken = sem("y_taken")
        y_var = sem("y_var")
        y_std = sem("y_std")
        y_norm_in = sem("y_norm_in")
        y_norm = sem("y_norm")
        y_times_g = sem("y_times_g")
        y_final = sem("y_final")
        y_final_last = sem("y_final_last")
        dve_step = sem("dve_step")
        pool_step = sem("pool_step")
        topk_step = sem("topk_step")
        conv_step = sem("conv_step")
        stored = sem("stored")
        idx_stored = sem("idx_stored")
        iq_new_ready = sem("iq_new_ready")
        q_new_ready = sem("q_new_ready")
        tailT_ready = sem("tailT_ready")

        stores = [0]

        def w_cols(c0, k0=0, kn=KC, width=P, w=w_in):
            return w[k0 * P:(k0 + kn) * P, c0:c0 + width] if isinstance(c0, int) else \
                w[k0 * P:(k0 + kn) * P, ds(c0, width)]

        def turn_bank(g):
            return g if g < 8 else 5 + g % 3

        groups = [(i, h0, nh) for i, nh in ((0, 8), (1, 8), (2, 4), (3, 4)) for h0 in range(0, HEADS, nh)]
        GROUPS = len(groups)
        S_LAST, O_LAST = GROUPS, GROUPS + 1
        S_NEW = [GROUPS + 2 + k for k in range(4)]
        O_NEW = [GROUPS + 4, GROUPS + 6]
        PAIRS = GT1 // 2
        assert PAIRS == O_NEW[1]

        HEAD_UNITS = 3 * IH
        Y_BANK = 4

        def units(s):
            i, h0, nh = groups[s]
            per = nh // 4
            before = sum(g[2] for g in groups[:s])
            return [(h0 + j, before + j, j // per, (j % per) * 2 * P) for j in range(nh)]

        def sample_cols(a, j):
            v = a[:, j, EXT:UW] if isinstance(j, int) else a[:, ds(j, 1), EXT:UW].rearrange("p a w -> p (a w)")
            return v.rearrange("p (b w) -> p b w", b=DB)

        block = ctx.enter_context(nc.Block())

        @block.sync
        def _(sp):
            def buffer_free(n):
                sp.wait_ge(hi_ready, n - 1)
                sp.wait_ge(lo_ready, n - 1)

            def load_rows(n, w, k0, c0):
                if n >= 2:
                    buffer_free(n)
                sp.dma_start(raw[:, n % 2, :].rearrange("p (k c) -> p k c", k=4),
                             w[k0 * P:(k0 + 4) * P, c0:c0 + 512].rearrange("(k p) c -> p k c", p=P)
                             ).then_inc(raw_here[n % 2], 16)

            def load_tile(n, c0, buf):
                buffer_free(n)
                sp.dma_start(raw[:, buf, :].rearrange("p (k c) -> p k c", k=KC),
                             w_cols(c0).rearrange("(k p) c -> p k c", p=P)).then_inc(raw_here[buf], 16)

            def load_tiles(n0, count, c0, c1=None):
                with sp.Fori(0, count // 2) as i:
                    if c1 is None:
                        load_tile(n0 + i * 2, c0 + i * 256, n0 % 2)
                        load_tile(n0 + 1 + i * 2, c0 + P + i * 256, (n0 + 1) % 2)
                    else:
                        load_tile(n0 + i * 2, c0 + i * P, n0 % 2)
                        load_tile(n0 + 1 + i * 2, c1 + i * P, (n0 + 1) % 2)

            sp.dma_start(cst[:, :], consts).then_inc(consts_here, 16)
            sp.dma_start(xn[0:META, 0, :], meta_tokens).then_inc(x_here[0], 16)
            sp.dma_start(xn[META:P, 0, :], x_prompt[0, 0:P - META, :]).then_inc(x_here[0], 16)
            load_rows(0, w_in, 0, CUT["kv"])
            for t in range(1, 4):
                sp.dma_start(xn[:, t, :], x_prompt[0, t * P - META:(t + 1) * P - META, :]).then_inc(x_here[t], 16)
            sp.dma_start(xn[0:LAST, 4, :], x_prompt[0, SEQ - LAST:SEQ, :]).then_inc(x_here[4], 16)
            sp.dma_start(xn[LAST:ROWS[4], 4, :], x_sample.rearrange("b t d -> (b t) d")).then_inc(x_here[4], 16)
            for n in range(1, 4):
                load_rows(n, w_in, 4 * n, CUT["kv"])
            sp.dma_start(pages[:, :], page_table.rearrange("(o b) n -> o (b n)", o=1)).then_inc(pages_here, 16)
            buffer_free(N_IK)
            sp.dma_start(raw[:, 0, 0:KC * 80].rearrange("p (k c) -> p k c", k=KC),
                         w_cols(CUT["ik"], width=80).rearrange("(k p) c -> p k c", p=P)).then_inc(raw_here[0], 16)
            sp.wait_ge(xT_out, 4 * TILES)
            sp.dma_start(dw_rows[0:CW, :], w_dw).then_inc(dw_here, 16)
            for r, v in enumerate((b_dw, ln_conv_g, ln_conv_b)):
                sp.dma_start(dw_rows[CW + r:CW + r + 1, :], v.rearrange("(o c) -> o c", o=1)).then_inc(dw_here, 16)
            for r, v in enumerate((ln_idx_g, ln_idx_b)):
                sp.dma_start(idx_gb[:, r, :], v.rearrange("(o c) -> o c", o=1).broadcast_to([P, IDIM])
                             ).then_inc(dw_here, 16)
            sp.wait_ge(pages_here, 16)

            def page(b, n):
                return sp.value_load(pages[0:1, b * PAGES + n:b * PAGES + n + 1], min_val=0,
                                     max_val=cache_k.shape[0] - 1)

            def load_idx(b):
                if b >= 4:
                    sp.wait_ge(idx_turned, b - 3)
                for n in range(PAGES):
                    v = page(b, n)
                    sp.dma_start(idx_page[:, b % 4, n, :, :],
                                 cache_idx_k[ds(v, 1), :, :].rearrange("a t (o d) -> (a t) o d", o=1)
                                 .broadcast_to([P, 2, IDIM])).then_inc(idx_here[b % 4], 16)

            for b in range(4):
                load_idx(b)
            load_tiles(N_IQ, 8, CUT["iq"])
            load_tile(N_Q, CUT["q"], N_Q % 2)
            sp.wait_ge(kv_ready, TILES)
            for t in range(4):
                for c, o in ((0, k_prompt), (1, v_prompt)):
                    sp.dma_start(o[0, t * P:(t + 1) * P].rearrange("t g d -> t (g d)"),
                                 kv[:, t, 256 * c:256 * c + 256]).then_inc(stored, 16)
                    stores[0] += 1
            for c, o, s in ((0, k_prompt, k_sample), (1, v_prompt, v_sample)):
                sp.dma_start(o[0, 4 * P:LP].rearrange("t g d -> t (g d)"),
                             kv[0:LAST, 4, 256 * c:256 * c + 256]).then_inc(stored, 16)
                sp.dma_start(s.rearrange("b t g d -> (b t) (g d)"),
                             kv[LAST:ROWS[4], 4, 256 * c:256 * c + 256]).then_inc(stored, 16)
                stores[0] += 2
            kv_stores = stores[0]
            sp.wait_ge(ikiw_ready, 2)
            sp.dma_start(iw_dram[:, :], ikiw[0:ROWS[4], 4, IDIM:]).then_inc(iw_stored, 16)
            sp.wait_ge(iw_stored, 16)
            for h in range(IH):
                p0 = 64 * (h % 2) + DS * (h // 2)
                sp.dma_start(wcol[p0:p0 + DS, :], iw_dram[LAST:ROWS[4], h:h + 1].rearrange("(b t) o -> t (b o)", t=DS),
                             allow_slow_non_contiguous=True).then_inc(wcol_here, 16)
            for j in range(IH // 2):
                sp.dma_start(wcol_last[LAST * j:LAST * (j + 1), :], iw_dram[0:LAST, 2 * j:2 * j + 2]
                             ).then_inc(wcol_here, 16)
            sp.wait_ge(ik_ready, TILES)
            for t in range(4):
                sp.dma_start(idx_k_prompt[0, t * P:(t + 1) * P, :], ik_norm[:, t, 0, :]).then_inc(idx_stored, 16)
            sp.dma_start(idx_k_prompt[0, 4 * P:LP, :], ik_norm[0:LAST, 4, 0, :]).then_inc(idx_stored, 16)
            sp.dma_start(idx_k_sample.rearrange("b t d -> (b t) d"), ik_norm[LAST:ROWS[4], 4, 0, :]
                         ).then_inc(idx_stored, 16)

            for b in range(4, DB):
                load_idx(b)
            load_tile(N_Q + 1, CUT["q"] + P, (N_Q + 1) % 2)
            sp.wait_ge(idx_out, HEAD_UNITS + 2 + DB)
            sp.dma_start(dist_c[:, :], consts2[:, 0:2 * LP]).then_inc(consts2_here, 16)
            sp.dma_start(rep_c[:, :], consts2[:, E_REP:E_END]).then_inc(consts2_here, 16)
            load_tiles(N_Q + 2, 6, CUT["q"] + 2 * P)
            def load_v(half):
                for b in range(4):
                    for n in range(PAGES):
                        v = page(4 * half + b, n)
                        sp.dma_start(vpage[:, b, n, :], cache_v[ds(v, 1)].rearrange("a t g d -> (a t) (g d)")
                                     ).then_inc(vpage_here, 16)

            def load_k(b):
                for n in range(PAGES):
                    v = page(b, n)
                    sp.dma_start(kpage[:, b % 2, n, :], cache_k[ds(v, 1)].rearrange("a t g d -> (a t) (g d)")
                                 ).then_inc(kpage_here[b % 2], 16)

            def load_v_new(half):
                sp.dma_start(v_new[:, :, :], v_sample[4 * half:4 * half + 4].rearrange("b t g d -> t b (g d)")
                             ).then_inc(v_new_here, 16)

            def load_pair(s):
                for b in range(2):
                    load_tile(N_GT + 2 * s + b, CUT["gt"] + (2 * s + b) * P, (N_GT + b) % 2)

            load_tiles(N_GT, 2 * (O_LAST + 1), CUT["gt"])
            sp.wait_ge(bias_ready, TILES)
            load_v(0)
            load_pair(O_LAST + 1)
            sp.wait_ge(last_o_out, 1)
            sp.wait_ge(stored, 16 * kv_stores)
            load_k(0)
            load_k(1)
            load_v_new(0)
            load_pair(O_LAST + 2)
            for k in range(1, 3):
                sp.wait_ge(kTs_out, 4 * k)
                load_k(2 * k)
                load_k(2 * k + 1)
                load_pair(O_LAST + 2 + k)
            sp.wait_ge(kTs_out, 12)
            load_k(6)
            load_k(7)
            sp.wait_ge(s_o_out, 1)
            load_v(1)
            load_v_new(1)
            load_tile(N_ZA, CUT["za"], N_ZA % 2)
            load_tile(N_ZA + 1, CUT["za"] + P, (N_ZA + 1) % 2)
            load_tiles(N_ZA + 2, 6, CUT["za"] + 2 * P)
            sp.wait_ge(kTs_out, 2 * DB)
            for c in range(2):
                sp.dma_start(state[0:4 * TAIL, c, :], state_conv[4 * c:4 * c + 4].rearrange("b t c -> (b t) c")
                             ).then_inc(state_here, 16)
            sp.dma_start(conv_sample[:, 0:TAIL - DS, :], state_conv[:, DS:TAIL, :]).then_inc(stored, 16)
            stores[0] += 1
            load_tiles(N_CU, 16, CUT["ga"], CUT["gb"])
            load_tile(N_ZC, CUT["zc"], N_ZC % 2)
            load_tile(N_ZC + 1, CUT["zc"] + P, (N_ZC + 1) % 2)
            load_tiles(N_ZC + 2, 6, CUT["zc"] + 2 * P)
            sp.wait_ge(tail_ready, 1)
            sp.dma_start(conv_prompt[0], u_tail[0:TAIL, :]).then_inc(tail_stored, 16)
            for b in range(DB):
                sp.dma_start(conv_sample[b, TAIL - DS:TAIL, :], u_tail[TAIL + DS * b:TAIL + DS * b + DS, :]
                             ).then_inc(tail_stored, 16)
            load_tiles(N_G2, N_BR - N_G2, CUT["gt"] + GT1 * P)

            def branch_pair(i):
                for b in range(2):
                    n = N_BR + 2 * i + b
                    buffer_free(n)
                    for c, w in ((0, w_att_out), (1, w_conv_out)):
                        sp.dma_start(raw[:, n % 2, c * DC:(c + 1) * DC].rearrange("p (k c) -> p k c", k=8),
                                     w[:, (2 * i + b) * P:(2 * i + b + 1) * P].rearrange("(k p) c -> p k c", p=P)
                                     ).then_inc(raw_here[n % 2], 16)

            branch_pair(0)
            for s in gate_stored:
                sp.wait_ge(s, 16 * 16)
            sp.wait_ge(xhi_ready, 4 * TILES + KC)
            sp.wait_ge(xlo_ready, 4 * TILES + KC)
            for i in range(8):
                if i:
                    branch_pair(i)
                for g, dst in ((0, gate0), (1, gate1)):
                    sp.dma_start(dst[:, 2 * i:2 * i + 2, :],
                                 gates[16 * g + 2 * i:16 * g + 2 * i + 2].rearrange("j p t -> p j t")
                                 ).then_inc(gate_here[i], 16)
            for r in range(2):
                load_rows(N_WO + r, w_o, 4 * r, 0)
            load_rows(N_WO + 2, w_o, 8, 0)
            sp.wait_ge(block_used, N_WO)
            sp.dma_start(y[0:META, 0, :], meta_tokens).then_inc(y_here, 16)
            sp.dma_start(y[META:P, 0, :], x_prompt[0, 0:P - META, :]).then_inc(y_here, 16)
            for t in range(1, 4):
                sp.dma_start(y[:, t, :], x_prompt[0, t * P - META:(t + 1) * P - META, :]).then_inc(y_here, 16)
            sp.dma_start(y[0:LAST, 4, :], x_prompt[0, SEQ - LAST:SEQ, :]).then_inc(y_here, 16)
            sp.dma_start(y[LAST:ROWS[4], 4, :], x_sample.rearrange("b t d -> (b t) d")).then_inc(y_here, 16)
            for v, dst in ((ln_post_g, post_g), (ln_post_b, post_b)):
                sp.dma_start(dst[:, :], v.rearrange("(o c) -> o c", o=1).broadcast_to([P, D])).then_inc(post_here, 16)
            for n in range(N_WO + 3, N_END):
                r = n - N_WO
                load_rows(n, w_o, 4 * (r % 4), 512 * (r // 4))
            for t in range(TILES):
                for half in range(2):
                    c = slice(half * (D // 2), (half + 1) * (D // 2))
                    if t < 4:
                        sp.wait_ge(y_final, 2 * t + half + 1)
                    else:
                        sp.wait_ge(y_final_last, half + 1)
                    if t == 0:
                        sp.dma_start(y_prompt[0, 0:P - META, c], y[META:P, 0, c]).then_inc(stored, 16)
                    elif t < 4:
                        sp.dma_start(y_prompt[0, t * P - META:(t + 1) * P - META, c], y[:, t, c]).then_inc(stored, 16)
                    else:
                        sp.dma_start(y_prompt[0, SEQ - LAST:SEQ, c], y[0:LAST, 4, c]).then_inc(stored, 16)
                        sp.dma_start(y_sample.rearrange("b t d -> (b t) d")[:, c], y[LAST:ROWS[4], 4, c]
                                     ).then_inc(stored, 16)
                        stores[0] += 1
                    stores[0] += 1
            sp.wait_ge(tail_stored, 16 * (1 + DB))
            sp.wait_ge(idx_stored, 16 * 6)
            sp.wait_ge(stored, 16 * stores[0])

        @block.gpsimd
        def _(pool):
            steps = [0]

            def link(ins):
                steps[0] += 1
                ins.then_inc(pool_step, 1)
                pool.wait_ge(pool_step, steps[0])

            def split_lo(n, buf, width=KC * P):
                pool.wait_ge(hi_ready, n + 1)
                nc.gpsimd.tensor_tensor(wlo[:, buf, 0:width], raw[:, buf, 0:width],
                                        whi[:, buf, 0:width].bitcast(F32), ALU.subtract).then_inc(lo_ready, 1)

            for n in range(N_IK):
                split_lo(n, n % 2)
            split_lo(N_IK, 0, KC * 80)
            with pool.Fori(0, (N_ZA - N_IQ) // 2) as i:
                for b in range(2):
                    split_lo(N_IQ + b + i * 2, (N_IQ + b) % 2)
            split_lo(N_ZA, N_ZA % 2)
            for j in range(8):
                split_lo(N_ZA + j + 1, (N_ZA + j + 1) % 2)
                pool.wait_ge(tile_taken, N_ZA + j - C_OF + 3)
                s = j % 2
                link(nc.gpsimd.tensor_tensor(tmp_tanh[:, s, :], tmp_tanh[:, s, :], tmp_lin[:, s, :], ALU.mult))
                link(nc.gpsimd.tensor_tensor(tmp_tanh[:, s, :], tmp_tanh[:, s, :], tmp_lin[:, s, :], ALU.add))
                pool.wait_ge(s_o_taken, 2)
                nc.gpsimd.tensor_tensor(qT[:, j, :], qT[:, j, :], tmp_tanh[:, s, :], ALU.mult).then_inc(za_used, 1)
            with pool.Fori(0, (N_ZC - N_CU) // 2) as i:
                for b in range(2):
                    split_lo(N_CU + 1 + b + i * 2, (N_CU + 1 + b) % 2)

            def sum_conv(k):
                pool.wait_ge(conv_done, k + 1)
                sums = c_sum[:, LP:TOK].rearrange("p (b t) -> p b t", b=DB)
                before, before_s = c_sum[:, 0:LP], sums
                if k == 1:
                    before, before_s = U[:, 0, TAIL:EXT], sample_cols(U, 0)[:, :, TAIL:]
                nc.gpsimd.tensor_tensor(c_sum[:, 0:LP], before, U[:, k, TAIL:EXT], ALU.add)
                link(nc.gpsimd.tensor_tensor(sums, before_s, sample_cols(U, k)[:, :, TAIL:], ALU.add))

            for j in range(8):
                split_lo(N_ZC + j + 1, (N_ZC + j + 1) % 2)
                for k in {0: (1,), 1: (2, 3), 2: (4,), 3: (5,), 5: (6,), 7: (7,)}.get(j, ()):
                    sum_conv(k)
                if j == 7:
                    pool.sem_inc(conv_summed, 1)
                pool.wait_ge(tile_taken, N_ZC + j - C_OF + 3)
                s = j % 2
                link(nc.gpsimd.tensor_tensor(tmp_tanh[:, s, :], tmp_tanh[:, s, :], zc[:, j, :], ALU.mult))
                nc.gpsimd.tensor_tensor(zc[:, j, :], tmp_tanh[:, s, :], zc[:, j, :], ALU.add).then_inc(zc_done, 1)
            with pool.Fori(0, (N_BR - N_G2) // 2) as i:
                for b in range(2):
                    split_lo(N_G2 + 1 + b + i * 2, (N_G2 + 1 + b) % 2)
            for n in range(N_BR + 1, N_END):
                split_lo(n, n % 2)
            pool.wait_ge(post_here, 32)
            for t in range(4):
                pool.wait_ge(y_times_g, t + 1)
                for half in range(2):
                    c = slice(half * (D // 2), (half + 1) * (D // 2))
                    nc.gpsimd.tensor_tensor(y[:, t, c], y[:, t, c], post_b[:, c], ALU.add).then_inc(y_final, 1)

        @block.scalar
        def _(act):
            def split_hi(n, buf, landed, width=KC * P, first=False):
                act.wait_ge(raw_here[buf], landed)
                if not first:
                    act.wait_ge(block_used, n - 1)
                nc.scalar.activation(whi[:, buf, 0:width], raw[:, buf, 0:width], ACT.Copy).then_inc(hi_ready, 1)

            def tile_ps(b):
                return ps[:, 2 * b:2 * b + 2, 0:HALF]

            def pairs(a):
                return a.rearrange("p (h t) -> p h t", h=2)

            def flat(a, j):
                return pairs(a[:, j, :]) if isinstance(j, int) else \
                    a[:, ds(j, 1), :].rearrange("p a (h t) -> p (a h) t", h=2)

            def each_pair(n0, count, take):
                with act.Fori(0, count // 2) as i:
                    for b in range(2):
                        n = n0 + b
                        split_hi(n + 1 + i * 2, (n + 1) % 2, LANDED[n + 1] + i * 16)
                        act.wait_ge(block_used, n + 1 + i * 2)
                        take(i, b)

            for g in range(4 * TILES):
                t, q = g // 4, g % 4
                act.wait_ge(xT_out, g + 1)
                nc.scalar.activation(xhi[:, 4 * q:4 * q + 4, t * P:t * P + ROWS[t]],
                                     ps[:, turn_bank(g), :].rearrange("p (k t) -> p k t", k=4)[:, :, 0:ROWS[t]],
                                     ACT.Copy).then_inc(xhi_ready, 1)
                if g == 3:
                    split_hi(0, 0, LANDED[0], first=True)
                if g == 15:
                    split_hi(1, 1, LANDED[1], first=True)
            split_hi(2, 0, LANDED[2])
            split_hi(3, 1, LANDED[3])
            split_hi(4, 0, LANDED[4], KC * 80)
            for t in range(TILES):
                if t < 4:
                    act.wait_ge(kv_out, t + 1)
                else:
                    act.wait_ge(block_used, N_IK)
                nc.scalar.activation(kv[0:ROWS[t], t, :], ps[0:ROWS[t], t, :], ACT.Copy).then_inc(kv_ready, 1)
            act.wait_ge(kv_ready, TILES)
            act.sem_inc(tile_taken, 2)
            split_hi(5, 1, LANDED[5])
            act.wait_ge(block_used, N_IK + 1)
            nc.scalar.activation(pairs(ikiwT[:, :]), ps[0:80, 5:7, 0:HALF], ACT.Copy).then_inc(ikiwT_ready, 1)
            act.wait_ge(dw_out, 1)
            nc.scalar.activation(dwT[:, :, :], ps[:, 7, 0:8 * (CW + 3)].rearrange("p (j r) -> p j r", j=8), ACT.Copy
                                 ).then_inc(dwT_ready, 1)

            def take_iq(first):
                def take(i, b):
                    nc.scalar.activation(flat(iqT, i * 2 + b + first), tile_ps(b), ACT.Copy).then_inc(tile_taken, 1)
                return take

            each_pair(N_IQ, 2, take_iq(0))
            act.wait_ge(ikiw_out, 1)
            nc.scalar.activation(ikiw[:, 0:4, :], ps[:, 5, 0:320].rearrange("p (t c) -> p t c", t=4), ACT.Copy
                                 ).then_inc(ikiw_ready, 1)
            nc.scalar.activation(ikiw[0:ROWS[4], 4, :], ps[0:ROWS[4], 5, 320:400], ACT.Copy).then_inc(ikiw_ready, 1)

            each_pair(N_IQ + 2, 2, take_iq(2))
            act.wait_ge(ik_var, 1)
            nc.scalar.activation(rs, mv.rearrange("p (t c) -> p t c", c=2)[:, :, 1], ACT.Sqrt).then_inc(ik_std, 1)
            each_pair(N_IQ + 4, 4, take_iq(4))
            act.wait_ge(turned, 1)
            nc.scalar.activation(kT[:, :, 0:512], ps[:, 4:6, :], ACT.Copy).then_inc(turned_taken, 1)
            act.wait_ge(turned, 2)
            nc.scalar.activation(kT[:, :, 512:TOK], ps[:, 6, 0:160].rearrange("p (g t) -> p g t", g=2), ACT.Copy
                                 ).then_inc(turned_taken, 1)
            act.wait_ge(ikZ_clear, 1)
            act.wait_ge(turned, 3)
            nc.scalar.activation(ikZ[0:64, 0, 0:512], ps[0:64, 7, :], ACT.Copy)
            nc.scalar.activation(ikZ[64:128, 1, 0:512], ps[64:128, 7, :], ACT.Copy).then_inc(turned_taken, 1)
            act.wait_ge(turned, 4)
            nc.scalar.activation(ikZ[0:64, 0, 512:LP], ps[0:64, 2, 0:LAST], ACT.Copy)
            nc.scalar.activation(ikZ[64:128, 1, 512:LP], ps[64:128, 2, 0:LAST], ACT.Copy)
            nc.scalar.activation(ik_new[:, :], ps[:, 2, LAST:80], ACT.Copy).then_inc(turned_taken, 1)

            scale = (IDIM ** -0.5) * (IH ** -0.5)
            for u in range(HEAD_UNITS):
                n = (2 + u % 3) * P
                act.wait_ge(idx_out, u + 1)
                if u >= 4:
                    act.wait_ge(relu_used, u - 3)
                nc.scalar.activation(relus[:, u % 4, 0:n], ps[:, 4 + u % 4, 0:n], ACT.Relu, scale=scale
                                     ).then_inc(relu_ready, 1)
            act.wait_ge(relu_used, HEAD_UNITS)
            for v in range(2 + DB):
                n, o = (LP if v < 2 else LS), 2048 + 1024 * (v % 2)
                act.wait_ge(idx_out, HEAD_UNITS + v + 1)
                if v >= 2:
                    act.wait_ge(sums_out, v - 1)
                nc.scalar.activation(scores[:, v % 2, 0:n], ps_t[:, o:o + n], ACT.Relu, scale=scale
                                     ).then_inc(relu_ready, 1)
                if v < DB:
                    act.wait_ge(idx_turned, v + 1)
                    nc.scalar.activation(idx_kT[:, v % 2, :], ps[:, 2 + v % 2, :], ACT.Copy).then_inc(idx_kT_ready, 1)
            act.wait_ge(sums_out, 2 + DB)
            nc.scalar.activation(bias[0:ROWS[4], bias_at[4] + PAD:], ps_t[0:ROWS[4], 0:LP], ACT.Copy
                                 ).then_inc(last_scored, 1)

            def take_q(i, b):
                nc.scalar.activation(flat(qT, i * 2 + b), tile_ps(b), ACT.Copy, scale=DH ** -0.5
                                     ).then_inc(tile_taken, 1)

            act.wait_ge(idx_stored, 16 * 6)
            each_pair(N_Q, 8, take_q)
            act.wait_ge(relu_used, HEAD_UNITS)

            def take_gate(i, b):
                if i:
                    act.wait_ge(gate_stored[b], i * 16)
                nc.scalar.activation(pairs(tmp_gate[:, b, :]), tile_ps(b), ACT.Tanh, scale=0.5).then_inc(tile_taken, 1)
                act.wait_ge(tile_taken, N_GT - C_OF + b + 3 + i * 2)
                act.dma_start(gates[i * 2 + b], tmp_gate[:, b, :]).then_inc(gate_stored[b], 16)

            def before_pair(s):
                if 1 <= s <= GROUPS:
                    i, h0, nh = groups[s - 1]
                    if s >= 2:
                        act.wait_ge(o_out, s - 1)
                    for k in range(4):
                        act.wait_ge(pT_out, 4 * (s - 1) + k + 1)
                        if nh == 8:
                            src, dst = [a.rearrange("p (u t) -> p u t", u=2)[:, :, 0:(i + 1) * P]
                                        for a in (ps[:, 4 + k, :], pT[:, k, :])]
                        else:
                            src, dst = [a[:, 0:(i + 1) * P] for a in (ps[:, 4 + k, :], pT[:, k, :])]
                        nc.scalar.activation(dst, src, ACT.Copy).then_inc(pT_ready, 1)
                if s == O_LAST:
                    act.wait_ge(last_pT_out, 1)
                    nc.scalar.activation(pT[:, 0, :], ps[:, 5, :], ACT.Copy)
                    nc.scalar.activation(pT[0:LAST, 1, 0:P], ps[0:LAST, 6, 0:P], ACT.Copy).then_inc(last_pT_ready, 1)
                if s in O_NEW:
                    half = O_NEW.index(s)
                    for g in range(KVH):
                        act.wait_ge(s_pT_out, 2 * half + g + 1)
                        nc.scalar.activation(pT[:, g, :], ps[:, 4 + g, :], ACT.Copy)
                        nc.scalar.activation(pT_new[:, g, :], ps[0:DS, 6 + g, 0:P], ACT.Copy).then_inc(s_pT_ready, 1)

            def within_pair(s):
                if s in S_NEW:
                    for u in range(4 * S_NEW.index(s), 4 * S_NEW.index(s) + 4):
                        act.wait_ge(kTs_out, u + 1)
                        if u >= 2:
                            act.wait_ge(s_logits, u - 1)
                        nc.scalar.activation(kTs[:, u % 2, :], ps[:, 2 + u % 2, :], ACT.Copy).then_inc(kTs_ready, 1)

            def exps(s):
                if s < GROUPS:
                    n = (groups[s][0] + 1) * P
                    for j, (h, count, k, off) in enumerate(units(s)):
                        act.wait_ge(max_ready, count + 1)
                        nc.scalar.activation(probs[:, k, off:off + n], probs[:, k, off:off + n], ACT.Exp,
                                             bias=neg_max[:, j:j + 1], accum_out=exp_sum[:, j:j + 1]
                                             ).then_inc(exp_ready, 1)
                if s == S_LAST:
                    act.wait_ge(last_max, 1)
                    nc.scalar.activation(probs_last[:, :], probs_last[:, :], ACT.Exp, bias=neg_max[:, 0:1],
                                         accum_out=exp_sum[:, 0:1]).then_inc(last_exp, 1)
                if s in (S_NEW[1], S_NEW[3]):
                    half = S_NEW.index(s) // 2
                    for g in range(KVH):
                        act.wait_ge(s_max, 2 * half + g + 1)
                        nc.scalar.activation(scores_s[:, g, 0:LS], scores_s[:, g, 0:LS], ACT.Exp,
                                             bias=neg_max[:, g:g + 1], accum_out=exp_sum[:, g:g + 1]).then_inc(s_exp, 1)

            for s in range(PAIRS):
                before_pair(s)
                for b in range(2):
                    n = N_GT + 2 * s + b
                    if b == 1:
                        within_pair(s)
                    split_hi(n + 1, (n + 1) % 2, LANDED[n + 1])
                    if b == 1:
                        exps(s)
                    act.wait_ge(block_used, n + 1)
                    take_gate(s, b)
            before_pair(PAIRS)
            split_hi(N_ZA + 1, (N_ZA + 1) % 2, LANDED[N_ZA + 1])
            for t in gate_stored:
                act.wait_ge(t, 16 * PAIRS)
            act.wait_ge(s_o_out, 2)

            for j in range(8):
                n = N_ZA + j
                if j:
                    split_hi(n + 1, (n + 1) % 2, LANDED[n + 1])
                act.wait_ge(block_used, n + 1)
                if j >= 2:
                    act.wait_ge(za_used, j - 1)
                b = j % 2
                nc.scalar.activation(pairs(tmp_lin[:, b, :]), tile_ps(b), ACT.Copy, scale=0.5)
                nc.scalar.activation(pairs(tmp_tanh[:, b, :]), tile_ps(b), ACT.Tanh, scale=0.5).then_inc(tile_taken, 1)

            act.wait_ge(state_taken, 16)
            with act.Fori(0, 8) as i:
                for b in range(2):
                    n = N_CU + b
                    split_hi(n + 1 + i * 2, (n + 1) % 2, LANDED[n + 1] + i * 16)
                    act.wait_ge(block_used, n + 1 + i * 2)
                    if b == 0:
                        row = U[:, ds(i, 1), :].rearrange("p a w -> p (a w)")
                        nc.scalar.activation(row[:, TAIL:TAIL + HALF], ps[:, 0, 0:HALF], ACT.Copy, scale=0.5)
                        nc.scalar.activation(row[:, TAIL + HALF:EXT], ps[:, 1, 0:LP - HALF], ACT.Copy, scale=0.5)
                        nc.scalar.activation(sample_cols(U, i)[:, :, TAIL:],
                                             ps[:, 1, LP - HALF:HALF].rearrange("p (b t) -> p b t", b=DB),
                                             ACT.Copy, scale=0.5).then_inc(tile_taken, 1)
                    else:
                        nc.scalar.activation(flat(zc, i), tile_ps(1), ACT.Tanh, scale=0.5).then_inc(tile_taken, 1)

            def normed(j):
                act.wait_ge(n_ready, j + 1)
                if j >= 2:
                    act.wait_ge(c_ready, j - 1)
                b = j % 2
                nc.scalar.activation(tmp_lin[:, b, 0:LP], U[:, j, TAIL:EXT], ACT.Identity,
                                     scale=half_g[:, j:j + 1], bias=half_b[:, j:j + 1])
                nc.scalar.activation(tmp_lin[:, b, LP:TOK].rearrange("p (b t) -> p b t", b=DB),
                                     sample_cols(U, j)[:, :, TAIL:], ACT.Identity,
                                     scale=half_g[:, j:j + 1], bias=half_b[:, j:j + 1]).then_inc(lin_ready, 1)
                act.wait_ge(lin_ready, j + 1)
                nc.scalar.activation(U[:, j, 0:TOK], tmp_lin[:, b, :], ACT.Tanh).then_inc(tanh_ready, 1)

            for j in range(8):
                n = N_ZC + j
                split_hi(n + 1, (n + 1) % 2, LANDED[n + 1])
                act.wait_ge(block_used, n + 1)
                act.wait_ge(tailT_ready, j + 1)
                if j >= 2:
                    act.wait_ge(zc_done, j - 1)
                b = j % 2
                nc.scalar.activation(flat(zc, j), tile_ps(b), ACT.Copy, scale=0.5)
                nc.scalar.activation(pairs(tmp_tanh[:, b, :]), tile_ps(b), ACT.Tanh, scale=0.5).then_inc(tile_taken, 1)
                if j == 5:
                    act.wait_ge(tail_out, 1)
                    nc.scalar.activation(u_tail[0:TAIL + DB * DS, :].rearrange("p (h c) -> p h c", h=2),
                                         ps[0:TAIL + DB * DS, 4:6, :], ACT.Copy).then_inc(tail_ready, 1)
            def take_late_gate(j):
                b = j % 2
                nc.scalar.activation(pairs(tmp_tanh[:, b, :]), tile_ps(b), ACT.Tanh, scale=0.5).then_inc(tile_taken, 1)
                act.wait_ge(tile_taken, N_G2 + j - C_OF + 3)
                act.dma_start(gates[GT1 + j], tmp_tanh[:, b, :]).then_inc(gate_stored[b], 16)

            act.wait_ge(zc_done, 8)
            for j in range(N_BR - N_G2):
                n = N_G2 + j
                split_hi(n + 1, (n + 1) % 2, LANDED[n + 1])
                for k in {4: (0, 1, 2), 5: (3, 4, 5), 6: (6, 7)}.get(j, ()):
                    normed(k)
                act.wait_ge(block_used, n + 1)
                b = j % 2
                if j >= 2:
                    act.wait_ge(gate_stored[b], (GT1 + j) // 2 * 16)
                if j < N_BR - N_G2 - 1:
                    take_late_gate(j)
                if j == 3:
                    act.wait_ge(std_in, 1)
                    nc.scalar.activation(c_rstd[:, :], c_sum[:, :], ACT.Sqrt).then_inc(std_ready, 1)
                    act.wait_ge(tail_stored, 16 * (1 + DB))
            act.wait_ge(block_used, N_BR)
            for k in range(KC):
                if k == 4:
                    take_late_gate(N_BR - N_G2 - 1)
                if k == 10:
                    split_hi(N_BR + 1, (N_BR + 1) % 2, LANDED[N_BR + 1])
                if k >= 8:
                    act.wait_ge(c_ready, k - 7)
                nc.scalar.activation(xhi[:, k, :], qT[:, k, :] if k < 8 else zc[:, k - 8, :], ACT.Copy
                                     ).then_inc(xhi_ready, 1)

            for j in range(KC):
                n = N_BR + j
                if j:
                    split_hi(n + 1, (n + 1) % 2, LANDED[n + 1])
                act.wait_ge(m_ready, j + 1)
                nc.scalar.activation(mhi[:, j, :], m_tmp[:, j % 2, :], ACT.Copy).then_inc(mhi_ready, 1)
            for r in range(16):
                n = N_WO + r
                if n + 1 < N_END:
                    split_hi(n + 1, (n + 1) % 2, LANDED[n + 1])
                if r == 1:
                    act.wait_ge(y_here, 16 * 7)
                for t in {1: (0, 1), 2: (2, 3), 3: (4,)}.get(r, ()):
                    rows = ROWS[t]
                    nc.scalar.mul(y[0:rows, t, :], y[0:rows, t, :], ALPHA).then_inc(y_scaled, 1)
            for t in range(TILES):
                rows = ROWS[t]
                act.wait_ge(y_var, t + 1)
                nc.scalar.activation(y_rstd[0:rows, t:t + 1], ymv[0:rows, 1:2], ACT.Sqrt).then_inc(y_std, 1)
                act.wait_ge(y_norm_in, t + 1)
                nc.scalar.activation(y[0:rows, t, :], y[0:rows, t, :], ACT.Identity,
                                     scale=y_rstd[0:rows, t:t + 1], bias=y_shift[0:rows, t:t + 1]).then_inc(y_norm, 1)

        @block.vector
        def _(dve):
            steps = [0]

            def link(ins):
                steps[0] += 1
                ins.then_inc(dve_step, 1)
                dve.wait_ge(dve_step, steps[0])

            link(nc.vector.memset(ones[:, :], 1.0 / DC))
            link(nc.vector.memset(mv, 1.0))
            for g in range(4 * TILES):
                t, q = g // 4, g % 4
                dve.wait_ge(xhi_ready, g + 1)
                cols = slice(t * P, t * P + ROWS[t])
                nc.vector.tensor_tensor(xlo[:, 4 * q:4 * q + 4, cols],
                                        ps[:, turn_bank(g), :].rearrange("p (k t) -> p k t", k=4)[:, :, 0:ROWS[t]],
                                        xhi[:, 4 * q:4 * q + 4, cols].bitcast(F32), ALU.subtract
                                        ).then_inc(xlo_ready, 1)

            dve.wait_ge(ikiw_ready, 2)
            dve.wait_ge(dw_here, 16 * 6)
            for t in range(TILES):
                r = ROWS[t]
                link(nc.vector.bn_stats(st[0:r, 6 * t:6 * t + 6], ikiw[0:r, t, 0:IDIM]))
                link(nc.vector.bn_aggr(mv[0:r, 2 * t:2 * t + 2], st[0:r, 6 * t:6 * t + 6]))
            var = mv.rearrange("p (t c) -> p t c", c=2)[:, :, 1]
            nc.vector.tensor_scalar(var, var, EPS, None, ALU.add).then_inc(ik_var, 1)
            dve.wait_ge(ik_std, 1)
            link(nc.vector.reciprocal(rs, rs))
            for t in range(TILES):
                r = ROWS[t]
                a = ik_norm[0:r, t, 0, :]
                link(nc.vector.tensor_scalar(a, ikiw[0:r, t, 0:IDIM], mv[0:r, 2 * t:2 * t + 1], rs[0:r, t:t + 1],
                                             ALU.subtract, ALU.mult))
                link(nc.vector.tensor_tensor(a, a, idx_gb[0:r, 0, :], ALU.mult))
                link(nc.vector.tensor_tensor(a, a, idx_gb[0:r, 1, :], ALU.add))
                nc.vector.tensor_copy(ik_norm[0:r, t, 1, :], a).then_inc(ik_ready, 1)

            dve.wait_ge(dw_out, 1)
            link(nc.vector.memset(ikZ[64:128, 0, :], 0.0))
            nc.vector.memset(ikZ[0:64, 1, :], 0.0).then_inc(ikZ_clear, 1)
            link(nc.vector.memset(w_sel[:, :, :], 0.0))
            link(nc.vector.memset(w_last[:, :, :], 0.0))
            link(nc.vector.memset(iq_new[:, :, :, :], 0.0))
            dve.wait_ge(wcol_here, 16 * (IH + IH // 2))
            for b in range(DB):
                nc.vector.tensor_scalar(w_sel[:, b, LAST + DS * b:LAST + DS * b + DS], cst[:, C_DIV:C_DIV + DS],
                                        wcol[:, b:b + 1], None, ALU.mult).then_inc(wsel_ready, 1)
            for par in range(2):
                nc.vector.tensor_scalar(w_last[:, par, 0:LAST], cst[:, C_DIV2:C_DIV2 + LAST],
                                        wcol_last[:, par:par + 1], None, ALU.mult).then_inc(wsel_ready, 1)

            def sc(i):
                rows = P if i < 4 else ROWS[4]
                return bias[0:rows, bias_at[i]:bias_at[i] + bias_w[i]]

            def gather(j):
                nc.vector.tensor_copy(iq_last[:, LAST * j:LAST * (j + 1)], iqT[:, j, 4 * P:LP])
                for par in range(2):
                    half = slice(64 * par, 64 * par + 64)
                    ins = nc.vector.tensor_copy(iq_new[half, :, par, DS * j:DS * j + DS],
                                                iqT[half, j, LP:TOK].rearrange("p (b t) -> p b t", b=DB))
                ins.then_inc(iq_new_ready, 1)

            dve.wait_ge(tile_taken, 8 + 2)
            for u in range(HEAD_UNITS):
                h, i = u // 3, 1 + u % 3
                src = relus[:, u % 4, 0:(i + 1) * P]
                w = ikiw[:, i, IDIM + h:IDIM + h + 1]
                dve.wait_ge(relu_ready, u + 1)
                if h == 0:
                    nc.vector.tensor_scalar(sc(i), src, w, None, ALU.mult).then_inc(relu_used, 1)
                else:
                    dve.wait_ge(relu_used, u - 2)
                    nc.vector.scalar_tensor_tensor(sc(i), src, w, sc(i), ALU.mult, ALU.add).then_inc(relu_used, 1)
                if u % 3 == 2 and 4 <= h < 4 + IH // 2:
                    gather(h - 4)
            dve.wait_ge(relu_used, HEAD_UNITS)
            for i in range(1, 4):
                link(nc.vector.tensor_tensor(sc(i)[:, i * P:(i + 1) * P], sc(i)[:, i * P:(i + 1) * P],
                                             cst[:, C_TRI:C_TRI + P], ALU.add))
            link(nc.vector.tensor_copy(sc(4)[:, 0:PAD], cst[0:ROWS[4], C_PAD:C_PAD + PAD]))

            done = 0
            for i, rounds in ((1, TOP_P // 8), (2, TOP_P // 8), (3, TOP_P // 8), (4, (TOP_S + 6) // 8)):
                rows = P if i < 4 else ROWS[4]
                if i == 4:
                    dve.wait_ge(last_scored, 1)
                    link(nc.vector.tensor_tensor(sc(4)[:, PAD + 4 * P:], sc(4)[:, PAD + 4 * P:],
                                                 cst[0:ROWS[4], C_NEW:C_NEW + META], ALU.add))
                with dve.Fori(0, rounds) as r:
                    nc.vector.max(top8[0:rows, :], sc(i)).then_inc(topk_step, 1)
                    dve.wait_ge(topk_step, done + 1 + r * 2)
                    nc.vector.memset(wait_carrier, 0.0)
                    nc.vector.match_replace(sc(i), top8[0:rows, :], sc(i), TAKEN).then_inc(topk_step, 1)
                    dve.wait_ge(topk_step, done + 2 + r * 2)
                done += 2 * rounds

            dve.wait_ge(consts2_here, 32)
            for i in range(1, 5):
                rows = P if i < 4 else ROWS[4]
                s = sc(i) if i < 4 else sc(4)[:, PAD:]
                n = bias_w[i] if i < 4 else LP
                link(nc.vector.tensor_scalar(s, s, BETWEEN, FAR, ALU.is_ge, ALU.mult))
                dist = dist_c[0:rows, 0:n] if i < 4 else dist_c[0:rows, LP:LP + n]
                nc.vector.scalar_tensor_tensor(s, dist, float(-i * P) if i < 4 else 0.0, s, ALU.add, ALU.add
                                               ).then_inc(bias_ready, 1)
            link(nc.vector.tensor_scalar(sc(0), cst[:, C_TRI:C_TRI + P], 1e-6, None, ALU.mult))
            nc.vector.tensor_tensor(sc(0), sc(0), dist_c[:, 0:P], ALU.add).then_inc(bias_ready, 1)
            dve.wait_ge(bias_ready, TILES)
            dve.wait_ge(tile_taken, N_GT - C_OF + 2)
            dve.wait_ge(dwT_ready, 1)
            nc.vector.tensor_copy(q_last[:, :].rearrange("p (h t) -> p h t", h=HEADS), qT[:, :, 4 * P:LP]
                                  ).then_inc(q_last_ready, 1)
            for s in range(GROUPS + 1):
                if s >= 1:
                    i, h0, nh = groups[s - 1]
                    dve.wait_ge(o_out, s)
                    nc.vector.tensor_copy(qT[:, h0:h0 + nh, i * P:(i + 1) * P],
                                          ps_t[:, 4 * 512:4 * 512 + nh * P].rearrange("p (r t) -> p r t", r=nh)
                                          ).then_inc(o_taken, 1)
                if s == GROUPS:
                    break
                i = groups[s][0]
                n = (i + 1) * P
                for j, (h, count, k, off) in enumerate(units(s)):
                    t = probs[:, k, off:off + n]
                    dve.wait_ge(logits_out, 4 * s + k + 1)
                    link(nc.vector.scalar_tensor_tensor(t, sc(i)[:, 0:n], 2.0 ** -(h + 1.0),
                                                        ps[:, 4 + (k + 2) % 4, off:off + n], ALU.mult, ALU.add))
                    nc.vector.tensor_reduce(neg_max[:, j:j + 1], t, AX_X, ALU.max, negate=True).then_inc(max_ready, 1)
                for j, (h, count, k, off) in enumerate(units(s)):
                    t = probs[:, k, off:off + n]
                    dve.wait_ge(exp_ready, count + 1)
                    link(nc.vector.reciprocal(inv_sum[:, j:j + 1], exp_sum[:, j:j + 1]))
                    nc.vector.tensor_scalar(t, t, inv_sum[:, j:j + 1], None, ALU.mult).then_inc(probs_ready, 1)
            dve.wait_ge(last_logits, 1)
            nc.vector.tensor_copy(bias_s[:, 0:512], ps[:, 7, :])
            link(nc.vector.tensor_copy(bias_s[:, 512:LP], ps[:, 6, 64:64 + LAST]))
            link(nc.vector.scalar_tensor_tensor(probs_last[:, :], bias_s[:, :],
                                                cst[:, C_SLOPE + KVH:C_SLOPE + KVH + 1],
                                                ps_t[:, 5 * 512:5 * 512 + LP], ALU.mult, ALU.add))
            nc.vector.tensor_reduce(neg_max[:, 0:1], probs_last[:, :], AX_X, ALU.max, negate=True
                                    ).then_inc(last_max, 1)
            dve.wait_ge(last_exp, 1)
            link(nc.vector.reciprocal(inv_sum[:, 0:1], exp_sum[:, 0:1]))
            nc.vector.tensor_scalar(probs_last[:, :], probs_last[:, :], inv_sum[:, 0:1], None, ALU.mult
                                    ).then_inc(last_probs, 1)
            dve.wait_ge(last_o_out, 1)
            nc.vector.tensor_copy(qT[:, :, 4 * P:LP], ps[:, 7, 0:P].rearrange("p (h t) -> p h t", h=HEADS)
                                  ).then_inc(last_o_taken, 1)

            for h in range(HEADS):
                r = h % GROUP
                nc.vector.tensor_copy(q_new[:, h // GROUP, :, DS * r:DS * r + DS],
                                      qT[:, h, LP:TOK].rearrange("p (b t) -> p b t", b=DB)).then_inc(q_new_ready, 1)
            def rows_taken(half):
                dve.wait_ge(s_o_out, half + 1)
                nc.vector.tensor_copy(o_rows[:, :], ps[:, 7, 0:KVH * DH]).then_inc(s_o_rows, 1)

            def outputs_taken(half):
                dve.wait_ge(s_o_turned, half + 1)
                for g in range(KVH):
                    at0 = LP + 32 * half
                    link(nc.vector.tensor_copy(
                        qT[:, 4 * g:4 * g + 4, at0:at0 + 32].rearrange("p r (b t) -> p r b t", b=4),
                        ps[:, 7, g * P:(g + 1) * P].rearrange("p (b r t) -> p r b t", b=4, r=4)))
                dve.sem_inc(s_o_taken, 1)

            for half in range(2):
                dve.wait_ge(rep_out, half + 1)
                nc.vector.tensor_copy(bias_s[:, 0:PAST], ps[:, 7, :])
                nc.vector.tensor_copy(bias_s[:, PAST:LS], ps[:, 6, 64:64 + DS]).then_inc(rep_taken, 1)
                dve.wait_ge(rep_taken, half + 1)
                if half:
                    outputs_taken(0)
                dve.wait_ge(s_logits, 8 * half + 8)
                for g in range(KVH):
                    slope = cst[:, C_SLOPE + g:C_SLOPE + g + 1]
                    nc.vector.scalar_tensor_tensor(scores_s[:, g, 0:PAST], bias_s[:, 0:PAST], slope,
                                                   ps[:, 4 + g, :], ALU.mult, ALU.add)
                    link(nc.vector.scalar_tensor_tensor(scores_s[:, g, PAST:LS], bias_s[:, PAST:LS], slope,
                                                        ps[:, 6, DS * g:DS * g + DS], ALU.mult, ALU.add))
                    nc.vector.tensor_reduce(neg_max[:, g:g + 1], scores_s[:, g, 0:LS], AX_X, ALU.max, negate=True
                                            ).then_inc(s_max, 1)
                for g in range(KVH):
                    t = scores_s[:, g, 0:LS]
                    dve.wait_ge(s_exp, 2 * half + g + 1)
                    link(nc.vector.reciprocal(inv_sum[:, g:g + 1], exp_sum[:, g:g + 1]))
                    nc.vector.tensor_scalar(t, t, inv_sum[:, g:g + 1], None, ALU.mult).then_inc(s_probs, 1)
                rows_taken(half)
            outputs_taken(1)

            for c in range(16):
                j, part = c // 2, c % 2
                dve.wait_ge(state_out, c + 1)
                if c == 0:
                    link(nc.vector.memset(U[:, :, 0:TAIL], 0.0))
                nc.vector.tensor_copy(sample_cols(U, j)[:, 4 * part:4 * part + 4, 0:TAIL],
                                      ps[:, 4 + c % 4, 0:4 * TAIL].rearrange("p (b t) -> p b t", b=4)
                                      ).then_inc(state_taken, 1)
            link(nc.vector.tensor_scalar(half_g, dwT[:, :, CW + 1], 0.5, None, ALU.mult))
            link(nc.vector.tensor_scalar(half_b, dwT[:, :, CW + 2], 0.5, None, ALU.mult))

            TAPS = 4
            PER = TAPS + 2 * CW
            with dve.Fori(0, 8) as j:
                row = U[:, ds(j, 1), :].rearrange("p a w -> p (a w)")
                new = sample_cols(U, j)
                t = zc[:, ds(j, 1), :].rearrange("p a w -> p (a w)")
                accs = c_acc[:, LP:TOK].rearrange("p (b t) -> p b t", b=DB)
                tail = tailT[:, ds(j, 1), :].rearrange("p a w -> p (a w)")
                dve.wait_ge(tile_taken, N_CU + 2 - C_OF + 2 + j * 2)
                nc.vector.scalar_tensor_tensor(row[:, TAIL:EXT], t[:, 0:LP], 1.0, row[:, TAIL:EXT], ALU.add, ALU.mult
                                               ).then_inc(conv_step, 1)
                nc.vector.scalar_tensor_tensor(new[:, :, TAIL:], t[:, LP:TOK].rearrange("p (b t) -> p b t", b=DB),
                                               1.0, new[:, :, TAIL:], ALU.add, ALU.mult).then_inc(conv_step, 1)
                dve.wait_ge(conv_step, 2 + j * PER)
                nc.vector.tensor_copy(tail[:, 0:TAIL], row[:, EXT - TAIL:EXT]).then_inc(conv_step, 1)
                nc.vector.tensor_copy(tail[:, TAIL:].rearrange("p (b t) -> p b t", b=DB), new[:, :, TAIL:]
                                      ).then_inc(conv_step, 1)
                dve.wait_ge(conv_step, TAPS + j * PER)
                dve.sem_inc(tailT_ready, 1)
                for k in range(CW):
                    w = dwT[:, ds(j, 1), k:k + 1].rearrange("p a k -> p (a k)")
                    out_p = c_acc[:, 0:LP] if k < CW - 1 else row[:, TAIL:EXT]
                    out_s = accs if k < CW - 1 else new[:, :, TAIL:]
                    if k == 0:
                        bd = dwT[:, ds(j, 1), CW:CW + 1].rearrange("p a k -> p (a k)")
                        nc.vector.tensor_scalar(out_p, row[:, 0:LP], w, bd, ALU.mult, ALU.add).then_inc(conv_step, 1)
                        nc.vector.tensor_scalar(out_s, new[:, :, 0:DS], w, bd, ALU.mult, ALU.add
                                                ).then_inc(conv_step, 1)
                    else:
                        dve.wait_ge(conv_step, TAPS + 2 * k - 1 + j * PER)
                        nc.vector.scalar_tensor_tensor(out_p, row[:, k:k + LP], w, c_acc[:, 0:LP], ALU.mult, ALU.add
                                                       ).then_inc(conv_step, 1)
                        dve.wait_ge(conv_step, TAPS + 2 * k + j * PER)
                        nc.vector.scalar_tensor_tensor(out_s, new[:, :, k:k + DS], w, accs, ALU.mult, ALU.add
                                                       ).then_inc(conv_step, 1)
                dve.wait_ge(conv_step, PER + j * PER)
                dve.sem_inc(conv_done, 1)

            def dev(j):
                row = U[:, j, :]
                link(nc.vector.tensor_tensor(row[:, TAIL:TAIL + HALF], row[:, TAIL:TAIL + HALF], ps[:, 6, 0:HALF],
                                             ALU.subtract))
                link(nc.vector.tensor_tensor(row[:, TAIL + HALF:EXT], row[:, TAIL + HALF:EXT],
                                             ps[:, 7, 0:LP - HALF], ALU.subtract))
                link(nc.vector.tensor_tensor(sample_cols(U, j)[:, :, TAIL:], sample_cols(U, j)[:, :, TAIL:],
                                             ps[:, 7, LP - HALF:HALF].rearrange("p (b t) -> p b t", b=DB),
                                             ALU.subtract))

            def branch_input(j):
                dve.wait_ge(tanh_ready, j + 1)
                link(nc.vector.scalar_tensor_tensor(U[:, j, 0:TOK], U[:, j, 0:TOK], 1.0, tmp_lin[:, j % 2, :],
                                                    ALU.add, ALU.mult))
                dve.wait_ge(zc_done, j + 1)
                nc.vector.tensor_tensor(zc[:, j, :], zc[:, j, :], U[:, j, 0:TOK], ALU.mult).then_inc(c_ready, 1)

            dve.wait_ge(mean_out, 1)
            for j in range(8):
                row, new = U[:, j, :], sample_cols(U, j)[:, :, TAIL:]
                dev(j)
                accs = c_acc[:, LP:TOK].rearrange("p (b t) -> p b t", b=DB)
                dst, dsts = (c_sum, c_sum[:, LP:TOK].rearrange("p (b t) -> p b t", b=DB)) if j == 0 else (c_acc, accs)
                link(nc.vector.tensor_tensor(dst[:, 0:LP], row[:, TAIL:EXT], row[:, TAIL:EXT], ALU.mult))
                link(nc.vector.tensor_tensor(dsts, new, new, ALU.mult))
                if j:
                    link(nc.vector.tensor_tensor(c_sum[:, :], c_sum[:, :], c_acc[:, :], ALU.add))
            dve.sem_inc(sq_ready, 1)
            dve.wait_ge(var_out, 1)
            nc.vector.tensor_scalar(c_sum[:, :].rearrange("p (h t) -> p h t", h=2), ps[:, 4:6, 0:HALF], EPS, None,
                                    ALU.add).then_inc(std_in, 1)
            dve.wait_ge(std_ready, 1)
            link(nc.vector.reciprocal(c_rstd[:, :], c_rstd[:, :]))
            for j in range(8):
                row, new = U[:, j, :], sample_cols(U, j)[:, :, TAIL:]
                link(nc.vector.tensor_tensor(row[:, TAIL:EXT], row[:, TAIL:EXT], c_rstd[:, 0:LP], ALU.mult))
                nc.vector.tensor_tensor(new, new, c_rstd[:, LP:TOK].rearrange("p (b t) -> p b t", b=DB), ALU.mult
                                        ).then_inc(n_ready, 1)
                if j >= 1:
                    branch_input(j - 1)
            branch_input(7)
            for k in range(KC):
                dve.wait_ge(xhi_ready, 4 * TILES + k + 1)
                src = qT[:, k, :] if k < 8 else zc[:, k - 8, :]
                nc.vector.tensor_tensor(xlo[:, k, :], src, xhi[:, k, :].bitcast(F32), ALU.subtract
                                        ).then_inc(xlo_ready, 1)

            def low_mixed(j):
                dve.wait_ge(mhi_ready, j + 1)
                nc.vector.tensor_tensor(mlo[:, j, :], m_tmp[:, j % 2, :], mhi[:, j, :].bitcast(F32), ALU.subtract
                                        ).then_inc(mlo_ready, 1)

            for j in range(KC):
                o = 4 * ((j + 1) % 2)
                dve.wait_ge(gate_here[j // 2], 32)
                dve.wait_ge(block_used, N_BR + j + 1)
                for c, g in ((0, gate0), (1, gate1)):
                    gv = g[:, j, :].rearrange("p (h t) -> p h t", h=2)
                    ins = nc.vector.scalar_tensor_tensor(gv, gv, 1.0, ps[:, o + 2 * c:o + 2 * c + 2, 0:HALF],
                                                         ALU.add, ALU.mult)
                    link(ins)
                dve.sem_inc(br_taken, 1)
                nc.vector.tensor_tensor(m_tmp[:, j % 2, :], gate0[:, j, :], gate1[:, j, :], ALU.add
                                        ).then_inc(m_ready, 1)
                low_mixed(j)
                if j == KC - 2:
                    dve.sem_inc(y_taken, 4)
            dve.sem_inc(y_taken, 1)

            def scaled(t):
                r = ROWS[t]
                dve.wait_ge(y_norm, t + 1)
                dve.wait_ge(post_here, 32)
                nc.vector.tensor_tensor(y[0:r, t, :], y[0:r, t, :], post_g[0:r, :], ALU.mult).then_inc(y_times_g, 1)

            for n in range(4):
                for t in range(TILES):
                    r = ROWS[t]
                    if n == 0:
                        dve.wait_ge(y_scaled, t + 1)
                    if t < 4:
                        dve.wait_ge(y_out, 4 * n + t + 1)
                    else:
                        dve.wait_ge(block_used, N_WO + 4 * n + 4)
                    dst = y[0:r, t, 512 * n:512 * n + 512]
                    nc.vector.scalar_tensor_tensor(dst, ps[0:r, (Y_BANK + t) % 8, :], 0.5, dst, ALU.mult, ALU.add
                                                   ).then_inc(y_taken, 1)
                    dve.wait_ge(y_taken, TILES * (n + 1) + t + 1)
                    link(nc.vector.bn_stats(yst[0:r, t, 6 * n:6 * n + 6], dst))
                    if n == 3:
                        if t:
                            dve.wait_ge(y_norm, t)
                        link(nc.vector.bn_aggr(ymv[0:r, :], yst[0:r, t, :]))
                        nc.vector.tensor_scalar(ymv[0:r, 1:2], ymv[0:r, 1:2], EPS, None, ALU.add).then_inc(y_var, 1)
                        dve.wait_ge(y_std, t + 1)
                        link(nc.vector.reciprocal(y_rstd[0:r, t:t + 1], y_rstd[0:r, t:t + 1]))
                        nc.vector.scalar_tensor_tensor(y_shift[0:r, t:t + 1], ymv[0:r, 0:1], -1.0,
                                                       y_rstd[0:r, t:t + 1], ALU.mult, ALU.mult
                                                       ).then_inc(y_norm_in, 1)
                        if t >= 1:
                            scaled(t - 1)
            scaled(TILES - 1)
            r = ROWS[4]
            dve.wait_ge(y_times_g, TILES)
            for half in range(2):
                c = slice(half * (D // 2), (half + 1) * (D // 2))
                nc.vector.tensor_tensor(y[0:r, 4, c], y[0:r, 4, c], post_b[0:r, c], ALU.add).then_inc(y_final_last, 1)

        @block.tensor
        def _(pe):
            mm = nc.tensor.matmul

            def block_ready(n):
                pe.wait_ge(lo_ready, n + 1)

            def rows_block(n, buf, act_hi, act_lo, k0, first, last, out_sem, empty=None, ready=True,
                           some=range(TILES), bank=0):
                if ready:
                    block_ready(n)
                w = [t[:, buf, :].rearrange("p (k c) -> p k c", k=4) for t in (whi, wlo)]
                for t in some:
                    r = ROWS[t]
                    cols = slice(t * P, t * P + r)
                    if empty is not None:
                        pe.wait_ge(y_taken, empty + t + 1)
                    for k in range(4):
                        for m, (a, b) in enumerate(((act_hi, 0), (act_lo, 0), (act_hi, 1))):
                            ins = mm(ps[0:r, (bank + t) % 8, :], a[:, k0 + k, cols], w[b][:, k, :],
                                     start=(first and k == 0 and m == 0), stop=(last and k == 3 and m == 2))
                    if t == TILES - 1:
                        ins.then_inc(block_used, 1)
                    elif last:
                        ins.then_inc(out_sem, 1)

            def tile_block(buf, bank, k0=0, kn=KC):
                w = [t[:, buf, :].rearrange("p (k c) -> p k c", k=KC) for t in (whi, wlo)]
                for k in range(k0, k0 + kn):
                    for m, (b, x) in enumerate(((0, xhi), (0, xlo), (1, xhi))):
                        for half in range(2):
                            ins = mm(ps[:, bank + half, 0:HALF], w[b][:, k, :],
                                     x[:, k, half * HALF:(half + 1) * HALF],
                                     start=(k == k0 and m == 0), stop=(k == k0 + kn - 1 and m == 2))
                return ins

            def one_tile(n0, b, i=0):
                n = n0 + b
                block_ready(n + i * 2)
                pe.wait_ge(tile_taken, n - C_OF + 1 + i * 2)
                tile_block(n % 2, 2 * b).then_inc(block_used, 1)

            def tile_pair(n0, i):
                for b in range(2):
                    one_tile(n0, b, i)

            def tiles(n0, count):
                turns = count // 4
                if turns:
                    with pe.Fori(0, turns) as i:
                        tile_pair(n0, i * 2)
                        tile_pair(n0 + 2, i * 2)
                if count % 4:
                    tile_pair(n0 + 4 * turns, 0)

            def turn_tokens(t, quarters=range(4)):
                pe.wait_ge(x_here[t], 32 if t in (0, 4) else 16)
                r = ROWS[t]
                for q in quarters:
                    g = 4 * t + q
                    if g >= 8:
                        pe.wait_ge(xlo_ready, max(g - 2, 8))
                    for k in range(4):
                        ins = nc.tensor.transpose(ps[:, turn_bank(g), k * P:k * P + r],
                                                  xn[0:r, t, (4 * q + k) * P:(4 * q + k + 1) * P],
                                                  cst[0:r, C_ID:C_ID + r])
                    ins.then_inc(xT_out, 1)

            def kv_tiles(n, some):
                block_ready(n)
                for t in some:
                    pe.wait_ge(xlo_ready, 4 * t + 4)
                    rows_block(n, n % 2, xhi, xlo, 4 * n, n == 0, n == 3, kv_out, ready=False, some=(t,))

            pe.wait_ge(consts_here, 16)
            for t in range(3):
                turn_tokens(t)
            kv_tiles(0, (0,))
            turn_tokens(3, (0, 1, 2))
            kv_tiles(0, (1,))
            turn_tokens(3, (3,))
            turn_tokens(4, (0, 1))
            kv_tiles(0, (2,))
            turn_tokens(4, (2, 3))
            kv_tiles(0, (3, 4))
            for n in range(1, 4):
                kv_tiles(n, range(TILES))
            block_ready(N_IK)
            w = [t[:, 0, 0:KC * 80].rearrange("p (k c) -> p k c", k=KC) for t in (whi, wlo)]
            for k in range(KC):
                for m, (b, x) in enumerate(((0, xhi), (0, xlo), (1, xhi))):
                    for half in range(2):
                        ins = mm(ps[0:80, 5 + half, 0:HALF], w[b][:, k, :], x[:, k, half * HALF:(half + 1) * HALF],
                                 start=(k == 0 and m == 0), stop=(k == KC - 1 and m == 2))
            ins.then_inc(block_used, 1)
            pe.wait_ge(dw_here, 16 * 6)
            for j in range(8):
                ins = nc.tensor.transpose(ps[:, 7, j * (CW + 3):(j + 1) * (CW + 3)], dw_rows[:, j * P:(j + 1) * P],
                                          cst[0:CW + 3, C_ID:C_ID + CW + 3])
            ins.then_inc(dw_out, 1)
            tile_pair(N_IQ, 0)
            pe.wait_ge(ikiwT_ready, 1)
            for t in range(TILES):
                ins = nc.tensor.transpose(ps[0:ROWS[t], 5, 80 * t:80 * t + 80], ikiwT[:, t * P:t * P + ROWS[t]],
                                          cst[0:80, C_ID:C_ID + 80])
            ins.then_inc(ikiw_out, 1)
            tiles(N_IQ + 2, 6)
            pe.wait_ge(tile_taken, 8 + 2)
            pe.wait_ge(kv_ready, TILES)
            pe.wait_ge(ikiw_ready, 2)
            for g in range(2):
                for t in range(4):
                    ins = nc.tensor.transpose(ps[:, 4 + g, t * P:t * P + P], kv[:, t, g * P:g * P + P], ident)
            ins.then_inc(turned, 1)
            r = ROWS[4]
            for g in range(2):
                ins = nc.tensor.transpose(ps[:, 6, 80 * g:80 * g + 80], kv[0:r, 4, g * P:g * P + P],
                                          cst[0:r, C_ID:C_ID + r])
            ins.then_inc(turned, 1)
            pe.wait_ge(ik_ready, TILES)
            for t in range(4):
                ins = nc.tensor.transpose(ps[:, 7, t * P:t * P + P],
                                          ik_norm[:, t, :, :].rearrange("p c d -> p (c d)"), ident)
            ins.then_inc(turned, 1)
            nc.tensor.transpose(ps[:, 2, 0:80], ik_norm[0:r, 4, :, :].rearrange("p c d -> p (c d)"),
                                cst[0:r, C_ID:C_ID + r]).then_inc(turned, 1)
            pe.wait_ge(turned_taken, 4)

            for u in range(HEAD_UNITS):
                h, i = u // 3, 1 + u % 3
                n = (i + 1) * P
                if u >= 4:
                    pe.wait_ge(relu_ready, u - 3)
                mm(ps[:, 4 + u % 4, 0:n], iqT[:, h // 2, i * P:(i + 1) * P], ikZ[:, h % 2, 0:n], start=True, stop=True
                   ).then_inc(idx_out, 1)

            def turn_idx(b):
                pe.wait_ge(idx_here[b % 4], 16 * PAGES * (b // 4 + 1))
                if b >= 2:
                    pe.wait_ge(idx_kT_ready, b - 1)
                for n in range(PAGES):
                    ins = nc.tensor.transpose(ps[:, 2 + b % 2, n * P:n * P + P],
                                              idx_page[:, b % 4, n, :, :].rearrange("p c d -> p (c d)"), ident)
                ins.then_inc(idx_turned, 1)

            def idx_products(v):
                o = 2048 + 1024 * (v % 2)
                pe.wait_ge(relu_ready, HEAD_UNITS if v < 2 else HEAD_UNITS + v - 1)
                if v < 2:
                    mm(ps_t[:, o:o + 512], iq_last[:, :], ikZ[:, v, 0:512], start=True, stop=True)
                    ins = mm(ps_t[:, o + 512:o + LP], iq_last[:, :], ikZ[:, v, 512:LP], start=True, stop=True)
                else:
                    b = v - 2
                    pe.wait_ge(idx_kT_ready, b + 1)
                    lhs = iq_new[:, b, :, :].rearrange("p c t -> p (c t)")
                    mm(ps_t[:, o:o + PAST], lhs, idx_kT[:, b % 2, :], start=True, stop=True)
                    ins = mm(ps_t[:, o + PAST:o + LS], lhs, ik_new[:, DS * b:DS * b + DS], start=True, stop=True)
                ins.then_inc(idx_out, 1)

            pe.wait_ge(wsel_ready, DB + 2)
            pe.wait_ge(iq_new_ready, IH // 2)
            idx_products(0)
            for v in range(2 + DB):
                if v < DB:
                    turn_idx(v)
                if v + 1 < 2 + DB:
                    idx_products(v + 1)
                pe.wait_ge(relu_ready, HEAD_UNITS + v + 1)
                w = w_last[:, v, :] if v < 2 else w_sel[:, v - 2, :]
                n = LP if v < 2 else LS
                mm(ps[0:ROWS[4], 0, :], w, scores[:, v % 2, 0:512], start=(v == 0), stop=(v == 1 + DB))
                mm(ps[0:ROWS[4], 1, 0:n - 512], w, scores[:, v % 2, 512:n], start=(v == 0), stop=(v == 1 + DB)
                   ).then_inc(sums_out, 1)
            pe.wait_ge(last_scored, 1)

            tiles(N_Q, 8)

            def logits_new(b, g):
                u, rows, at0 = 2 * b + g, slice(32 * (b % 4), 32 * (b % 4) + 32), LP + DS * b
                pe.wait_ge(kTs_ready, u + 1)
                mm(ps[rows, 4 + g, :], q_new[:, g, b, :], kTs[:, u % 2, :], start=True, stop=True)
                mm(ps[rows, 6, DS * g:DS * g + DS], q_new[:, g, b, :], kT[:, g, at0:at0 + DS], start=True, stop=True
                   ).then_inc(s_logits, 1)

            def turn_keys(b, g):
                for n in range(PAGES):
                    ins = nc.tensor.transpose(ps[:, 2 + g, n * P:n * P + P],
                                              kpage[:, b % 2, n, g * DH:(g + 1) * DH], ident)
                ins.then_inc(kTs_out, 1)

            def before_pair(s):
                if 1 <= s <= GROUPS:
                    i, h0, nh = groups[s - 1]
                    pe.wait_ge(probs_ready, units(s - 1)[-1][1] + 1)
                    for j, (h, count, k, off) in enumerate(units(s - 1)):
                        for c in range(i + 1):
                            ins = nc.tensor.transpose(ps[:, 4 + k, off + c * P:off + (c + 1) * P],
                                                      probs[:, k, off + c * P:off + (c + 1) * P], ident)
                        if (j + 1) % (nh // 4) == 0:
                            ins.then_inc(pT_out, 1)
                if s == O_LAST:
                    pe.wait_ge(last_probs, 1)
                    for c in range(4):
                        nc.tensor.transpose(ps[:, 5, c * P:(c + 1) * P], probs_last[:, c * P:(c + 1) * P], ident)
                    nc.tensor.transpose(ps[0:LAST, 6, 0:P], probs_last[:, 4 * P:LP], ident).then_inc(last_pT_out, 1)
                if s in O_NEW:
                    half = O_NEW.index(s)
                    pe.wait_ge(s_probs, 2 * half + 2)
                    for g in range(KVH):
                        for n in range(PAGES):
                            nc.tensor.transpose(ps[:, 4 + g, n * P:n * P + P], scores_s[:, g, n * P:n * P + P], ident)
                        nc.tensor.transpose(ps[0:DS, 6 + g, 0:P], scores_s[:, g, PAST:LS], ident).then_inc(s_pT_out, 1)

            def within_pair(s):
                if 1 <= s <= GROUPS:
                    i, h0, nh = groups[s - 1]
                    for j, (h, count, k, off) in enumerate(units(s - 1)):
                        pe.wait_ge(pT_ready, 4 * (s - 1) + k + 1)
                        g0 = KVH * DH + h // GROUP * DH
                        for c in range(i + 1):
                            ins = mm(ps[:, 4 + j // 4, (j % 4) * P:(j % 4 + 1) * P], kv[:, c, g0:g0 + DH],
                                     pT[:, k, off + c * P:off + (c + 1) * P], start=(c == 0), stop=(c == i))
                    ins.then_inc(o_out, 1)
                if s < GROUPS:
                    i = groups[s][0]
                    for j, (h, count, k, off) in enumerate(units(s)):
                        if s and k == 2:
                            pe.wait_ge(o_taken, s)
                        ins = mm(ps[:, 4 + (k + 2) % 4, off:off + (i + 1) * P], qT[:, h, i * P:(i + 1) * P],
                                 kT[:, h // GROUP, 0:(i + 1) * P], start=True, stop=True)
                        if (j + 1) % (groups[s][2] // 4) == 0:
                            ins.then_inc(logits_out, 1)
                if s == S_LAST:
                    pe.wait_ge(q_last_ready, 1)
                    pe.wait_ge(o_taken, GROUPS)
                    for g in range(KVH):
                        rows = slice(64 * g, 64 * g + 64)
                        mm(ps[rows, 5, :], q_last[:, rows], kT[:, g, 0:512], start=True, stop=True)
                        mm(ps[rows, 6, 0:LAST], q_last[:, rows], kT[:, g, 512:LP], start=True, stop=True)
                    r = ROWS[4]
                    s4 = bias[0:r, bias_at[4] + PAD:bias_at[4] + PAD + LP]
                    mm(ps[:, 7, :], rep_c[0:r, 2 * P:3 * P], s4[:, 0:512], start=True, stop=True)
                    mm(ps[:, 6, 64:64 + LAST], rep_c[0:r, 2 * P:3 * P], s4[:, 512:LP], start=True, stop=True
                       ).then_inc(last_logits, 1)
                if s == O_LAST:
                    pe.wait_ge(last_pT_ready, 1)
                    for g in range(KVH):
                        g0 = KVH * DH + g * DH
                        cols = slice(64 * g, 64 * g + 64)
                        for c in range(4):
                            mm(ps[:, 7, cols], kv[:, c, g0:g0 + DH], pT[:, 0, c * P + 64 * g:c * P + 64 * g + 64],
                               start=(c == 0), stop=False)
                        ins = mm(ps[:, 7, cols], kv[0:LAST, 4, g0:g0 + DH], pT[0:LAST, 1, cols], start=False, stop=True)
                    ins.then_inc(last_o_out, 1)
                if s in O_NEW:
                    half = O_NEW.index(s)
                    pe.wait_ge(vpage_here, 16 * PAGES * 4 * (half + 1))
                    pe.wait_ge(v_new_here, 16 * (half + 1))
                    pe.wait_ge(s_pT_ready, 2 * half + 2)
                    for g in range(KVH):
                        v, out = slice(g * DH, (g + 1) * DH), slice(g * P, (g + 1) * P)
                        for n in range(PAGES):
                            for b4 in range(4):
                                mm(ps[32 * b4:32 * b4 + 32, 7, out], pT[:, g, n * P + 32 * b4:n * P + 32 * b4 + 32],
                                   vpage[:, b4, n, v], start=(n == 0), stop=False)
                        for b4 in range(4):
                            rows = slice(32 * b4, 32 * b4 + 32)
                            ins = mm(ps[rows, 7, out], pT_new[:, g, rows], v_new[:, b4, v], start=False, stop=True)
                    ins.then_inc(s_o_out, 1)
                if s in S_NEW:
                    k = S_NEW.index(s)
                    if k == 0:
                        pe.wait_ge(last_o_taken, 1)
                        pe.wait_ge(q_new_ready, HEADS)
                    pe.wait_ge(tile_taken, N_GT + 2 * s - C_OF + 2)
                    b = 2 * k
                    for c in range(2):
                        pe.wait_ge(kpage_here[c], 16 * PAGES * (k + 1))
                    turn_keys(b, 0)
                    turn_keys(b, 1)
                    if k == 1 or k == 3:
                        pe.wait_ge(rep_taken, k // 2 + 1)
                    logits_new(b, 0)
                    turn_keys(b + 1, 0)
                    logits_new(b, 1)
                    turn_keys(b + 1, 1)
                    logits_new(b + 1, 0)
                    logits_new(b + 1, 1)
                    if k % 2 == 0:
                        r = ROWS[4]
                        s4 = bias[0:r, bias_at[4] + PAD:bias_at[4] + PAD + LS]
                        sel = rep_c[0:r, (k // 2) * P:(k // 2 + 1) * P]
                        if k == 2:
                            pe.wait_ge(s_o_rows, 1)
                        mm(ps[:, 7, :], sel, s4[:, 0:512], start=True, stop=True)
                        mm(ps[:, 6, 64:64 + DS], sel, s4[:, 512:LS], start=True, stop=True).then_inc(rep_out, 1)

            def turn_outputs(half):
                pe.wait_ge(s_o_rows, half + 1)
                for g in range(KVH):
                    ins = nc.tensor.transpose(ps[:, 7, g * P:(g + 1) * P], o_rows[:, g * DH:(g + 1) * DH], ident)
                ins.then_inc(s_o_turned, 1)

            for s in range(PAIRS + 1):
                before_pair(s)
                if s == O_NEW[0] + 1:
                    pe.wait_ge(rep_taken, 2)
                    turn_outputs(0)
                one_tile(N_GT + 2 * s, 0)
                if s == 0:
                    pe.wait_ge(tile_taken, N_GT - C_OF + 2)
                within_pair(s)
                if s == O_NEW[1]:
                    turn_outputs(1)
                one_tile(N_GT + 2 * s, 1)
            tiles(N_ZA + 2, 6)
            pe.wait_ge(s_o_taken, 2)
            pe.wait_ge(state_here, 32)
            for c in range(16):
                j, part = c // 2, c % 2
                if c >= 4:
                    pe.wait_ge(state_taken, c - 3)
                nc.tensor.transpose(ps[:, 4 + c % 4, 0:4 * TAIL], state[0:4 * TAIL, part, j * P:(j + 1) * P],
                                    cst[0:4 * TAIL, C_ID:C_ID + 4 * TAIL]).then_inc(state_out, 1)
            pe.wait_ge(state_taken, 16)
            tiles(N_CU, 16)
            tiles(N_ZC, 6)
            pe.wait_ge(tailT_ready, 8)
            for j in range(8):
                ins = nc.tensor.transpose(ps[0:TAIL + DB * DS, 4 + j // 4, (j % 4) * P:(j % 4 + 1) * P],
                                          tailT[:, j, :], ident)
            ins.then_inc(tail_out, 1)
            tile_pair(N_ZC + 6, 0)
            pe.wait_ge(conv_summed, 1)
            for half in range(2):
                ins = mm(ps[:, 6 + half, 0:HALF], ones[:, :], c_sum[:, half * HALF:(half + 1) * HALF],
                         start=True, stop=True)
            ins.then_inc(mean_out, 1)
            tiles(N_G2, 4)
            pe.wait_ge(sq_ready, 1)
            pe.wait_ge(tail_ready, 1)
            for half in range(2):
                ins = mm(ps[:, 4 + half, 0:HALF], ones[:, :], c_sum[:, half * HALF:(half + 1) * HALF],
                         start=True, stop=True)
            ins.then_inc(var_out, 1)
            tiles(N_G2 + 4, 4)

            block_ready(N_BR)
            for k in range(KC):
                pe.wait_ge(xlo_ready, 4 * TILES + k + 1)
                for m, (b, x) in enumerate(((whi, xhi), (whi, xlo), (wlo, xhi))):
                    for half in range(2):
                        ins = mm(ps[:, 4 + 2 * (k // 8) + half, 0:HALF], b[:, 1, k * P:(k + 1) * P],
                                 x[:, k, half * HALF:(half + 1) * HALF],
                                 start=(k % 8 == 0 and m == 0), stop=(k % 8 == 7 and m == 2))
            ins.then_inc(block_used, 1)

            def branch(n, buf, o):
                block_ready(n)
                tile_block(buf, o, 0, 8)
                tile_block(buf, o + 2, 8, 8).then_inc(block_used, 1)

            pe.wait_ge(tile_taken, N_BR - C_OF + 2)
            branch(N_BR + 1, 0, 0)
            with pe.Fori(0, 7) as i:
                for b in range(2):
                    pe.wait_ge(br_taken, 1 + b + i * 2)
                    branch(N_BR + 2 + b + i * 2, (1 + b) % 2, 4 * (1 - b))

            with pe.Fori(0, 3) as i:
                for r in range(4):
                    pe.wait_ge(mlo_ready, 4 * r + 4)
                    rows_block(N_WO + r + i * 4, (N_WO + r) % 2, mhi, mlo, 4 * r, r == 0, r == 3, y_out,
                               i * TILES if r == 0 else None, bank=Y_BANK)
            for r in range(2):
                rows_block(N_WO + 12 + r, (N_WO + r) % 2, mhi, mlo, 4 * r, r == 0, False, y_out,
                           3 * TILES if r == 0 else None, bank=Y_BANK)
            for k, (r, some) in enumerate(((2, (0, 1, 2)), (3, (0, 1, 2)), (2, (3,)), (3, (3,)), (2, (4,)), (3, (4,)))):
                rows_block(N_WO + 12 + r, (N_WO + r) % 2, mhi, mlo, 4 * r, False, r == 3, y_out, ready=(k < 2),
                           some=some, bank=Y_BANK)

    return nc


INS = ["x_prompt", "x_sample", "cache_k", "cache_v", "cache_idx_k", "state_conv", "page_table", "meta_tokens",
       "w_in", "ln_idx_g", "ln_idx_b", "w_dw", "b_dw", "ln_conv_g", "ln_conv_b", "w_att_out", "w_conv_out", "w_o",
       "ln_post_g", "ln_post_b"]
OUTS = [(1, SEQ, D), (DB, DS, D), (1, LP, KVH, DH), (1, LP, KVH, DH), (1, LP, IDIM), (1, TAIL, DC),
        (DB, DS, KVH, DH), (DB, DS, KVH, DH), (DB, DS, IDIM), (DB, TAIL, DC)]


def kernel(**inputs):
    import numpy as _np
    import concourse.bacc as _bacc
    from concourse import mybir as _mybir
    from concourse.bass_utils import run_bass_kernel_spmd as _run

    nc = _bacc.Bacc("TRN2", target_bir_lowering=False, num_devices=1)
    arrays, args = {}, []
    for name in INS:
        arrays[f"in_{name}_dram"] = _np.ascontiguousarray(inputs[name])
    for name, a in zip(("consts", "consts2"), shape_constants()):
        arrays[f"in_{name}_dram"] = a
    for name, a in arrays.items():
        args.append(nc.dram_tensor(name, a.shape, _mybir.dt.from_np(a.dtype), kind="ExternalInput").ap())
    for i, shape in enumerate(OUTS):
        args.append(nc.dram_tensor(f"out_{i}_dram", shape, _mybir.dt.float32, kind="ExternalOutput").ap())
    build(nc, *args)
    r = _run(nc, [arrays], core_ids=[0])
    return tuple(r.results[0][f"out_{i}_dram"] for i in range(len(OUTS)))
```
